# Optimizing a Trainium2 kernel written in Bass

```python
import jax, jax.numpy as jnp
from jax import lax
import numpy as np
import math

D_MODEL = 1024
BATCH = 1
SEQ = 256
DEPTH = 2

FOX_HEADS = 8
FOX_HEAD_DIM = 64
FOX_WIDTH = FOX_HEADS * FOX_HEAD_DIM
MLA_HEADS = 8
MLA_NOPE_DIM = 64
MLA_ROPE_DIM = 32
MLA_V_DIM = 64
MLA_WIDTH = MLA_HEADS * MLA_V_DIM
D_MIX = FOX_WIDTH + MLA_WIDTH
Q_LORA_RANK = 256
KV_LORA_RANK = 128
ROPE_THETA = 10000.0
IN_WIDTH = 3 * FOX_WIDTH + FOX_HEADS + Q_LORA_RANK + KV_LORA_RANK + MLA_ROPE_DIM
Q_BLOCK = 128
N_GROUPS = 8
EXPERTS_PER_GROUP = 4
N_EXPERTS = N_GROUPS * EXPERTS_PER_GROUP
TOP_K_IN_GROUP = 2
D_EXPERT = 256
EXPERT_BLOCK = 128
NORM_EPS = 1e-6


def rms_norm(x, gain):
    xf = x.astype(jnp.float32)
    y = xf * lax.rsqrt(jnp.mean(xf * xf, axis=-1, keepdims=True) + NORM_EPS)
    return (y * gain.astype(jnp.float32)).astype(x.dtype)

def rotary(x, positions):
    half = MLA_ROPE_DIM // 2
    inv_freq = ROPE_THETA ** (-jnp.arange(half, dtype=jnp.float32) / half)
    ang = positions.astype(jnp.float32)[..., None] * inv_freq
    ang = ang.reshape(ang.shape[:2] + (1,) * (x.ndim - 3) + (half,))
    cos, sin = jnp.cos(ang), jnp.sin(ang)
    xf = x.astype(jnp.float32)
    x1, x2 = xf[..., :half], xf[..., half:]
    return jnp.concatenate([x1 * cos - x2 * sin, x2 * cos + x1 * sin], axis=-1).astype(x.dtype)

def causal_block_attention(q, k, v, log_forget_cum=None):
    B, S, H, dk = q.shape
    dv = v.shape[-1]
    nb = S // Q_BLOCK
    scale = dk ** -0.5
    kf = k.astype(jnp.float32)
    vf = v.astype(jnp.float32)
    key_pos = jnp.arange(S)
    q_blocks = q.reshape(B, nb, Q_BLOCK, H, dk).transpose(1, 0, 2, 3, 4)
    has_decay = log_forget_cum is not None
    if has_decay:
        d_keys = log_forget_cum.transpose(0, 2, 1)
        d_blocks = log_forget_cum.reshape(B, nb, Q_BLOCK, H).transpose(1, 0, 3, 2)
        xs = (jnp.arange(nb), q_blocks, d_blocks)
    else:
        xs = (jnp.arange(nb), q_blocks)

    def one_block(args):
        i, q_i = args[0], args[1]
        s = jnp.einsum('bqhd,bkhd->bhqk', q_i.astype(jnp.float32), kf) * scale
        if has_decay:
            s = s + args[2][..., :, None] - d_keys[:, :, None, :]
        q_pos = i * Q_BLOCK + jnp.arange(Q_BLOCK)
        s = jnp.where(key_pos[None, :] <= q_pos[:, None], s, -jnp.inf)
        p = jax.nn.softmax(s, axis=-1)
        return jnp.einsum('bhqk,bkhd->bqhd', p, vf)

    out = lax.map(one_block, xs)
    return out.transpose(1, 0, 2, 3, 4).reshape(B, S, H, dv).astype(v.dtype)

def hybrid_mixer(xn, positions, w_in, b_f, q_norm, w_uq, kv_norm, w_ukv, fox_out_norm, mla_out_norm, w_o):
    B, S, _ = xn.shape
    proj = xn @ w_in
    offs = [FOX_WIDTH, 2 * FOX_WIDTH, 3 * FOX_WIDTH, 3 * FOX_WIDTH + FOX_HEADS,
            3 * FOX_WIDTH + FOX_HEADS + Q_LORA_RANK,
            3 * FOX_WIDTH + FOX_HEADS + Q_LORA_RANK + KV_LORA_RANK]
    fq, fk, fv, f_logit, c_q, c_kv, k_rope = jnp.split(proj, offs, axis=-1)

    log_f = jax.nn.log_sigmoid(f_logit.astype(jnp.float32) + b_f.astype(jnp.float32))
    log_f_cum = jnp.cumsum(log_f, axis=1)
    fox = causal_block_attention(fq.reshape(B, S, FOX_HEADS, FOX_HEAD_DIM),
                                 fk.reshape(B, S, FOX_HEADS, FOX_HEAD_DIM),
                                 fv.reshape(B, S, FOX_HEADS, FOX_HEAD_DIM), log_f_cum)
    fox = rms_norm(fox, fox_out_norm.reshape(FOX_HEADS, FOX_HEAD_DIM)).reshape(B, S, FOX_WIDTH)

    q = (rms_norm(c_q, q_norm) @ w_uq).reshape(B, S, MLA_HEADS, MLA_NOPE_DIM + MLA_ROPE_DIM)
    q = jnp.concatenate([q[..., :MLA_NOPE_DIM], rotary(q[..., MLA_NOPE_DIM:], positions)], axis=-1)
    kv = (rms_norm(c_kv, kv_norm) @ w_ukv).reshape(B, S, MLA_HEADS, MLA_NOPE_DIM + MLA_V_DIM)
    k_nope, v = kv[..., :MLA_NOPE_DIM], kv[..., MLA_NOPE_DIM:]
    k_pe = rotary(k_rope, positions)
    k = jnp.concatenate([k_nope, jnp.broadcast_to(k_pe[:, :, None, :], (B, S, MLA_HEADS, MLA_ROPE_DIM))], axis=-1)
    mla = causal_block_attention(q, k, v)
    mla = rms_norm(mla, mla_out_norm.reshape(MLA_HEADS, MLA_V_DIM)).reshape(B, S, MLA_WIDTH)

    return jnp.concatenate([fox, mla], axis=-1) @ w_o

def hierarchical_moe(xn, w_group, w_router, w_gate, w_up, w_down):
    B, S, D = xn.shape
    T = B * S
    xt = xn.reshape(T, D)
    group_p = jax.nn.softmax((xt @ w_group).astype(jnp.float32), axis=-1)
    group_w, group_id = lax.top_k(group_p, 1)
    expert_logits = (xt @ w_router).astype(jnp.float32).reshape(T, N_GROUPS, EXPERTS_PER_GROUP)
    in_group = jnp.take_along_axis(expert_logits, group_id[:, :, None], axis=1)[:, 0]
    top_logits, local_id = lax.top_k(in_group, TOP_K_IN_GROUP)
    gates = group_w * jax.nn.softmax(top_logits, axis=-1)
    expert_id = group_id * EXPERTS_PER_GROUP + local_id

    A = T * TOP_K_IN_GROUP
    e_flat = expert_id.reshape(A)
    tok_flat = jnp.repeat(jnp.arange(T), TOP_K_IN_GROUP)
    g_flat = gates.reshape(A)
    order = jnp.argsort(e_flat)
    e_sorted, tok_sorted, g_sorted = e_flat[order], tok_flat[order], g_flat[order]
    counts = jnp.bincount(e_flat, length=N_EXPERTS)
    padded = (counts + EXPERT_BLOCK - 1) // EXPERT_BLOCK * EXPERT_BLOCK
    start = jnp.cumsum(counts) - counts
    pend = jnp.cumsum(padded)
    pstart = pend - padded
    dest = pstart[e_sorted] + (jnp.arange(A) - start[e_sorted])
    n_blocks = (A + N_EXPERTS * (EXPERT_BLOCK - 1) + EXPERT_BLOCK - 1) // EXPERT_BLOCK
    buf = jnp.zeros((n_blocks * EXPERT_BLOCK, D), xn.dtype).at[dest].set(xt[tok_sorted])
    block_expert = jnp.clip(jnp.searchsorted(pend, jnp.arange(n_blocks) * EXPERT_BLOCK, side='right'), 0, N_EXPERTS - 1)

    def expert_block(args):
        xb, e = args
        h = jax.nn.silu(xb @ w_gate[e]) * (xb @ w_up[e])
        return h @ w_down[e]

    ybuf = lax.map(expert_block, (buf.reshape(n_blocks, EXPERT_BLOCK, D), block_expert)).reshape(-1, D)
    contrib = ybuf[dest].astype(jnp.float32) * g_sorted[:, None]
    y = jax.ops.segment_sum(contrib, tok_sorted, num_segments=T)
    return y.reshape(B, S, D).astype(xn.dtype)

def first_inputs(seed: int = 0) -> dict:
    key = jax.random.key(seed)
    ks = jax.random.split(key, 20)
    f32 = jnp.float32

    def dense(k, shape, fan_in):
        return jax.random.normal(k, shape, f32) * (fan_in ** -0.5)

    def gain(k, shape):
        return 1.0 + 0.02 * jax.random.normal(k, shape, f32)

    return {
        'x': jax.random.normal(ks[0], (BATCH, SEQ, D_MODEL), f32),
        'positions': jnp.broadcast_to(jnp.arange(SEQ, dtype=jnp.int32), (BATCH, SEQ)),
        'attn_norm': gain(ks[1], (DEPTH, D_MODEL)),
        'w_in': dense(ks[2], (DEPTH, D_MODEL, IN_WIDTH), D_MODEL),
        'b_f': jax.random.uniform(ks[3], (DEPTH, FOX_HEADS), f32, 1.0, 4.0),
        'q_norm': gain(ks[4], (DEPTH, Q_LORA_RANK)),
        'w_uq': dense(ks[5], (DEPTH, Q_LORA_RANK, MLA_HEADS * (MLA_NOPE_DIM + MLA_ROPE_DIM)), Q_LORA_RANK),
        'kv_norm': gain(ks[6], (DEPTH, KV_LORA_RANK)),
        'w_ukv': dense(ks[7], (DEPTH, KV_LORA_RANK, MLA_HEADS * (MLA_NOPE_DIM + MLA_V_DIM)), KV_LORA_RANK),
        'fox_out_norm': gain(ks[8], (DEPTH, FOX_WIDTH)),
        'mla_out_norm': gain(ks[9], (DEPTH, MLA_WIDTH)),
        'w_o': dense(ks[10], (DEPTH, D_MIX, D_MODEL), D_MIX),
        'ffn_norm': gain(ks[11], (DEPTH, D_MODEL)),
        'w_group': dense(ks[12], (DEPTH, D_MODEL, N_GROUPS), D_MODEL),
        'w_router': dense(ks[13], (DEPTH, D_MODEL, N_EXPERTS), D_MODEL),
        'w_gate': dense(ks[14], (DEPTH, N_EXPERTS, D_MODEL, D_EXPERT), D_MODEL),
        'w_up': dense(ks[15], (DEPTH, N_EXPERTS, D_MODEL, D_EXPERT), D_MODEL),
        'w_down': dense(ks[16], (DEPTH, N_EXPERTS, D_EXPERT, D_MODEL), D_EXPERT),
        'final_norm': gain(ks[17], (D_MODEL,)),
    }

def first_block(x, positions, attn_norm, w_in, b_f, q_norm, w_uq, kv_norm, w_ukv, fox_out_norm, mla_out_norm, w_o,
              ffn_norm, w_group, w_router, w_gate, w_up, w_down, final_norm):
    h = x
    for l in range(DEPTH):
        h = h + hybrid_mixer(rms_norm(h, attn_norm[l]), positions, w_in[l], b_f[l], q_norm[l], w_uq[l],
                             kv_norm[l], w_ukv[l], fox_out_norm[l], mla_out_norm[l], w_o[l])
        h = h + hierarchical_moe(rms_norm(h, ffn_norm[l]), w_group[l], w_router[l], w_gate[l], w_up[l], w_down[l])
    return rms_norm(h, final_norm)


MIX_WIDTH = D_MODEL // 2
RET_HEAD_DIM = 128
RET_HEADS = MIX_WIDTH // RET_HEAD_DIM
RET_CHUNK = 128
ROPE_BASE = 10000.0
RWKV_HEAD_DIM = 64
RWKV_HEADS = MIX_WIDTH // RWKV_HEAD_DIM
DECAY_LORA = 64
AAA_LORA = 64
GATE_LORA = 128
CONV_WIDTH = 3
N_BRANCHES = 3
RET_COLS = 4 * MIX_WIDTH
RWKV_COLS = 3 * MIX_WIDTH + DECAY_LORA + AAA_LORA + GATE_LORA
CONV_COLS = 3 * MIX_WIDTH
IN_COLS = RET_COLS + RWKV_COLS + CONV_COLS
N_GROUPS_2 = 4
EXPERTS_PER_GROUP_2 = 8
N_EXPERTS_2 = N_GROUPS_2 * EXPERTS_PER_GROUP_2
EXPERT_FF = D_MODEL // 2
TOP_K = 2
MOE_BLOCK = 128
HEAD_NORM_EPS = 1e-5
RWKV_NORM_EPS = 64e-5


F32 = jnp.float32

def rms_norm_2(x, g):
    xf = x.astype(F32)
    y = xf * lax.rsqrt(jnp.mean(xf * xf, axis=-1, keepdims=True) + NORM_EPS)
    return (y * g.astype(F32)).astype(x.dtype)

def modulate(h, shift, scale):
    return (h.astype(F32) * (1.0 + scale[:, None, :]) + shift[:, None, :]).astype(h.dtype)

def head_norm(y, g, eps):
    yf = y.astype(F32)
    mu = jnp.mean(yf, axis=-1, keepdims=True)
    var = jnp.mean(jnp.square(yf - mu), axis=-1, keepdims=True)
    return (yf - mu) * lax.rsqrt(var + eps) * g.astype(F32).reshape(y.shape[-2:])

def rotary_2(t, positions):
    half = t.shape[-1] // 2
    inv_freq = ROPE_BASE ** (-jnp.arange(half, dtype=F32) / half)
    ang = positions.astype(F32)[..., None] * inv_freq
    cos = jnp.cos(ang)[:, :, None, :]
    sin = jnp.sin(ang)[:, :, None, :]
    t1 = t[..., :half].astype(F32)
    t2 = t[..., half:].astype(F32)
    return jnp.concatenate([t1 * cos - t2 * sin, t1 * sin + t2 * cos], axis=-1)

def retention(q, k, v, g, positions, gn_g):
    bsz, seq, _ = q.shape
    split = lambda t: t.reshape(bsz, seq, RET_HEADS, RET_HEAD_DIM)
    qh = rotary_2(split(q), positions)
    kh = rotary_2(split(k), positions) * (RET_HEAD_DIM ** -0.5)
    vh = split(v).astype(F32)
    n_chunks = seq // RET_CHUNK

    def to_chunks(t):
        return t.reshape(bsz, n_chunks, RET_CHUNK, RET_HEADS, RET_HEAD_DIM).transpose(1, 0, 3, 2, 4)

    log_gamma = jnp.log1p(-jnp.exp2(-5.0 - jnp.arange(RET_HEADS, dtype=F32)))
    pos = jnp.arange(RET_CHUNK, dtype=F32)
    rel = pos[:, None] - pos[None, :]
    decay_in = jnp.where(rel >= 0, jnp.exp(log_gamma[:, None, None] * jnp.maximum(rel, 0.0)), 0.0)
    decay_k = jnp.exp(log_gamma[:, None] * (RET_CHUNK - 1 - pos))
    decay_q = jnp.exp(log_gamma[:, None] * (pos + 1.0))
    decay_chunk = jnp.exp(log_gamma * RET_CHUNK)

    def chunk_step(state, qkv):
        qc, kc, vc = qkv
        scores = jnp.einsum('bhid,bhjd->bhij', qc, kc) * decay_in
        inner = jnp.einsum('bhij,bhjv->bhiv', scores, vc)
        cross = jnp.einsum('bhid,bhdv->bhiv', qc, state) * decay_q[None, :, :, None]
        state = state * decay_chunk[None, :, None, None] + jnp.einsum(
            'bhjd,bhjv->bhdv', kc * decay_k[None, :, :, None], vc)
        return state, inner + cross

    state0 = jnp.zeros((bsz, RET_HEADS, RET_HEAD_DIM, RET_HEAD_DIM), F32)
    _, out = lax.scan(chunk_step, state0, (to_chunks(qh), to_chunks(kh), to_chunks(vh)))
    out = out.transpose(1, 0, 3, 2, 4).reshape(bsz, seq, RET_HEADS, RET_HEAD_DIM)
    out = head_norm(out, gn_g, HEAD_NORM_EPS).reshape(bsz, seq, MIX_WIDTH)
    return (jax.nn.silu(g.astype(F32)) * out).astype(q.dtype)

def rwkv7_time_mix(p, mu, w0, w_lora, a0, a_lora, g_lora, k_k, k_a, r_k, gn_g):
    bsz, seq, _ = p.shape
    mw = MIX_WIDTH
    pf = p.astype(F32)
    prev = jnp.pad(pf, ((0, 0), (1, 0), (0, 0)))[:, :-1]
    pf = pf + mu * (prev - pf)
    o_w = 3 * mw
    o_a = o_w + DECAY_LORA
    o_g = o_a + AAA_LORA
    r = pf[..., 0:mw]
    k = pf[..., mw:2 * mw]
    v = pf[..., 2 * mw:3 * mw]
    wd = pf[..., o_w:o_a]
    ad = pf[..., o_a:o_g]
    gd = pf[..., o_g:o_g + GATE_LORA]
    w = jnp.exp(-math.exp(-0.5) * jax.nn.sigmoid(w0 + jnp.tanh(wd) @ w_lora))
    a = jax.nn.sigmoid(a0 + ad @ a_lora)
    g = jax.nn.sigmoid(gd) @ g_lora
    heads = lambda t: t.reshape(bsz, seq, RWKV_HEADS, RWKV_HEAD_DIM)
    r, w, k, v, a = heads(r), heads(w), heads(k), heads(v), heads(a)
    kk = k * k_k.reshape(RWKV_HEADS, RWKV_HEAD_DIM)
    kh = kk * lax.rsqrt(jnp.maximum(jnp.sum(kk * kk, axis=-1, keepdims=True), 1e-12))
    kt = k * (1.0 + (a - 1.0) * k_a.reshape(RWKV_HEADS, RWKV_HEAD_DIM))

    def time_step(state, inp):
        rt, wt, ktt, vt, kht, at = inp
        sk = jnp.einsum('bhvk,bhk->bhv', state, kht)
        state = (state * wt[:, :, None, :]
                 - sk[..., None] * (at * kht)[:, :, None, :]
                 + vt[..., None] * ktt[:, :, None, :])
        return state, jnp.einsum('bhvk,bhk->bhv', state, rt)

    tm = lambda t: jnp.moveaxis(t, 1, 0)
    state0 = jnp.zeros((bsz, RWKV_HEADS, RWKV_HEAD_DIM, RWKV_HEAD_DIM), F32)
    _, y = lax.scan(time_step, state0, (tm(r), tm(w), tm(kt), tm(v), tm(kh), tm(a)))
    y = jnp.moveaxis(y, 0, 1)
    y = head_norm(y, gn_g, RWKV_NORM_EPS)
    y = y + jnp.sum(r * kt * r_k.astype(F32), axis=-1, keepdims=True) * v
    return (y.reshape(bsz, seq, mw) * g).astype(p.dtype)

def short_conv(p, conv_w):
    h, bgate, cgate = jnp.split(p, 3, axis=-1)
    u = cgate * h
    seq = u.shape[1]
    up = jnp.pad(u, ((0, 0), (CONV_WIDTH - 1, 0), (0, 0)))
    conv = conv_w[0] * up[:, 0:seq]
    for i in range(1, CONV_WIDTH):
        conv = conv + conv_w[i] * up[:, i:i + seq]
    return bgate * conv

def hier_moe(h, w_router_group, b_router_group, w_router_expert, b_router_expert,
             w_exp_gate, w_exp_up, w_exp_down):
    bsz, seq, d = h.shape
    n_tok = bsz * seq
    xf = h.reshape(n_tok, d)
    g_logits = (xf @ w_router_group + b_router_group).astype(F32)
    g_prob = jax.nn.softmax(g_logits, axis=-1)
    g_sel = jnp.argmax(g_logits, axis=-1).astype(jnp.int32)
    p_group = jnp.take_along_axis(g_prob, g_sel[:, None], axis=-1)
    e_logits = (xf @ w_router_expert + b_router_expert).astype(F32).reshape(n_tok, N_GROUPS_2, EXPERTS_PER_GROUP_2)
    e_logits = jnp.take_along_axis(e_logits, g_sel[:, None, None], axis=1)[:, 0]
    top_v, top_i = lax.top_k(e_logits, TOP_K)
    weights = (jax.nn.softmax(top_v, axis=-1) * p_group).reshape(-1)
    eid = (g_sel[:, None] * EXPERTS_PER_GROUP_2 + top_i).reshape(-1).astype(jnp.int32)
    tok = jnp.repeat(jnp.arange(n_tok, dtype=jnp.int32), TOP_K)
    n_assign = n_tok * TOP_K
    order = jnp.argsort(eid)
    eid_s, tok_s, w_s = eid[order], tok[order], weights[order]
    counts = jnp.bincount(eid, length=N_EXPERTS_2).astype(jnp.int32)
    starts = jnp.cumsum(counts) - counts
    padded = (counts + MOE_BLOCK - 1) // MOE_BLOCK * MOE_BLOCK
    pends = jnp.cumsum(padded)
    pstarts = pends - padded
    dest = pstarts[eid_s] + jnp.arange(n_assign, dtype=jnp.int32) - starts[eid_s]
    n_rows = n_assign + N_EXPERTS_2 * MOE_BLOCK
    n_blocks = n_rows // MOE_BLOCK
    row_tok = jnp.full((n_rows,), n_tok, jnp.int32).at[dest].set(tok_s)
    row_w = jnp.zeros((n_rows,), F32).at[dest].set(w_s)
    block_e = jnp.minimum(
        jnp.searchsorted(pends, jnp.arange(n_blocks, dtype=jnp.int32) * MOE_BLOCK, side='right'),
        N_EXPERTS_2 - 1)
    x_rows = jnp.concatenate([xf, jnp.zeros((1, d), xf.dtype)], axis=0)[row_tok]
    x_rows = x_rows.reshape(n_blocks, MOE_BLOCK, d)

    def expert_block(args):
        xb, e = args
        return (jax.nn.silu(xb @ w_exp_gate[e]) * (xb @ w_exp_up[e])) @ w_exp_down[e]

    y_rows = lax.map(expert_block, (x_rows, block_e)).reshape(n_rows, d)
    y_rows = y_rows.astype(F32) * row_w[:, None]
    out = jax.ops.segment_sum(y_rows, row_tok, num_segments=n_tok + 1)[:n_tok]
    return out.reshape(bsz, seq, d).astype(h.dtype)

def decoder_layer(x, c, positions, norm1_g, norm2_g, w_ada, b_ada, w_in, w_gate, b_gate,
                  ret_gn_g, rwkv_mu, rwkv_w0, rwkv_w_lora, rwkv_a0, rwkv_a_lora, rwkv_g_lora,
                  rwkv_k_k, rwkv_k_a, rwkv_r_k, rwkv_gn_g, conv_w, w_branch, w_o,
                  w_router_group, b_router_group, w_router_expert, b_router_expert,
                  w_exp_gate, w_exp_up, w_exp_down):
    d = D_MODEL
    mod = jax.nn.silu(c.astype(F32)) @ w_ada + b_ada
    shift1, scale1, gate1, shift2, scale2, gate2 = jnp.split(mod, 6, axis=-1)

    h = modulate(rms_norm_2(x, norm1_g), shift1, scale1)
    p = h @ w_in
    p_ret = p[..., :RET_COLS]
    p_rwkv = p[..., RET_COLS:RET_COLS + RWKV_COLS]
    p_conv = p[..., RET_COLS + RWKV_COLS:]
    q, k, v, g = jnp.split(p_ret, 4, axis=-1)
    y_ret = retention(q, k, v, g, positions, ret_gn_g)
    y_rwkv = rwkv7_time_mix(p_rwkv, rwkv_mu, rwkv_w0, rwkv_w_lora, rwkv_a0, rwkv_a_lora,
                            rwkv_g_lora, rwkv_k_k, rwkv_k_a, rwkv_r_k, rwkv_gn_g)
    y_conv = short_conv(p_conv, conv_w)
    gates = jax.nn.sigmoid((h @ w_gate + b_gate).astype(F32))
    merged = jnp.zeros(x.shape, F32)
    for i, y in enumerate((y_ret, y_rwkv, y_conv)):
        merged = merged + gates[..., i * d:(i + 1) * d] * (y @ w_branch[i])
    x = x + (gate1[:, None, :] * (merged.astype(x.dtype) @ w_o)).astype(x.dtype)

    h2 = modulate(rms_norm_2(x, norm2_g), shift2, scale2)
    y_moe = hier_moe(h2, w_router_group, b_router_group, w_router_expert, b_router_expert,
                     w_exp_gate, w_exp_up, w_exp_down)
    x = x + (gate2[:, None, :] * y_moe).astype(x.dtype)
    return x

def second_inputs(seed: int = 0) -> dict:
    key = jax.random.key(seed)
    k = jax.random.split(key, 32)
    L, D, MW = DEPTH, D_MODEL, MIX_WIDTH

    def nrm(kk, shape, scale):
        return scale * jax.random.normal(kk, shape, jnp.float32)

    return {
        'x': nrm(k[0], (BATCH, SEQ, D), 1.0),
        'c': nrm(k[1], (BATCH, D), 1.0),
        'positions': jnp.tile(jnp.arange(SEQ, dtype=jnp.int32)[None, :], (BATCH, 1)),
        'norm1_g': 1.0 + nrm(k[2], (L, D), 0.02),
        'norm2_g': 1.0 + nrm(k[3], (L, D), 0.02),
        'final_norm_g': 1.0 + nrm(k[4], (D,), 0.02),
        'w_ada': nrm(k[5], (L, D, 6 * D), 0.5 * D ** -0.5),
        'b_ada': nrm(k[6], (L, 6 * D), 0.01),
        'w_in': nrm(k[7], (L, D, IN_COLS), D ** -0.5),
        'w_gate': nrm(k[8], (L, D, N_BRANCHES * D), D ** -0.5),
        'b_gate': nrm(k[9], (L, N_BRANCHES * D), 0.01),
        'ret_gn_g': 1.0 + nrm(k[10], (L, MW), 0.02),
        'rwkv_mu': jax.random.uniform(k[11], (L, RWKV_COLS), jnp.float32),
        'rwkv_w0': nrm(k[12], (L, MW), 0.5),
        'rwkv_w_lora': nrm(k[13], (L, DECAY_LORA, MW), DECAY_LORA ** -0.5),
        'rwkv_a0': nrm(k[14], (L, MW), 0.5),
        'rwkv_a_lora': nrm(k[15], (L, AAA_LORA, MW), AAA_LORA ** -0.5),
        'rwkv_g_lora': nrm(k[16], (L, GATE_LORA, MW), GATE_LORA ** -0.5),
        'rwkv_k_k': 0.85 + nrm(k[17], (L, MW), 0.05),
        'rwkv_k_a': 1.0 + nrm(k[18], (L, MW), 0.05),
        'rwkv_r_k': nrm(k[19], (L, RWKV_HEADS, RWKV_HEAD_DIM), 0.1),
        'rwkv_gn_g': 1.0 + nrm(k[20], (L, MW), 0.02),
        'conv_w': nrm(k[21], (L, CONV_WIDTH, MW), CONV_WIDTH ** -0.5),
        'w_branch': nrm(k[22], (L, N_BRANCHES, MW, D), MW ** -0.5),
        'w_o': nrm(k[23], (L, D, D), D ** -0.5),
        'w_router_group': nrm(k[24], (L, D, N_GROUPS_2), D ** -0.5),
        'b_router_group': nrm(k[25], (L, N_GROUPS_2), 0.01),
        'w_router_expert': nrm(k[26], (L, D, N_EXPERTS_2), D ** -0.5),
        'b_router_expert': nrm(k[27], (L, N_EXPERTS_2), 0.01),
        'w_exp_gate': nrm(k[28], (L, N_EXPERTS_2, D, EXPERT_FF), D ** -0.5),
        'w_exp_up': nrm(k[29], (L, N_EXPERTS_2, D, EXPERT_FF), D ** -0.5),
        'w_exp_down': nrm(k[30], (L, N_EXPERTS_2, EXPERT_FF, D), EXPERT_FF ** -0.5),
    }

def second_block(x, c, positions, norm1_g, norm2_g, final_norm_g, w_ada, b_ada, w_in, w_gate, b_gate,
              ret_gn_g, rwkv_mu, rwkv_w0, rwkv_w_lora, rwkv_a0, rwkv_a_lora, rwkv_g_lora,
              rwkv_k_k, rwkv_k_a, rwkv_r_k, rwkv_gn_g, conv_w, w_branch, w_o,
              w_router_group, b_router_group, w_router_expert, b_router_expert,
              w_exp_gate, w_exp_up, w_exp_down):
    for l in range(DEPTH):
        x = decoder_layer(
            x, c, positions, norm1_g[l], norm2_g[l], w_ada[l], b_ada[l], w_in[l], w_gate[l], b_gate[l],
            ret_gn_g[l], rwkv_mu[l], rwkv_w0[l], rwkv_w_lora[l], rwkv_a0[l], rwkv_a_lora[l],
            rwkv_g_lora[l], rwkv_k_k[l], rwkv_k_a[l], rwkv_r_k[l], rwkv_gn_g[l], conv_w[l],
            w_branch[l], w_o[l], w_router_group[l], b_router_group[l], w_router_expert[l],
            b_router_expert[l], w_exp_gate[l], w_exp_up[l], w_exp_down[l])
    return rms_norm_2(x, final_norm_g)


def setup_inputs(seed=0):
    out = dict(first_inputs(seed))
    for name, value in second_inputs(seed + 1).items():
        if name != "x":
            out[name + "_2"] = value
    return out


def reference(
    x, positions, attn_norm, w_in, b_f, q_norm, w_uq, kv_norm, w_ukv, fox_out_norm,
    mla_out_norm, w_o, ffn_norm, w_group, w_router, w_gate, w_up, w_down, final_norm, c_2,
    positions_2, norm1_g_2, norm2_g_2, final_norm_g_2, w_ada_2, b_ada_2, w_in_2, w_gate_2,
    b_gate_2, ret_gn_g_2, rwkv_mu_2, rwkv_w0_2, rwkv_w_lora_2, rwkv_a0_2, rwkv_a_lora_2,
    rwkv_g_lora_2, rwkv_k_k_2, rwkv_k_a_2, rwkv_r_k_2, rwkv_gn_g_2, conv_w_2, w_branch_2, w_o_2,
    w_router_group_2, b_router_group_2, w_router_expert_2, b_router_expert_2, w_exp_gate_2,
    w_exp_up_2, w_exp_down_2,
):
    x = first_block(
        x, positions, attn_norm, w_in, b_f, q_norm, w_uq, kv_norm, w_ukv, fox_out_norm,
        mla_out_norm, w_o, ffn_norm, w_group, w_router, w_gate, w_up, w_down, final_norm,
    )
    return second_block(
        x, c_2, positions_2, norm1_g_2, norm2_g_2, final_norm_g_2, w_ada_2, b_ada_2, w_in_2,
        w_gate_2, b_gate_2, ret_gn_g_2, rwkv_mu_2, rwkv_w0_2, rwkv_w_lora_2, rwkv_a0_2,
        rwkv_a_lora_2, rwkv_g_lora_2, rwkv_k_k_2, rwkv_k_a_2, rwkv_r_k_2, rwkv_gn_g_2, conv_w_2,
        w_branch_2, w_o_2, w_router_group_2, b_router_group_2, w_router_expert_2,
        b_router_expert_2, w_exp_gate_2, w_exp_up_2, w_exp_down_2,
    )


_drawn_inputs = setup_inputs


def setup_inputs(seed=0):
    import zlib

    import numpy as np

    out = dict(_drawn_inputs(seed))
    spreads = {}
    factors = {'q_norm': 2.889,
     'norm1_g_2': 3.206,
     'norm2_g_2': 3.994,
     'final_norm_g_2': 8.601,
     'b_ada_2': 2.672,
     'b_gate_2': 8.0,
     'ret_gn_g_2': 8.0,
     'rwkv_k_k_2': 17.804,
     'rwkv_gn_g_2': 29.979,
     'b_router_group_2': 22.755,
     'b_router_expert_2': 7.081}
    for name, (base, spread) in spreads.items():
        noise = np.random.default_rng([zlib.crc32(name.encode()), seed]).standard_normal(out[name].shape)
        drawn = base * np.exp(spread * noise) if base else spread * noise
        out[name] = __import__('jax').numpy.asarray(drawn.astype(out[name].dtype))
    for name, factor in factors.items():
        out[name] = (out[name] * factor).astype(out[name].dtype)
    return out
```

```python
from contextlib import ExitStack

import numpy as np

import concourse.bass as bass
from concourse import mybir

F32 = mybir.dt.float32
I32 = mybir.dt.int32
ALU = mybir.AluOpType
ACT = mybir.ActivationFunctionType
AX = mybir.AxisListType.X

P = 128
L = 2
T = 256
TT = T // P
D = 1024
KT = D // P
HEADS = 8
HD = 64
NOPE, ROPE = 64, 32
QKD = NOPE + ROPE
QR, KVR = 256, 128
REST = HEADS + QR + KVR + ROPE
NE = 32
NG1, NG2 = 8, 4
F1, F2 = 256, 512
MW = 512
MT = MW // P
RH = 4
CH = 32
NCH = P // CH
EPS, HEPS, REPS = 1e-6, 1e-5, 64e-5
BIG = 1e30
RING = 6
SLOT = 4096
UQ_N, UKV_N = HEADS * QKD, HEADS * 2 * HD

CONST = {}


def constants():
    p = np.arange(P)
    cols = []

    def put(name, a):
        a = np.asarray(a, np.float32).reshape(P, -1)
        at = sum(c.shape[1] for c in cols)
        CONST[name] = (at, at + a.shape[1])
        cols.append(a)

    put("ident", np.eye(P))
    put("ones", np.ones((P, P)))
    put("zeros", np.zeros((P, P)))
    put("blk64", p[:, None] // HD == p[None, :] // HD)
    key = np.concatenate([p, np.arange(T)])
    query = np.concatenate([np.tile(p[:, None], (1, P)), np.tile(p[:, None] + P, (1, T))], 1)
    put("causal", np.where(key[None, :] <= query, 0.0, -BIG))
    put("tri", np.stack([(p[:, None] + P * s <= np.arange(T)[None, :]) for s in range(TT)], 1))
    for half in (ROPE // 2, P // 2):
        freq = np.float32(10000.0) ** (-np.arange(half, dtype=np.float32) / np.float32(half))
        put(f"freq{half}", np.tile(freq.astype(np.float32)[None, :], (P, 1)))
    lg = np.log1p(-np.exp2(-5.0 - np.arange(RH, dtype=np.float32))).astype(np.float32)
    rel = (p[None, :] - p[:, None]).astype(np.float32)
    scale = np.float32(P ** -0.5)
    put("ret_in", np.stack([np.where(rel >= 0, np.exp(lg[h] * np.maximum(rel, 0)), 0) * scale for h in range(RH)], 1))
    put("ret_k", np.exp(lg[None, :] * (P - 1 - p[:, None])) * scale)
    put("ret_q", np.exp(lg[None, :] * (p[:, None] + 1.0)))
    same = p[:, None] // CH == p[None, :] // CH
    put("before", same & (p[:, None] < p[None, :]))
    put("upto", same & (p[:, None] <= p[None, :]))
    put("after", same & (p[:, None] > p[None, :]))
    put("chunk", p[:, None] // CH == np.arange(NCH)[None, :])
    put("start", np.tile((np.arange(T) % CH == 0)[None, :], (P, 1)))
    put("inner", np.tile((np.arange(T) % CH != 0)[None, :], (P, 1)))
    return np.ascontiguousarray(np.concatenate(cols, 1))


CONST_TABLE = constants()

VEC1, VEC2, VECG = {}, {}, {}
VEC1_PARTS = [("attn_norm", 8), ("q_norm", 2), ("kv_norm", 1), ("fox_out_norm", 4), ("mla_out_norm", 4), ("ffn_norm", 8)]
VEC2_PARTS = [("norm1_g_2", 8), ("norm2_g_2", 8), ("b_ada_2", 48), ("ret_gn_g_2", 4), ("rwkv_mu_2", 14), ("rwkv_w0_2", 4),
              ("rwkv_a0_2", 4), ("rwkv_k_k_2", 4), ("rwkv_k_a_2", 4), ("rwkv_r_k_2", 4), ("rwkv_gn_g_2", 4),
              ("conv_w_2", 12), ("b_gate_2", 24)]
VECG_PARTS = [("final_norm", 8), ("final_norm_g_2", 8), ("c_2", 8)]
for _table, _parts in ((VEC1, VEC1_PARTS), (VEC2, VEC2_PARTS), (VECG, VECG_PARTS)):
    _at = 0
    for _name, _n in _parts:
        _table[_name] = (_at, _at + _n)
        _at += _n
N1 = sum(n for _, n in VEC1_PARTS)
N2 = sum(n for _, n in VEC2_PARTS)
NV = sum(n for _, n in VECG_PARTS)
R1_N, R2_N = NG1 + NE, NG2 + NE
SMALL1 = 2 * UQ_N + UKV_N + KT * R1_N


def build(nc, dram, out):
    ctx = ExitStack()
    with ctx:
        def sb(name, shape, dt=F32):
            return ctx.enter_context(nc.sbuf_tensor(name, shape, dt))

        owners, layer_sems = [ctx], []

        def sem(name):
            s = owners[-1].enter_context(nc.semaphore(name))
            layer_sems.append(s)
            return s

        def step(eng, s):
            count = [0]

            def run(ins):
                count[0] += 1
                ins.then_inc(s, 1)
                eng.wait_ge(s, count[0])
            return run

        ring = sb("ring", [P, RING, SLOT])
        hT = sb("hT", [P, KT, T])
        xnT = sb("xnT", [P, KT, T])
        cst = sb("cst", [P, CONST_TABLE.shape[1]])
        vec = sb("vec", [P, max(N1, N2)])
        vecg = sb("vecg", [P, NV])
        row = sb("row", [1, 64])
        small = sb("small", [P, SMALL1])
        rope_tab = sb("rope_tab", [P, 2, TT, ROPE // 2])
        ret_tab = sb("ret_tab", [P, 2, TT, P // 2])
        arena = sb("arena", [P, 17920])
        silu_c = sb("silu_c", [P, KT])
        mod = sb("mod", [P, 6 * KT])
        gains = sb("gains", [P, 2, KT])
        pc = sb("pc", [P, MT, TT * NCH])
        bank = [ctx.enter_context(nc.psum_tensor(f"bank{i}", [P, 512], F32)) for i in range(8)]

        def K(name, n=P):
            a, b = CONST[name]
            return cst[0:n, a:b]

        def V1(name):
            a, b = VEC1[name]
            return vec[:, a:b]

        def V2(name):
            a, b = VEC2[name]
            return vec[:, a:b]

        def VG(name):
            a, b = VECG[name]
            return vecg[:, a:b]

        def ar(at, *shape, n=P):
            size = int(np.prod(shape))
            v = arena[0:n, at:at + size]
            if len(shape) == 2:
                v = v.rearrange("p (a b) -> p a b", a=shape[0])
            if len(shape) == 3:
                v = v.rearrange("p (a b c) -> p a b c", a=shape[0], b=shape[1])
            return v

        w_loaded = [sem(f"w_loaded{s}") for s in range(RING)]
        w_used = sem("w_used")

        def load(sp, n, src, width=SLOT):
            if n >= RING:
                sp.wait_ge(w_used, n - RING + 1)
            sp.dma_start(ring[:, n % RING, 0:width], src).then_inc(w_loaded[n % RING], 16)

        def arrived(pe, n):
            pe.wait_ge(w_loaded[n % RING], 16 * (n // RING + 1))

        def chunk(n, kt, width):
            return ring[:, n % RING, 0:kt * width].rearrange("p (k w) -> p k w", k=kt)

        def setup():
            in_loaded = sem("in_loaded")
            s_dve = sem("setup_dve")
            angles = sem("angles_ready")
            pos_i = arena[:, 0:2 * TT].bitcast(I32)
            pos_f = ar(8, 2 * TT)
            turns = ar(16, 2, TT, 80)
            turns_i = arena[:, 400:400 + 320].bitcast(I32)
            ang = ar(800, 2, TT, 80)
            ang2 = ar(1200, 2, TT, 80)
            neg = ar(1600, 2, TT, 80)
            half = (ROPE // 2, P // 2)
            with nc.Block() as block:
                @block.sync
                def _(sp):
                    sp.dma_start(cst[:], dram["consts"]).then_inc(in_loaded, 16)
                    sp.dma_start(hT[:], dram["x"]).then_inc(in_loaded, 16)
                    sp.dma_start(vecg[:], dram["vecg"]).then_inc(in_loaded, 16)
                    sp.dma_start(pos_i[:, 0:TT], dram["positions"]).then_inc(in_loaded, 16)
                    sp.dma_start(pos_i[:, TT:2 * TT], dram["positions_2"]).then_inc(in_loaded, 16)

                @block.vector
                def _(dve):
                    then = step(dve, s_dve)
                    dve.wait_ge(in_loaded, 80)
                    then(nc.vector.tensor_copy(pos_f, pos_i))
                    for a in (ang, ang2):
                        then(nc.vector.memset(a, 0.0))
                    for w in range(2):
                        for t in range(TT):
                            then(nc.vector.tensor_scalar(ang[:, w, t, 0:half[w]], K(f"freq{half[w]}"),
                                                         pos_f[:, TT * w + t:TT * w + t + 1], None, ALU.mult))
                    flat, flat2 = ang.rearrange("p a b c -> p (a b c)"), ang2.rearrange("p a b c -> p (a b c)")
                    tf, nf = turns.rearrange("p a b c -> p (a b c)"), neg.rearrange("p a b c -> p (a b c)")
                    then(nc.vector.tensor_scalar(tf, flat, 1.0 / (2 * np.pi), None, ALU.mult))
                    then(nc.vector.tensor_copy(turns_i, tf))
                    then(nc.vector.tensor_copy(tf, turns_i))
                    c1 = 6.28125
                    c2 = float(np.float32(2 * np.pi - c1).view(np.uint32) & 0xFFFFF000)
                    c2 = float(np.uint32(int(c2)).view(np.float32))
                    c3 = float(2 * np.pi - c1 - c2)
                    for c in (c1, c2, c3):
                        then(nc.vector.scalar_tensor_tensor(flat, tf, -c, flat, ALU.mult, ALU.add))
                    for sign in (1.0, -1.0):
                        then(nc.vector.tensor_scalar(nf, flat, sign, float(np.pi), ALU.mult, ALU.is_gt))
                        then(nc.vector.scalar_tensor_tensor(flat, nf, -sign * 2 * float(np.pi), flat, ALU.mult, ALU.add))
                    then(nc.vector.tensor_scalar(flat, flat, float(np.float32(np.pi)) * (1 - 1e-7), -float(np.float32(np.pi)) * (1 - 1e-7), ALU.min, ALU.max))
                    then(nc.vector.scalar_tensor_tensor(flat2, flat, -1.0, flat, ALU.mult, ALU.max))
                    nc.vector.tensor_scalar(flat2, flat2, -1.0, float(np.pi / 2), ALU.mult, ALU.add).then_inc(angles, 1)

                @block.scalar
                def _(act):
                    act.wait_ge(angles, 1)
                    for w, tab in enumerate((rope_tab, ret_tab)):
                        nc.scalar.activation(tab[:, 0], ang2[:, w, :, 0:half[w]], ACT.Sin)
                        nc.scalar.activation(tab[:, 1], ang[:, w, :, 0:half[w]], ACT.Sin)

        def norm(tag, gain, shift, at, feed=None, dest=None):
            dest = xnT if dest is None else dest
            sq = ar(at, KT, T)
            rstd = ar(at + KT * T, T)
            sq_ready, sum_ready, ms_ready, root_ready, rstd_ready, scaled = (
                sem(f"{tag}_{n}") for n in ("sq", "sum", "ms", "root", "rstd", "scaled"))
            with nc.Block() as block:
                @block.sync
                def _(sp):
                    if feed:
                        feed(sp)

                @block.scalar
                def _(act):
                    for q in range(4):
                        nc.scalar.activation(sq[:, 2 * q:2 * q + 2, :], hT[:, 2 * q:2 * q + 2, :], ACT.Square).then_inc(sq_ready, 1)
                    act.wait_ge(ms_ready, 1)
                    nc.scalar.activation(rstd, rstd, ACT.Sqrt).then_inc(root_ready, 1)
                    if shift is not None:
                        for k in range(KT):
                            act.wait_ge(scaled, k + 1)
                            nc.scalar.activation(dest[:, k, :], sq[:, k, :], ACT.Identity, bias=shift[:, k:k + 1])

                @block.tensor
                def _(pe):
                    for k in range(KT):
                        pe.wait_ge(sq_ready, k // 2 + 1)
                        last = nc.tensor.matmul(bank[0][:, 0:T], K("ones"), sq[:, k, :], start=k == 0, stop=k == KT - 1)
                    last.then_inc(sum_ready, 1)

                @block.vector
                def _(dve):
                    dve.wait_ge(sum_ready, 1)
                    nc.vector.tensor_scalar(rstd, bank[0][:, 0:T], 1.0 / D, EPS, ALU.mult, ALU.add).then_inc(ms_ready, 1)
                    dve.wait_ge(root_ready, 1)
                    nc.vector.reciprocal(rstd, rstd).then_inc(rstd_ready, 1)
                    dve.wait_ge(rstd_ready, 1)
                    for k in range(KT):
                        o = dest if shift is None else sq
                        nc.vector.scalar_tensor_tensor(o[:, k, :], hT[:, k, :], gain[:, k:k + 1], rstd, ALU.mult,
                                                       ALU.mult).then_inc(scaled, 1)

        fqT, fkT = ar(0, 4, T), ar(1024, 4, T)
        fv = ar(2048, TT, MW)
        rest = ar(3072, TT, REST)
        latn = ar(3920, TT, QR + KVR)
        cqT, ckvT = ar(4688, 2, T), ar(5200, T)
        qS = ar(5456, TT, HEADS * QKD).rearrange("p t (h d) -> p t h d", d=QKD)
        kS = ar(6992, TT, HEADS * QKD).rearrange("p t (h d) -> p t h d", d=QKD)
        vS = ar(8528, TT, MW)
        qmT, kmT = ar(9552, HEADS, T, n=QKD), ar(11600, HEADS, T, n=QKD)
        mixT = ar(13648, KT, T)
        lf = ar(15696, TT, HEADS)
        uq = small[:, 0:2 * UQ_N].rearrange("p (k n) -> p k n", k=2)
        ukv = small[:, 2 * UQ_N:2 * UQ_N + UKV_N]
        wr1 = small[:, 2 * UQ_N + UKV_N:SMALL1].rearrange("p (k n) -> p k n", k=KT)
        MOE1 = 6

        def moe1_chunk(l, n):
            return dram["w_exp1"][l, n - MOE1]

        def project1(l):
            small_in = sem("small1_in")
            with nc.Block() as block:
                @block.sync
                def _(sp):
                    sp.dma_start(small[:], dram["small1"][l]).then_inc(small_in, 16)
                    for n in range(MOE1, MOE1 + 4):
                        load(sp, n, moe1_chunk(l, n))
                    sp.wait_ge(small_in, 16)

                @block.tensor
                def _(pe):
                    for n in range(2):
                        arrived(pe, n)
                        w = chunk(n, KT, MW)
                        for j in range(4):
                            for k in range(KT):
                                last = nc.tensor.matmul(bank[2 * n + j // 2][:, T * (j % 2):T * (j % 2) + T], w[:, k, P * j:P * j + P],
                                                        xnT[:, k, :], start=k == 0, stop=k == KT - 1)
                        last.then_inc(w_used, 1)
                    for n, width in ((2, MW), (3, REST)):
                        arrived(pe, n)
                        w = chunk(n, KT, width)
                        for t in range(TT):
                            o = bank[2 * n + t]
                            for k in range(KT):
                                last = nc.tensor.matmul(o[:, 0:width], xnT[:, k, P * t:P * t + P], w[:, k, :],
                                                        start=k == 0, stop=k == KT - 1)
                                if k == 0 and n == 3:
                                    nc.tensor.matmul(o[:, 0:HEADS], K("ones", 1), row[0:1, 0:HEADS], start=False, stop=False)
                        last.then_inc(w_used, 1)

                dests = [fqT[:, 0:2], fqT[:, 2:4], fkT[:, 0:2], fkT[:, 2:4], fv[:, 0], fv[:, 1], rest[:, 0], rest[:, 1]]

                @block.scalar
                def _(act):
                    for b in (0, 2, 4, 6):
                        act.wait_ge(w_used, b // 2 + 1)
                        nc.scalar.copy(dests[b], bank[b][:, 0:REST if b == 6 else 512])

                @block.vector
                def _(dve):
                    for b in (1, 3, 5, 7):
                        dve.wait_ge(w_used, b // 2 + 1)
                        nc.vector.tensor_copy(dests[b], bank[b][:, 0:REST if b == 7 else 512])

        def rotate(then, x1, x2, cos, sin, tmp):
            for o, a, b in ((tmp[0], x1, cos), (tmp[1], x2, sin), (tmp[2], x2, cos)):
                nc.vector.tensor_tensor(o, a, b, ALU.mult)
            then(nc.vector.tensor_tensor(tmp[3], x1, sin, ALU.mult))
            nc.vector.tensor_tensor(x1, tmp[0], tmp[1], ALU.subtract)
            then(nc.vector.tensor_tensor(x2, tmp[2], tmp[3], ALU.add))

        def latents():
            sq_ready, ms_ready, root_ready, lat_ready, turned, lat_T, q_ready, kv_ready, kv_ready2, q_in_sbuf, forget_e, forget_l = (
                sem(f"lat_{n}") for n in ("sq", "ms", "root", "lat", "turned", "T", "q", "kv", "kv2", "qsb", "fe", "fl"))
            s_dve = sem("lat_dve")
            junk = ar(9552, QR)
            ss = ar(15712, 4)
            e = ar(15720, TT, HEADS)
            kr = rest[:, :, REST - ROPE:REST]
            kr1, kr2 = kr[:, :, 0:ROPE // 2], kr[:, :, ROPE // 2:ROPE]
            tmp = [ar(9900 + 256 * i, TT, HEADS * ROPE // 2).rearrange("p t (h d) -> p t h d", h=HEADS) for i in range(4)]
            tmpk = [ar(9900 + 32 * i, TT, ROPE // 2) for i in range(4)]
            fl = rest[:, :, 0:HEADS]
            with nc.Block() as block:
                @block.scalar
                def _(act):
                    for i in range(4):
                        t, lo, n = i % 2, (HEADS, HEADS + QR)[i // 2], (QR, KVR)[i // 2]
                        nc.scalar.activation(junk[:, 0:n], rest[:, t, lo:lo + n], ACT.Square, accum_out=ss[:, i:i + 1]).then_inc(sq_ready, 1)
                        act.wait_ge(sq_ready, i + 1)
                    act.wait_ge(ms_ready, 1)
                    nc.scalar.activation(ss, ss, ACT.Sqrt).then_inc(root_ready, 1)
                    act.wait_ge(forget_e, 1)
                    nc.scalar.activation(e, e, ACT.Exp, scale=-1.0).then_inc(forget_l, 1)
                    act.wait_ge(forget_l, 1)
                    nc.scalar.activation(e, e, ACT.Ln, bias=1.0).then_inc(forget_l, 1)
                    for t in range(TT):
                        act.wait_ge(q_ready, t + 1)
                        for g in range(2):
                            nc.scalar.copy(qS[:, t, 4 * g:4 * g + 4, :], bank[2 + 2 * t + g][:, 0:4 * QKD]).then_inc(q_in_sbuf, 1)
                    for t in range(TT):
                        act.wait_ge((kv_ready, kv_ready2)[t], 1)
                        for g in range(2):
                            kv = bank[(6, 0)[t] + g][:, :].rearrange("p (h d) -> p h d", h=4)
                            nc.scalar.copy(kS[:, t, 4 * g:4 * g + 4, 0:NOPE], kv[:, :, 0:NOPE])
                            nc.scalar.copy(vS[:, t, 256 * g:256 * g + 256].rearrange("p (h d) -> p h d", h=4), kv[:, :, NOPE:NOPE + HD])

                @block.vector
                def _(dve):
                    then = step(dve, s_dve)
                    dve.wait_ge(sq_ready, 4)
                    nc.vector.tensor_scalar(ss[:, 0:2], ss[:, 0:2], 1.0 / QR, EPS, ALU.mult, ALU.add)
                    nc.vector.tensor_scalar(ss[:, 2:4], ss[:, 2:4], 1.0 / KVR, EPS, ALU.mult, ALU.add).then_inc(ms_ready, 1)
                    dve.wait_ge(root_ready, 1)
                    then(nc.vector.reciprocal(ss, ss))
                    for i in range(4):
                        t, lo, n = i % 2, (HEADS, HEADS + QR)[i // 2], (QR, KVR)[i // 2]
                        nc.vector.tensor_scalar(latn[:, t, lo - HEADS:lo - HEADS + n], rest[:, t, lo:lo + n], ss[:, i:i + 1], None,
                                                ALU.mult).then_inc(lat_ready, 1)
                    nc.vector.scalar_tensor_tensor(e, fl, -1.0, fl, ALU.mult, ALU.max).then_inc(forget_e, 1)
                    rotate(then, kr1, kr2, rope_tab[:, 0], rope_tab[:, 1], tmpk)
                    nc.vector.tensor_copy(kS[:, :, :, NOPE:QKD], kr.unsqueeze(2).broadcast_to([P, TT, HEADS, ROPE]))
                    dve.wait_ge(turned, 1)
                    for j in range(2):
                        nc.vector.tensor_scalar(cqT[:, j, :], bank[0][:, T * j:T * j + T], V1("q_norm")[:, j:j + 1], None, ALU.mult).then_inc(lat_T, 1)
                    nc.vector.tensor_scalar(ckvT, bank[1][:, 0:T], V1("kv_norm"), None, ALU.mult).then_inc(lat_T, 1)
                    dve.wait_ge(forget_l, 2)
                    nc.vector.scalar_tensor_tensor(lf, fl, 0.0, e, ALU.min, ALU.subtract)
                    dve.wait_ge(q_in_sbuf, 4)
                    cos, sin = (rope_tab[:, i].unsqueeze(2).broadcast_to([P, TT, HEADS, ROPE // 2]) for i in range(2))
                    rotate(then, qS[:, :, :, NOPE:NOPE + ROPE // 2], qS[:, :, :, NOPE + ROPE // 2:QKD], cos, sin, tmp)

                @block.tensor
                def _(pe):
                    pe.wait_ge(lat_ready, 4)
                    for j in range(3):
                        for t in range(TT):
                            last = nc.tensor.transpose(bank[j // 2][:, T * (j % 2) + P * t:T * (j % 2) + P * t + P],
                                                       latn[:, t, P * j:P * j + P], K("ident"))
                    last.then_inc(turned, 1)
                    pe.wait_ge(lat_T, 3)
                    for t in range(TT):
                        for g in range(2):
                            for k in range(2):
                                last = nc.tensor.matmul(bank[2 + 2 * t + g][:, 0:4 * QKD], cqT[:, k, P * t:P * t + P],
                                                        uq[:, k, 4 * QKD * g:4 * QKD * g + 4 * QKD], start=k == 0, stop=k == 1)
                        last.then_inc(q_ready, 1)
                    for t in range(TT):
                        for g in range(2):
                            last = nc.tensor.matmul(bank[(6, 0)[t] + g][:, :], ckvT[:, P * t:P * t + P], ukv[:, 512 * g:512 * g + 512],
                                                    start=True, stop=True)
                        last.then_inc((kv_ready, kv_ready2)[t], 1)

        def turn_qk():
            turned = sem("qk_turned")
            with nc.Block() as block:
                @block.tensor
                def _(pe):
                    for b in range(8):
                        src = (qS, kS)[b // 4]
                        for i in range(2):
                            for t in range(TT):
                                last = nc.tensor.transpose(bank[b][0:QKD, T * i + P * t:T * i + P * t + P], src[:, t, 2 * (b % 4) + i, :], K("ident"))
                        last.then_inc(turned, 1)

                def to_sbuf(eng, copy, banks):
                    for b in banks:
                        eng.wait_ge(turned, b + 1)
                        copy((qmT, kmT)[b // 4][:, 2 * (b % 4):2 * (b % 4) + 2, :], bank[b][0:QKD, :].rearrange("p (h t) -> p h t", h=2))

                @block.scalar
                def _(act):
                    to_sbuf(act, nc.scalar.copy, (0, 2, 4, 6))

                @block.vector
                def _(dve):
                    to_sbuf(dve, nc.vector.tensor_copy, (1, 3, 5, 7))

        def attention():
            NH = 2 * HEADS
            COLS = P + T
            z_free, decay_ready, scores_ready, z_ready, top_ready, e_ready, r_ready, p_ready, p_turned, pT_ready, out_ready, out_taken = (
                sem(f"att_{n}") for n in ("zfree", "decay", "scores", "z", "top", "e", "r", "p", "turned", "pT", "out", "taken"))
            s_dve = sem("att_dve")
            Z = [ar(3920 + 512 * i, TT, T) for i in range(2)]
            zb = [ar(5456 + 384 * i, COLS) for i in range(2)]
            pT = [ar(6224 + 384 * i, COLS) for i in range(2)]
            top = [ar(15712 + 2 * i, 2) for i in range(2)]
            tot = [ar(15716 + 2 * i, 2) for i in range(2)]
            rec = [ar(15720 + 2 * i, 2) for i in range(2)]
            parts = ((0, P), (P, COLS))
            scale = (HD ** -0.5, QKD ** -0.5)

            def q_of(h):
                return fqT[HD * (h % 2):HD * (h % 2) + HD, h // 2, :] if h < HEADS else qmT[:, h - HEADS, :]

            def k_of(h):
                return fkT[HD * (h % 2):HD * (h % 2) + HD, h // 2, :] if h < HEADS else kmT[:, h - HEADS, :]

            def v_of(h, t):
                return (fv if h < HEADS else vS)[:, t, HD * (h % HEADS):HD * (h % HEADS) + HD]

            with nc.Block() as block:
                @block.tensor
                def _(pe):
                    def scores(h):
                        o = bank[h % 2]
                        if h >= 2:
                            pe.wait_ge(z_ready, h - 1)
                        fox = h < HEADS
                        if fox:
                            pe.wait_ge(decay_ready, h + 1)
                        for t, (a, b) in enumerate(parts):
                            last = nc.tensor.matmul(o[:, a:b], q_of(h)[:, P * t:P * t + P], k_of(h)[:, 0:b - a], start=True, stop=not fox)
                            if fox:
                                last = nc.tensor.matmul(o[:, a:b], K("ones"), Z[h % 2][:, 0, 0:b - a], start=False, stop=t == 0)
                                if t == 1:
                                    last = nc.tensor.matmul(o[:, a + P:b], K("ones"), Z[h % 2][:, 1, P:T], start=False, stop=True)
                        last.then_inc(scores_ready, 1)

                    def turn(h):
                        pe.wait_ge(p_ready, 2 * h + 2)
                        if h >= 2:
                            pe.wait_ge(pT_ready, h - 1)
                        for i in range(3):
                            last = nc.tensor.transpose(bank[2 + h % 2][:, P * i:P * i + P], zb[h % 2][:, P * i:P * i + P], K("ident"))
                        last.then_inc(p_turned, 1)

                    def product(h):
                        pe.wait_ge(pT_ready, h + 1)
                        if h % 2 == 0 and h >= 4:
                            pe.wait_ge(out_taken, h // 2 - 1)
                        o = bank[4 + h // 2 % 2][HD * (h % 2):HD * (h % 2) + HD, :]
                        nc.tensor.matmul(o[:, 0:T], v_of(h, 0), pT[h % 2][:, 0:T], start=True, stop=False)
                        nc.tensor.matmul(o[:, P:T], v_of(h, 1), pT[h % 2][:, T:COLS], start=False, stop=True).then_inc(out_ready, 1)

                    for i in range(NH + 2):
                        if i < NH:
                            scores(i)
                        if 1 <= i <= NH:
                            turn(i - 1)
                        if i >= 2:
                            product(i - 2)

                @block.vector
                def _(dve):
                    then = step(dve, s_dve)

                    def decays(h):
                        if h >= 2:
                            dve.wait_ge(scores_ready, h - 1)
                        for s in range(TT):
                            last = nc.vector.tensor_scalar(Z[h % 2][:, s, :], K("tri")[:, T * s:T * s + T], lf[:, s, h:h + 1], -1.0 / scale[0],
                                                           ALU.mult, ALU.mult)
                        last.then_inc(decay_ready, 1)

                    def softmax(h):
                        z = zb[h % 2]
                        dve.wait_ge(scores_ready, h + 1)
                        if h >= 2:
                            dve.wait_ge(p_turned, h - 1)
                        nc.vector.scalar_tensor_tensor(z, bank[h % 2][:, 0:COLS], scale[h // HEADS], K("causal"), ALU.mult, ALU.add).then_inc(z_ready, 1)
                        dve.wait_ge(z_ready, h + 1)
                        for t, (a, b) in enumerate(parts):
                            last = nc.vector.tensor_reduce(top[h % 2][:, t:t + 1], z[:, a:b], AX, ALU.max, negate=True)
                        last.then_inc(top_ready, 1)

                    def finish(h):
                        dve.wait_ge(e_ready, 2 * h + 2)
                        nc.vector.reciprocal(rec[h % 2], tot[h % 2]).then_inc(r_ready, 1)
                        dve.wait_ge(r_ready, h + 1)
                        for t, (a, b) in enumerate(parts):
                            nc.vector.tensor_scalar(zb[h % 2][:, a:b], zb[h % 2][:, a:b], rec[h % 2][:, t:t + 1], None, ALU.mult).then_inc(p_ready, 1)

                    def take(j):
                        dve.wait_ge(out_ready, 2 * j + 2)
                        nc.vector.tensor_copy(mixT[:, j, :], bank[4 + j % 2][:, 0:T]).then_inc(out_taken, 1)

                    decays(0)
                    for i in range(NH + 3):
                        if i + 1 < HEADS:
                            decays(i + 1)
                        if i < NH:
                            softmax(i)
                            finish(i)
                        if i >= 3 and (i - 3) % 2 == 1:
                            take((i - 3) // 2)

                @block.scalar
                def _(act):
                    def exps(h):
                        act.wait_ge(top_ready, h + 1)
                        for t, (a, b) in enumerate(parts):
                            nc.scalar.activation(zb[h % 2][:, a:b], zb[h % 2][:, a:b], ACT.Exp, bias=top[h % 2][:, t:t + 1],
                                                 accum_out=tot[h % 2][:, t:t + 1]).then_inc(e_ready, 1)

                    def to_sbuf(h):
                        act.wait_ge(p_turned, h + 1)
                        if h >= 2:
                            act.wait_ge(out_ready, h - 1)
                        nc.scalar.copy(pT[h % 2], bank[2 + h % 2][:, 0:COLS]).then_inc(pT_ready, 1)

                    for i in range(NH + 1):
                        if i < NH:
                            exps(i)
                        if i >= 1:
                            to_sbuf(i - 1)

        def head_rms_out(l):
            sq_ready, sums_ready, ms_ready, root_ready, rstd_ready, mix_ready = (
                sem(f"mix_{n}") for n in ("sq", "sums", "ms", "root", "rstd", "ready"))
            sq = ar(5456, KT, T)
            gain = vec[:, VEC1["fox_out_norm"][0]:VEC1["mla_out_norm"][1]]
            with nc.Block() as block:
                @block.sync
                def _(sp):
                    for n in range(MOE1 + 4, MOE1 + 6):
                        load(sp, n, moe1_chunk(l, n))

                @block.scalar
                def _(act):
                    for b in range(4):
                        nc.scalar.activation(sq[:, 2 * b:2 * b + 2, :], mixT[:, 2 * b:2 * b + 2, :], ACT.Square).then_inc(sq_ready, 1)
                    for b in range(4):
                        act.wait_ge(ms_ready, b + 1)
                        nc.scalar.activation(sq[:, 2 * b:2 * b + 2, :], sq[:, 2 * b:2 * b + 2, :], ACT.Sqrt).then_inc(root_ready, 1)

                @block.tensor
                def _(pe):
                    for b in range(4):
                        pe.wait_ge(sq_ready, b + 1)
                        nc.tensor.matmul(bank[b][:, :], K("blk64"), sq[:, 2 * b:2 * b + 2, :], start=True, stop=True).then_inc(sums_ready, 1)
                    pe.wait_ge(mix_ready, KT)
                    for n in range(4, 6):
                        arrived(pe, n)
                        w = chunk(n, KT, MW)
                        for j in range(4):
                            b = 4 + 2 * (n - 4) + j // 2
                            for k in range(KT):
                                last = nc.tensor.matmul(bank[b][:, T * (j % 2):T * (j % 2) + T], w[:, k, P * j:P * j + P], mixT[:, k, :],
                                                        start=k == 0, stop=k == KT - 1)
                        last.then_inc(w_used, 1)

                @block.vector
                def _(dve):
                    for b in range(4):
                        dve.wait_ge(sums_ready, b + 1)
                        nc.vector.tensor_scalar(sq[:, 2 * b:2 * b + 2, :], bank[b][:, :], 1.0 / HD, EPS, ALU.mult, ALU.add).then_inc(ms_ready, 1)
                    for b in range(4):
                        dve.wait_ge(root_ready, b + 1)
                        nc.vector.reciprocal(sq[:, 2 * b:2 * b + 2, :], sq[:, 2 * b:2 * b + 2, :]).then_inc(rstd_ready, 1)
                    for j in range(KT):
                        dve.wait_ge(rstd_ready, j // 2 + 1)
                        nc.vector.scalar_tensor_tensor(mixT[:, j, :], mixT[:, j, :], gain[:, j:j + 1], sq[:, j, :], ALU.mult,
                                                       ALU.mult).then_inc(mix_ready, 1)
                    for n in range(4, 6):
                        dve.wait_ge(w_used, n + 1)
                        for i in range(2):
                            j = 4 * (n - 4) + 2 * i
                            nc.vector.tensor_tensor(hT[:, j:j + 2, :], hT[:, j:j + 2, :], bank[4 + 2 * (n - 4) + i][:, :], ALU.add)

        qt, kt_, vt = (ar(1024 * i, TT, MW) for i in range(3))
        sgT = ar(3072, MT, T)
        mixed = ar(4096, 14, T)
        rT, kT, vT = (ar(4096 + 1024 * i, MT, T) for i in range(3))
        lowT = ar(7168, 2, T)
        convT = [ar(7680 + 1024 * i, MT, T) for i in range(3)]
        y_ret, y_rwkv, y_conv = (ar(10752 + 1024 * i, MT, T) for i in range(3))
        lora_wa, lora_g = small[:, 0:MW], small[:, MW:2 * MW]
        wr2 = small[:, 2 * MW:2 * MW + KT * R2_N].rearrange("p (k n) -> p k n", k=KT)
        ADA, IN2, LORA, CONV, MERGE, OUT2, MOE2 = 0, 12, 19, 20, 23, 32, 34

        def load2(sp, l, n):
            if n < IN2:
                load(sp, n, dram["w_ada2"][l, n])
            elif n < LORA:
                load(sp, n, dram["w_in2"][l, n - IN2])
            elif n == LORA:
                load(sp, n, dram["w_low2"][l], KT * 2 * P)
            elif n < MERGE:
                load(sp, n, dram["w_conv2"][l, n - CONV])
            elif n < OUT2:
                load(sp, n, dram["w_merge2"][l, n - MERGE])
            elif n < MOE2:
                load(sp, n, dram["w_o2"][l, n - OUT2])
            else:
                load(sp, n, dram["w_exp2"][l, n - MOE2])

        def modulation(l):
            c_ready, mod_ready, small_in = sem("ada_c"), sem("ada_mod"), sem("small2_in")
            with nc.Block() as block:
                @block.sync
                def _(sp):
                    sp.dma_start(small[:, 0:2 * MW + KT * R2_N], dram["small2"][l]).then_inc(small_in, 16)
                    for n in range(RING, IN2 + RING):
                        load2(sp, l, n)
                    sp.wait_ge(small_in, 16)

                @block.scalar
                def _(act):
                    nc.scalar.activation(silu_c[:], VG("c_2"), ACT.Silu).then_inc(c_ready, 1)

                @block.tensor
                def _(pe):
                    pe.wait_ge(c_ready, 1)
                    for n in range(12):
                        arrived(pe, n)
                        w = chunk(n, KT, MW)
                        for j in range(4):
                            for k in range(KT):
                                last = nc.tensor.matmul(bank[0][:, 4 * n + j:4 * n + j + 1], w[:, k, P * j:P * j + P], silu_c[:, k:k + 1],
                                                        start=k == 0, stop=k == KT - 1)
                        last.then_inc(w_used, 1)

                @block.vector
                def _(dve):
                    dve.wait_ge(w_used, 12)
                    nc.vector.tensor_tensor(mod[:], bank[0][:, 0:48], V2("b_ada_2"), ALU.add).then_inc(mod_ready, 1)
                    dve.wait_ge(mod_ready, 1)
                    for i, g in enumerate(("norm1_g_2", "norm2_g_2")):
                        nc.vector.scalar_tensor_tensor(gains[:, i, :], mod[:, 24 * i + 8:24 * i + 16], 1.0, V2(g), ALU.add, ALU.mult)

        def project2(l):
            taken = [sem("p2_act_taken"), sem("p2_dve_taken")]
            loads = []
            for n in range(3):
                loads += [(IN2 + n, (qt, kt_, vt)[n][:, t, :], MW) for t in range(TT)]
            for n, d in ((3, sgT), (4, rT), (5, kT), (6, vT)):
                loads += [(IN2 + n, d[:, 2 * i:2 * i + 2, :], MW) for i in range(2)]
            loads += [(LORA, lowT, MW)]
            for n in range(3):
                loads += [(CONV + n, convT[n][:, 2 * i:2 * i + 2, :], MW) for i in range(2)]
            with nc.Block() as block:
                @block.sync
                def _(sp):
                    for n in range(IN2 + RING, MERGE + RING):
                        load2(sp, l, n)

                @block.tensor
                def _(pe):
                    for i, (n, d, width) in enumerate(loads):
                        o = bank[i % 8]
                        first = i == 0 or loads[i - 1][0] != n
                        if first:
                            arrived(pe, n)
                        if i >= 8:
                            pe.wait_ge(taken[i % 2], (i - 8) // 2 + 1)
                        if n < IN2 + 3:
                            w = chunk(n, KT, MW)
                            for k in range(KT):
                                last = nc.tensor.matmul(o[:, 0:MW], xnT[:, k, P * (not first):P * (not first) + P], w[:, k, :], start=k == 0, stop=k == KT - 1)
                        else:
                            w = chunk(n, KT, 2 * P if n == LORA else MW)
                            for j in range(2):
                                for k in range(KT):
                                    col = P * (j + 2 * (not first))
                                    last = nc.tensor.matmul(o[:, T * j:T * j + T], w[:, k, col:col + P], xnT[:, k, :], start=k == 0, stop=k == KT - 1)
                        if i + 1 == len(loads) or loads[i + 1][0] != n:
                            last.then_inc(w_used, 1)

                def take(eng, copy, parity):
                    for i, (n, d, width) in enumerate(loads):
                        if i % 2 == parity:
                            eng.wait_ge(w_used, n + 1)
                            copy(d, bank[i % 8][:, 0:width]).then_inc(taken[parity], 1)

                @block.scalar
                def _(act):
                    take(act, nc.scalar.copy, 0)

                @block.vector
                def _(dve):
                    take(dve, nc.vector.tensor_copy, 1)

        def shift_and_convolve():
            s_dve, s_act = sem("conv_dve"), sem("conv_act")
            before = ar(13824, 14, T)
            mu, cw = V2("rwkv_mu_2"), V2("conv_w_2")
            h, b, c = convT
            with nc.Block() as block:
                @block.scalar
                def _(act):
                    nc.scalar.activation(sgT, sgT, ACT.Silu)

                @block.vector
                def _(dve):
                    then = step(dve, s_dve)
                    nc.vector.tensor_tensor(before[:, :, 1:T], mixed[:, :, 0:T - 1], mixed[:, :, 1:T], ALU.subtract)
                    nc.vector.tensor_scalar(before[:, :, 0:1], mixed[:, :, 0:1], -1.0, None, ALU.mult)
                    then(nc.vector.tensor_tensor(c, c, h, ALU.mult))
                    for j in range(14):
                        nc.vector.scalar_tensor_tensor(mixed[:, j, :], before[:, j, :], mu[:, j:j + 1], mixed[:, j, :], ALU.mult, ALU.add)
                    for j in range(MT):
                        last = nc.vector.tensor_scalar(y_conv[:, j, :], c[:, j, :], cw[:, 2 * MT + j:2 * MT + j + 1], None, ALU.mult)
                    then(last)
                    for d in (1, 2):
                        for j in range(MT):
                            col = (2 - d) * MT + j
                            last = nc.vector.scalar_tensor_tensor(y_conv[:, j, d:T], c[:, j, 0:T - d], cw[:, col:col + 1], y_conv[:, j, d:T], ALU.mult, ALU.add)
                        then(last)
                    nc.vector.tensor_tensor(y_conv, y_conv, b, ALU.mult)

        def retention():
            rot_ready, turned, qk_ready, s_ready, st_ready, o_ready, o_taken = (sem(f"ret_{n}") for n in ("rot", "turned", "qk", "s", "st", "o", "taken"))
            s_dve = sem("ret_dve")
            tmp = [ar(13824 + 512 * i, TT, 4 * 64).rearrange("p t (h d) -> p t h d", h=RH) for i in range(4)]
            qd, kd = ar(15872, RH, P), ar(16384, RH, P)
            tr = [ar(7680 + 512 * i, RH, P) for i in range(5)]
            st = [ar(13824 + 512 * i, RH, P) for i in range(2)]
            state = ar(14848, RH, P)
            def halves(x):
                v = x.rearrange("p t (h d) -> p t h d", h=RH)
                return v[:, :, :, 0:64], v[:, :, :, 64:P]
            with nc.Block() as block:
                @block.vector
                def _(dve):
                    then = step(dve, s_dve)
                    cos, sin = (ret_tab[:, i].unsqueeze(2).broadcast_to([P, TT, RH, 64]) for i in range(2))
                    for x in (qt, kt_):
                        rotate(then, *halves(x), cos, sin, tmp)
                    heads = lambda x: x.rearrange("p (h d) -> p h d", h=RH)
                    nc.vector.tensor_tensor(qd, heads(qt[:, 1, :]), K("ret_q").unsqueeze(2).broadcast_to([P, RH, P]), ALU.mult).then_inc(rot_ready, 1)
                    nc.vector.tensor_tensor(kd, heads(kt_[:, 0, :]), K("ret_k").unsqueeze(2).broadcast_to([P, RH, P]), ALU.mult).then_inc(rot_ready, 1)
                    for i in range(5):
                        dve.wait_ge(turned, i + 1)
                        nc.vector.tensor_copy(tr[i], bank[i][:, :]).then_inc(qk_ready, 1)
                    dve.wait_ge(s_ready, 1)
                    nc.vector.tensor_copy(state, bank[7][:, :]).then_inc(st_ready, 1)
                    for t in range(TT):
                        dve.wait_ge(s_ready, t + 2)
                        nc.vector.tensor_tensor(st[t], bank[5 + t][:, :], K("ret_in"), ALU.mult).then_inc(st_ready, 1)
                    for i in range(2):
                        dve.wait_ge(o_ready, i + 1)
                        nc.vector.tensor_copy(y_ret[:, 2 * i:2 * i + 2, :], bank[i][:, :]).then_inc(o_taken, 1)

                @block.tensor
                def _(pe):
                    pe.wait_ge(rot_ready, 2)
                    srcs = [qt[:, 0, :], qt[:, 1, :], kt_[:, 0, :], kt_[:, 1, :], qd.rearrange("p h d -> p (h d)")]
                    for i, x in enumerate(srcs):
                        for h in range(RH):
                            last = nc.tensor.transpose(bank[i][:, P * h:P * h + P], x[:, P * h:P * h + P], K("ident"))
                        last.then_inc(turned, 1)
                    for h in range(RH):
                        last = nc.tensor.matmul(bank[7][:, P * h:P * h + P], kd[:, h, :], vt[:, 0, P * h:P * h + P], start=True, stop=True)
                    last.then_inc(s_ready, 1)
                    pe.wait_ge(qk_ready, 5)
                    for t in range(TT):
                        for h in range(RH):
                            last = nc.tensor.matmul(bank[5 + t][:, P * h:P * h + P], tr[2 + t][:, h, :], tr[t][:, h, :], start=True, stop=True)
                        last.then_inc(s_ready, 1)
                    pe.wait_ge(st_ready, 3)
                    for h in range(RH):
                        for t in range(TT):
                            o = bank[h // 2][:, T * (h % 2) + P * t:T * (h % 2) + P * t + P]
                            last = nc.tensor.matmul(o, vt[:, t, P * h:P * h + P], st[t][:, h, :], start=True, stop=t == 0)
                            if t:
                                last = nc.tensor.matmul(o, state[:, h, :], tr[4][:, h, :], start=False, stop=True)
                        if h % 2:
                            last.then_inc(o_ready, 1)

        def head_norm(tag, y, sq, sums, n, eps, gain, finish):
            mean_ready, flat, sq_ready, var_ready, ms_ready, root_ready = (sem(f"{tag}_{x}") for x in ("mean", "flat", "sq", "var", "ms", "root"))
            s_dve = sem(f"{tag}_dve")
            with nc.Block() as block:
                @block.tensor
                def _(pe):
                    for i in range(2):
                        nc.tensor.matmul(bank[i][:, :], K(sums), y[:, 2 * i:2 * i + 2, :], start=True, stop=True).then_inc(mean_ready, 1)
                    for i in range(2):
                        pe.wait_ge(sq_ready, i + 1)
                        nc.tensor.matmul(bank[2 + i][:, :], K(sums), sq[:, 2 * i:2 * i + 2, :], start=True, stop=True).then_inc(var_ready, 1)

                @block.scalar
                def _(act):
                    for i in range(2):
                        act.wait_ge(flat, i + 1)
                        nc.scalar.activation(sq[:, 2 * i:2 * i + 2, :], y[:, 2 * i:2 * i + 2, :], ACT.Square).then_inc(sq_ready, 1)
                    for i in range(2):
                        act.wait_ge(ms_ready, i + 1)
                        nc.scalar.activation(sq[:, 2 * i:2 * i + 2, :], sq[:, 2 * i:2 * i + 2, :], ACT.Sqrt).then_inc(root_ready, 1)

                @block.vector
                def _(dve):
                    then = step(dve, s_dve)
                    for i in range(2):
                        dve.wait_ge(mean_ready, i + 1)
                        nc.vector.scalar_tensor_tensor(y[:, 2 * i:2 * i + 2, :], bank[i][:, :].rearrange("p (a t) -> p a t", a=2), -1.0 / n,
                                                       y[:, 2 * i:2 * i + 2, :], ALU.mult, ALU.add).then_inc(flat, 1)
                    for i in range(2):
                        dve.wait_ge(var_ready, i + 1)
                        nc.vector.tensor_scalar(sq[:, 2 * i:2 * i + 2, :], bank[2 + i][:, :], 1.0 / n, eps, ALU.mult, ALU.add).then_inc(ms_ready, 1)
                    for i in range(2):
                        dve.wait_ge(root_ready, i + 1)
                        then(nc.vector.reciprocal(sq[:, 2 * i:2 * i + 2, :], sq[:, 2 * i:2 * i + 2, :]))
                    for j in range(MT):
                        last = nc.vector.scalar_tensor_tensor(y[:, j, :], y[:, j, :], gain[:, j:j + 1], sq[:, j, :], ALU.mult, ALU.mult)
                    then(last)
                    finish(then)

        wT, aT, gT = (ar(7680 + 1024 * i, MT, T) for i in range(3))
        khT, ktT, cumT, icumT, exT = ar(0, MT, T), ar(1024, MT, T), ar(2048, MT, T), ar(3072, MT, T), ar(13824, MT, T)
        qrT = ar(14848, MT * TT * 2, P).rearrange("p (j t i) s -> p j t i s", j=MT, t=TT)
        bT, kdT = aT, ktT
        bonus = cumT
        Vtok, Ktok, Btok = ar(0, TT, MW), ar(3072, TT, MW), ar(7680, TT, MW)
        X = ar(4096, TT * 4, 2 * P)
        X5 = X.rearrange("p q (w i d) -> p q w i d", w=2, i=2)

        def rwkv_inputs():
            low_ready, lora_ready, w_ready, a_ready, kk_ready, sq_ready, ss_ready, ms_ready, root_ready, rk_ready, rk_sum, kt_ready = (
                sem(f"wkv_{n}") for n in ("low", "lora", "w", "a", "kk", "sq", "ss", "ms", "root", "rk", "rksum", "kt"))
            s_dve, s_act = sem("wkv_dve"), sem("wkv_act")
            d0, d1 = ar(14848, MT, T), ar(15872, MT, T)
            sq = ar(16896, MT, T)
            def wide(name):
                return K(name).unsqueeze(1).broadcast_to([P, MT, T])
            with nc.Block() as block:
                @block.scalar
                def _(act):
                    nc.scalar.activation(lowT[0:64, 0, :], lowT[0:64, 0, :], ACT.Tanh).then_inc(low_ready, 1)
                    nc.scalar.activation(lowT[:, 1, :], lowT[:, 1, :], ACT.Sigmoid).then_inc(low_ready, 1)
                    for j in range(MT):
                        act.wait_ge(lora_ready, 1)
                        nc.scalar.activation(wT[:, j, :], bank[j // 2][:, T * (j % 2):T * (j % 2) + T], ACT.Sigmoid, bias=V2("rwkv_w0_2")[:, j:j + 1]).then_inc(s_act, 1)
                    for j in range(MT):
                        act.wait_ge(lora_ready, 2)
                        nc.scalar.activation(aT[:, j, :], bank[2 + j // 2][:, T * (j % 2):T * (j % 2) + T], ACT.Sigmoid, bias=V2("rwkv_a0_2")[:, j:j + 1]).then_inc(a_ready, 1)
                    act.wait_ge(s_act, 4)
                    nc.scalar.activation(wT, wT, ACT.Exp, scale=-float(np.exp(-0.5))).then_inc(w_ready, 1)
                    act.wait_ge(lora_ready, 3)
                    for i in range(2):
                        nc.scalar.copy(gT[:, 2 * i:2 * i + 2, :], bank[4 + i][:, :])
                    act.wait_ge(kk_ready, 1)
                    nc.scalar.activation(sq, khT, ACT.Square).then_inc(sq_ready, 1)
                    for i in range(2):
                        act.wait_ge(ms_ready, i + 1)
                        nc.scalar.activation(sq[:, 2 * i:2 * i + 2, :], sq[:, 2 * i:2 * i + 2, :], ACT.Sqrt).then_inc(root_ready, 1)

                @block.tensor
                def _(pe):
                    pe.wait_ge(low_ready, 2)
                    for i in range(3):
                        lo, hi, w, x = ((0, 64, lora_wa, lowT[:, 0, :]), (64, P, lora_wa, lowT[:, 0, :]), (0, P, lora_g, lowT[:, 1, :]))[i]
                        for j in range(MT):
                            last = nc.tensor.matmul(bank[2 * i + j // 2][:, T * (j % 2):T * (j % 2) + T], w[lo:hi, P * j:P * j + P], x[lo:hi, :], start=True, stop=True)
                        last.then_inc(lora_ready, 1)
                    pe.wait_ge(sq_ready, 1)
                    for i in range(2):
                        nc.tensor.matmul(bank[6 + i][:, :], K("blk64"), sq[:, 2 * i:2 * i + 2, :], start=True, stop=True).then_inc(ss_ready, 1)
                    pe.wait_ge(rk_ready, 1)
                    for i in range(2):
                        nc.tensor.matmul(bank[6 + i][:, :], K("blk64"), d0[:, 2 * i:2 * i + 2, :], start=True, stop=True).then_inc(rk_sum, 1)

                @block.vector
                def _(dve):
                    then = step(dve, s_dve)
                    for j in range(MT):
                        last = nc.vector.tensor_scalar(khT[:, j, :], kT[:, j, :], V2("rwkv_k_k_2")[:, j:j + 1], None, ALU.mult)
                    last.then_inc(kk_ready, 1)
                    for j in range(MT):
                        dve.wait_ge(a_ready, j + 1)
                        then(nc.vector.tensor_scalar(ktT[:, j, :], aT[:, j, :], -1.0, V2("rwkv_k_a_2")[:, j:j + 1], ALU.add, ALU.mult))
                    then(nc.vector.scalar_tensor_tensor(ktT, ktT, 1.0, kT, ALU.add, ALU.mult))
                    dve.wait_ge(w_ready, 1)
                    nc.vector.tensor_tensor(d0, wT, wide("inner"), ALU.mult)
                    then(nc.vector.tensor_tensor(d1, wT, wide("start"), ALU.mult))
                    flat = lambda x: x.rearrange("p j t -> p (j t)")
                    then(nc.vector.tensor_tensor_scan(flat(cumT), flat(d0), flat(d1), 0.0, ALU.mult, ALU.add))
                    nc.vector.memset(exT[:, :, 0:1], 1.0)
                    then(nc.vector.tensor_tensor(exT[:, :, 1:T], cumT[:, :, 0:T - 1], wide("inner")[:, :, 1:T], ALU.mult))
                    then(nc.vector.tensor_tensor(exT[:, :, 1:T], exT[:, :, 1:T], wide("start")[:, :, 1:T], ALU.add))
                    nc.vector.reciprocal(icumT, cumT)
                    nc.vector.tensor_copy(pc[:], cumT.rearrange("p j (c s) -> p j c s", s=CH)[:, :, :, CH - 1])
                    for j in range(MT):
                        last = nc.vector.scalar_tensor_tensor(d0[:, j, :], rT[:, j, :], V2("rwkv_r_k_2")[:, j:j + 1], ktT[:, j, :], ALU.mult, ALU.mult)
                    for i in range(2):
                        dve.wait_ge(ss_ready, i + 1)
                        nc.vector.tensor_scalar(sq[:, 2 * i:2 * i + 2, :], bank[6 + i][:, :], 1e-12, None, ALU.max).then_inc(ms_ready, 1)
                    for i in range(2):
                        dve.wait_ge(root_ready, i + 1)
                        then(nc.vector.reciprocal(sq[:, 2 * i:2 * i + 2, :], sq[:, 2 * i:2 * i + 2, :]))
                    nc.vector.tensor_tensor(khT, khT, sq, ALU.mult).then_inc(rk_ready, 1)
                    dve.wait_ge(rk_ready, 1)
                    nc.vector.tensor_tensor(rT, rT, cumT, ALU.mult)
                    nc.vector.tensor_tensor(exT, exT, khT, ALU.mult)
                    then(nc.vector.tensor_tensor(aT, aT, khT, ALU.mult))
                    nc.vector.tensor_tensor(bT, aT, icumT, ALU.mult)
                    then(nc.vector.tensor_tensor(kdT, ktT, icumT, ALU.mult))
                    for i in range(2):
                        dve.wait_ge(rk_sum, i + 1)
                        then(nc.vector.tensor_tensor(bonus[:, 2 * i:2 * i + 2, :], vT[:, 2 * i:2 * i + 2, :], bank[6 + i][:, :].rearrange("p (a t) -> p a t", a=2), ALU.mult))
                    for t in range(TT):
                        nc.vector.tensor_copy(qrT[:, :, t, 0, :], exT[:, :, P * t:P * t + P])
                        nc.vector.tensor_copy(qrT[:, :, t, 1, :], rT[:, :, P * t:P * t + P])

        def rwkv_turn():
            turned = sem("wkvt_turned")
            srcs = [(lambda j, t: qrT[:, j, t, 0, :], None), (lambda j, t: vT[:, j, P * t:P * t + P], Vtok),
                    (lambda j, t: kdT[:, j, P * t:P * t + P], Ktok), (lambda j, t: bT[:, j, P * t:P * t + P], Btok)]
            with nc.Block() as block:
                @block.tensor
                def _(pe):
                    for b in range(8):
                        for j in range(MT):
                            last = nc.tensor.transpose(bank[b][:, P * j:P * j + P], srcs[b // 2][0](j, b % 2), K("ident"))
                        last.then_inc(turned, 1)

                def take(eng, copy, t):
                    for i in range(4):
                        b = 2 * i + t
                        eng.wait_ge(turned, b + 1)
                        if i == 0:
                            copy(X[:, 4 * t:4 * t + 4, 0:P], bank[b][:, :].rearrange("p (q d) -> p q d", q=4))
                        else:
                            copy(srcs[i][1][:, t, :], bank[b][:, :])

                @block.scalar
                def _(act):
                    take(act, nc.scalar.copy, 0)

                @block.vector
                def _(dve):
                    take(dve, nc.vector.tensor_copy, 1)

        def rwkv_solve():
            mats, masked, akv_ready, x_ready, sq_done, pow_ready, x_prod, fin_ready, fin_taken, y_set = (
                sem(f"sol_{n}") for n in ("mats", "masked", "akv", "x", "sqr", "pow", "xprod", "fin", "taken", "yset"))
            s_dve = sem("sol_dve")
            M1, M2 = ar(6144, 4, 2 * P), ar(13824, 4, 2 * P)
            Lm = ar(7168, 4, P)
            powers = [ar(13824, 2, 512), ar(16896, 2, 512)]
            masks = cst[:, CONST["before"][0]:CONST["upto"][1]]
            groups = [(t, h) for t in range(TT) for h in (0, 4)]

            def part(x, h):
                return x[HD * (h % 2):HD * (h % 2) + HD]

            with nc.Block() as block:
                @block.tensor
                def _(pe):
                    for g, (t, h0) in enumerate(groups):
                        if g:
                            pe.wait_ge(fin_taken, 2 * g)
                            pe.wait_ge(pow_ready, 7 * g)
                        for x, b0 in ((kdT, 0), (bT, 2)):
                            for i in range(4):
                                h = h0 + i
                                last = nc.tensor.matmul(bank[b0 + i % 2][:, T * (i // 2):T * (i // 2) + T], part(x, h)[:, h // 2, P * t:P * t + P],
                                                        part(qrT, h)[:, h // 2, t, :, :], start=True, stop=True)
                            last.then_inc(mats, 1)
                        for i in range(4):
                            h = h0 + i
                            last = nc.tensor.matmul(bank[(4, 7)[i % 2]][:, P * (i // 2):P * (i // 2) + P], part(qrT, h)[:, h // 2, t, 0, :], part(bT, h)[:, h // 2, P * t:P * t + P],
                                                    start=True, stop=True)
                        last.then_inc(mats, 1)
                        pe.wait_ge(masked, 6 * g + 2)
                        for i in range(4):
                            h = h0 + i
                            nc.tensor.matmul(bank[5][:, HD * i:HD * i + HD], M2[:, i, 0:P], Vtok[:, t, HD * h:HD * h + HD], start=True, stop=True)
                            last = nc.tensor.matmul(bank[6][HD * (i % 2):HD * (i % 2) + HD, P * (i // 2):P * (i // 2) + P], Vtok[:, t, HD * h:HD * h + HD],
                                                    M2[:, i, P:2 * P], start=True, stop=True)
                        last.then_inc(akv_ready, 1)
                        pe.wait_ge(masked, 6 * g + 6)
                        for r in range(5):
                            if r == 0:
                                low = lambda i: Lm[:, i, :]
                                top = lambda i: M1[:, i, 0:P]
                            else:
                                pw = powers[(r - 1) % 2]
                                pe.wait_ge(pow_ready, 7 * g + (2 * r if r < 4 else 7))
                                low = lambda i, pw=pw: pw[:, 0, P * i:P * i + P]
                                top = lambda i, pw=pw: pw[:, 1, P * i:P * i + P]
                            if r < 4:
                                b0 = 2 * (r % 2)
                                for which in ((0, 1) if r < 3 else (1,)):
                                    for i in range(4):
                                        a, b = (top(i), low(i)) if which == 0 else (low(i), top(i))
                                        last = nc.tensor.matmul(bank[b0 + which][:, P * i:P * i + P], a, b, start=True, stop=True)
                                    last.then_inc(sq_done, 1)
                            pe.wait_ge(x_ready, 6 * g + r + 1)
                            for i in range(4):
                                o = bank[5][:, T * (i // 2):T * (i // 2) + T].rearrange("p (w i d) -> p w i d", w=2, i=2)[:, :, i % 2, :]
                                last = nc.tensor.matmul(o, top(i), X5[:, 4 * t + (h0 + i) // 2, :, i % 2, :], start=True, stop=True)
                            last.then_inc(x_prod, 1)
                        pe.wait_ge(x_ready, 6 * g + 6)
                        for i in range(4):
                            u = 4 * t + (h0 + i) // 2
                            rows, cols = slice(HD * (i % 2), HD * (i % 2) + HD), slice(P * (i // 2), P * (i // 2) + P)
                            nc.tensor.matmul(bank[6][rows, cols], X5[:, u, 0, i % 2, :], M1[:, i, P:2 * P], start=True, stop=True)
                            last = nc.tensor.matmul(bank[7][rows, cols], X5[:, u, 1, i % 2, :], M1[:, i, P:2 * P], start=True, stop=True)
                        last.then_inc(fin_ready, 1)

                @block.scalar
                def _(act):
                    for g in range(len(groups)):
                        for i in range(7):
                            act.wait_ge(sq_done, 7 * g + i + 1)
                            r, which = (i // 2, i % 2) if i < 6 else (3, 1)
                            nc.scalar.copy(powers[r % 2][:, which, :], bank[2 * (r % 2) + which][:, :]).then_inc(pow_ready, 1)

                @block.vector
                def _(dve):
                    for g, (t, h0) in enumerate(groups):
                        xs = X[:, 4 * t + h0 // 2:4 * t + h0 // 2 + 2, :]
                        ys = y_rwkv[:, h0 // 2:h0 // 2 + 2, P * t:P * t + P]
                        pair = masks.unsqueeze(1).broadcast_to([P, 2, 2 * P])
                        for m, dst in enumerate((M2, M1)):
                            dve.wait_ge(mats, 3 * g + m + 1)
                            for i in range(2):
                                nc.vector.tensor_tensor(dst[:, i:4:2, :], bank[2 * m + i][:, :].rearrange("p (a s) -> p a s", a=2), pair,
                                                        ALU.mult).then_inc(masked, 1)
                        dve.wait_ge(mats, 3 * g + 3)
                        for i in range(2):
                            nc.vector.tensor_tensor(Lm[:, i:4:2, :], bank[(4, 7)[i]][:, 0:T].rearrange("p (a s) -> p a s", a=2),
                                                    K("after").unsqueeze(1).broadcast_to([P, 2, P]), ALU.mult).then_inc(masked, 1)
                        dve.wait_ge(akv_ready, g + 1)
                        nc.vector.tensor_copy(xs[:, :, P:2 * P], bank[5][:, 0:2 * P].rearrange("p (q d) -> p q d", q=2)).then_inc(x_ready, 1)
                        nc.vector.tensor_copy(ys, bank[6][:, 0:T].rearrange("p (a s) -> p a s", a=2)).then_inc(y_set, 1)
                        for r in range(5):
                            dve.wait_ge(x_prod, 5 * g + r + 1)
                            px = bank[5][:, :].rearrange("p (q s) -> p q s", q=2)
                            if r == 0:
                                last = nc.vector.tensor_tensor(xs, xs, px, ALU.subtract)
                            elif r < 4:
                                last = nc.vector.tensor_tensor(xs, xs, px, ALU.add)
                            else:
                                last = nc.vector.scalar_tensor_tensor(xs, px, -1.0, xs, ALU.mult, ALU.subtract)
                            last.then_inc(x_ready, 1)
                        dve.wait_ge(fin_ready, g + 1)
                        dve.wait_ge(y_set, g + 1)
                        rs = qrT[:, h0 // 2:h0 // 2 + 2, t, 1, :]
                        nc.vector.tensor_tensor(rs, rs, bank[6][:, 0:T].rearrange("p (a s) -> p a s", a=2), ALU.add).then_inc(fin_taken, 1)
                        nc.vector.tensor_tensor(ys, ys, bank[7][:, 0:T].rearrange("p (a s) -> p a s", a=2), ALU.add).then_inc(fin_taken, 1)

        def rwkv_chain():
            wide_ready, gh_ready, gh_taken, next_ready, state_ready, y_ready, y_taken = (
                sem(f"chn_{n}") for n in ("wide", "gh", "taken", "next", "state", "y", "ytaken"))
            s_dve = sem("chn_dve")
            half_at = ((13824, 16896), (8704, 1024))
            G = [ar(half_at[q // 2][0] + 512 * (q % 2), NCH, P) for q in range(4)]
            H = [ar(half_at[q // 2][1] + 512 * (q % 2), NCH, P) for q in range(4)]
            wide = [ar(6144 + 512 * i, NCH, P) for i in range(3)]
            S = [qrT[:, :, i, 0, :] for i in range(2)]
            chunks = K("chunk").unsqueeze(2).broadcast_to([P, NCH, P])
            with nc.Block() as block:
                @block.tensor
                def _(pe):
                    for t in range(TT):
                        for q in range(4):
                            i = 4 * t + q
                            u = 4 * t + q
                            pe.wait_ge(wide_ready, 3 * (i + 1))
                            if i:
                                pe.wait_ge(gh_taken, 2 * i)
                            bs = Btok[:, t, P * q:P * q + P]
                            nc.tensor.matmul(bank[0][:, :], X[:, u, 0:P], wide[0], start=True, stop=True)
                            nc.tensor.matmul(bank[1][:, :], Ktok[:, t, P * q:P * q + P], wide[1], start=True, stop=False)
                            nc.tensor.matmul(bank[1][:, :], bs, wide[2], start=False, stop=True).then_inc(gh_ready, 1)
                        pe.wait_ge(gh_taken, 2 * (4 * t + 4))
                        for c in range(NCH):
                            n = NCH * t + c
                            pe.wait_ge(state_ready, n + 1)
                            if n:
                                pe.wait_ge(y_taken, n)
                            for q in range(4):
                                nc.tensor.matmul(bank[2][:, CH * q:CH * q + CH], S[n % 2][:, q, :], qrT[:, q, t, 1, CH * c:CH * c + CH], start=True, stop=True)
                            for q in range(4):
                                last = nc.tensor.matmul(bank[3][:, P * q:P * q + P], G[q][:, c, :], S[n % 2][:, q, :], start=True, stop=True)
                            last.then_inc(next_ready, 1)

                @block.vector
                def _(dve):
                    then = step(dve, s_dve)
                    nc.vector.memset(S[0], 0.0).then_inc(state_ready, 1)
                    for t in range(TT):
                        for q in range(4):
                            i = 4 * t + q
                            u = 4 * t + q
                            if i:
                                dve.wait_ge(gh_ready, i)
                            wideof = lambda x: x.unsqueeze(1).broadcast_to([P, NCH, P])
                            nc.vector.tensor_tensor(wide[0], wideof(Btok[:, t, P * q:P * q + P]), chunks, ALU.mult).then_inc(wide_ready, 1)
                            nc.vector.tensor_tensor(wide[1], wideof(Vtok[:, t, P * q:P * q + P]), chunks, ALU.mult).then_inc(wide_ready, 1)
                            nc.vector.tensor_tensor(wide[2], wideof(X[:, u, P:2 * P]), chunks, ALU.mult).then_inc(wide_ready, 1)
                            dve.wait_ge(gh_ready, i + 1)
                            blocks = K("blk64").unsqueeze(1).broadcast_to([P, NCH, P])
                            then(nc.vector.tensor_tensor(G[q], bank[0][:, :].rearrange("p (c s) -> p c s", c=NCH), blocks, ALU.mult))
                            nc.vector.tensor_tensor(G[q], G[q], K("ident").unsqueeze(1).broadcast_to([P, NCH, P]), ALU.add).then_inc(gh_taken, 1)
                            nc.vector.tensor_tensor(H[q], bank[1][:, :].rearrange("p (c s) -> p c s", c=NCH), blocks, ALU.mult).then_inc(gh_taken, 1)
                        dve.wait_ge(gh_taken, 2 * (4 * t + 4))
                        for c in range(NCH):
                            n = NCH * t + c
                            dve.wait_ge(next_ready, n + 1)
                            new = S[(n + 1) % 2]
                            for hf in range(2):
                                hh = ar(half_at[hf][1], 2, 512).rearrange("p q (c s) -> p q c s", c=NCH)[:, :, c, :]
                                last = nc.vector.tensor_tensor(new[:, 2 * hf:2 * hf + 2, :], bank[3][:, 2 * P * hf:2 * P * hf + 2 * P].rearrange("p (q s) -> p q s", q=2), hh, ALU.add)
                            then(last)
                            nc.vector.tensor_tensor(new, new, pc[:, :, n].unsqueeze(2).broadcast_to([P, 4, P]), ALU.mult).then_inc(state_ready, 1)
                            ys = y_rwkv[:, :, P * t + CH * c:P * t + CH * c + CH]
                            nc.vector.tensor_tensor(ys, ys, bank[2][:, 0:4 * CH].rearrange("p (q s) -> p q s", q=4), ALU.add).then_inc(y_taken, 1)

        merged = ar(14848, KT, T)

        def merge(l):
            pair_ready, gate_ready, taken, s_dve = sem("mrg_pair"), sem("mrg_gate"), sem("mrg_taken"), sem("mrg_dve")
            ys = (y_ret, y_rwkv, y_conv)
            sg = ar(13824, 4, T)
            tmp = ar(0, 2, T)
            with nc.Block() as block:
                @block.sync
                def _(sp):
                    for n in range(MERGE + RING, MOE2 + 4):
                        load2(sp, l, n)

                @block.tensor
                def _(pe):
                    for i in range(3):
                        n = MERGE + 3 * i
                        for d in range(KT):
                            m = KT * i + d
                            if d % 4 == 0:
                                arrived(pe, n + d // 4)
                            if m >= 8:
                                pe.wait_ge(taken, m - 7)
                            w = chunk(n + d // 4, KT, MW)
                            for k in range(KT):
                                last = nc.tensor.matmul(bank[m % 8][:, 0:T], w[:, k, P * (d % 4):P * (d % 4) + P], xnT[:, k, :], start=k == 0, stop=k == KT - 1)
                            if d % 4 == 3:
                                last.then_inc(w_used, 1)
                            if d == 0:
                                arrived(pe, n + 2)
                            w = chunk(n + 2, MT, D)
                            for k in range(MT):
                                last = nc.tensor.matmul(bank[m % 8][:, T:2 * T], w[:, k, P * d:P * d + P], ys[i][:, k, :], start=k == 0, stop=k == MT - 1)
                            last.then_inc(w_used if d == KT - 1 else pair_ready, 1)

                @block.scalar
                def _(act):
                    for i in range(3):
                        for d in range(KT):
                            m = KT * i + d
                            if d < KT - 1:
                                act.wait_ge(pair_ready, (KT - 1) * i + d + 1)
                            else:
                                act.wait_ge(w_used, MERGE + 3 * i + 3)
                            if m >= 4:
                                act.wait_ge(taken, m - 3)
                            nc.scalar.activation(sg[:, m % 4, :], bank[m % 8][:, 0:T], ACT.Sigmoid, bias=V2("b_gate_2")[:, m:m + 1]).then_inc(gate_ready, 1)

                @block.vector
                def _(dve):
                    then = step(dve, s_dve)
                    for m in range(3 * KT):
                        d = m % KT
                        dve.wait_ge(gate_ready, m + 1)
                        if m < KT:
                            nc.vector.tensor_tensor(merged[:, d, :], sg[:, m % 4, :], bank[m % 8][:, T:2 * T], ALU.mult).then_inc(taken, 1)
                        else:
                            nc.vector.tensor_tensor(tmp[:, m % 2, :], sg[:, m % 4, :], bank[m % 8][:, T:2 * T], ALU.mult).then_inc(taken, 1)
                            dve.wait_ge(taken, m + 1)
                            then(nc.vector.tensor_tensor(merged[:, d, :], merged[:, d, :], tmp[:, m % 2, :], ALU.add))

        def project_out2(l):
            with nc.Block() as block:
                @block.sync
                def _(sp):
                    for n in range(MOE2 + 4, MOE2 + RING):
                        load2(sp, l, n)

                @block.tensor
                def _(pe):
                    for n in range(OUT2, OUT2 + 2):
                        arrived(pe, n)
                        w = chunk(n, KT, MW)
                        for j in range(4):
                            for k in range(KT):
                                last = nc.tensor.matmul(bank[2 * (n - OUT2) + j // 2][:, T * (j % 2):T * (j % 2) + T], w[:, k, P * j:P * j + P], merged[:, k, :],
                                                        start=k == 0, stop=k == KT - 1)
                        last.then_inc(w_used, 1)

                @block.vector
                def _(dve):
                    for d in range(KT):
                        dve.wait_ge(w_used, OUT2 + d // 4 + 1)
                        nc.vector.scalar_tensor_tensor(hT[:, d, :], bank[d // 2][:, T * (d % 2):T * (d % 2) + T], mod[:, 16 + d:17 + d], hT[:, d, :], ALU.mult, ALU.add)

        def gated(y, g):
            def finish(then):
                nc.vector.tensor_tensor(y, y, g, ALU.mult)
            return finish

        def rwkv_finish(then):
            then(nc.vector.tensor_tensor(y_rwkv, y_rwkv, bonus, ALU.add))
            nc.vector.tensor_tensor(y_rwkv, y_rwkv, gT, ALU.mult)

        GB = ar(0, NE, T)
        silu = ar(8192, 4, T)
        hid = ar(9216, 4, T)

        def route(tag, wr, ng, bias_row):
            epg = NE // ng
            nr = ng + NE
            logits_ready, gs_ready, ge_ready, zs_ready, ze_ready, gate_ready, turned, gT_ready, wide_ready, wide_taken = (
                sem(f"{tag}_{n}") for n in ("logits", "gs", "ge", "zs", "ze", "gate", "turned", "gT", "wide", "taken"))
            s_dve = sem(f"{tag}_dve")
            at = 10240
            lg = ar(at, TT, nr)
            gs, ge, pen = (ar(at + 100 + 16 * i, TT, ng) for i in range(3))
            gtop, gsum, coef = (ar(at + 160 + 2 * i, TT, 1) for i in range(3))
            z, zs, ez, sel, gate = (ar(at + 200 + 64 * i, TT, NE) for i in range(5))
            v8 = ar(at + 560, TT, 8)
            d21 = ar(at + 580, TT, 1)
            gT = ar(at + 600, T, n=NE)
            with nc.Block() as block:
                @block.tensor
                def _(pe):
                    for t in range(TT):
                        for k in range(KT):
                            last = nc.tensor.matmul(bank[t][:, 0:nr], xnT[:, k, P * t:P * t + P], wr[:, k, :], start=k == 0, stop=k == KT - 1)
                            if k == 0 and bias_row is not None:
                                nc.tensor.matmul(bank[t][:, 0:nr], K("ones", 1), bias_row, start=False, stop=False)
                        last.then_inc(logits_ready, 1)
                    pe.wait_ge(gate_ready, TT)
                    for t in range(TT):
                        last = nc.tensor.transpose(bank[2][0:NE, P * t:P * t + P], gate[:, t, :], K("ident"))
                    last.then_inc(turned, 1)
                    pe.wait_ge(gT_ready, 1)
                    for i in range(NE // 2):
                        if i >= 4:
                            pe.wait_ge(wide_taken, i - 3)
                        for j in range(2):
                            last = nc.tensor.matmul(bank[4 + i % 4][:, T * j:T * j + T],
                                                    K("ident", NE)[:, 2 * i + j:2 * i + j + 1].broadcast_to([NE, P]), gT, start=True, stop=True)
                        last.then_inc(wide_ready, 1)

                @block.scalar
                def _(act):
                    act.wait_ge(gs_ready, 1)
                    nc.scalar.activation(ge, gs, ACT.Exp).then_inc(ge_ready, 1)
                    act.wait_ge(zs_ready, 2)
                    nc.scalar.activation(ez, zs, ACT.Exp).then_inc(ze_ready, 1)
                    nc.scalar.activation(d21, d21, ACT.Exp).then_inc(ze_ready, 1)
                    for i in range(NE // 2):
                        act.wait_ge(wide_ready, i + 1)
                        nc.scalar.copy(GB[:, 2 * i:2 * i + 2, :], bank[4 + i % 4][:, :].rearrange("p (e t) -> p e t", e=2)).then_inc(wide_taken, 1)

                @block.vector
                def _(dve):
                    then = step(dve, s_dve)
                    dve.wait_ge(logits_ready, 2)
                    for t in range(TT):
                        then(nc.vector.tensor_copy(lg[:, t, :], bank[t][:, 0:nr]))
                    g, e = lg[:, :, 0:ng], lg[:, :, ng:nr]
                    then(nc.vector.tensor_reduce(gtop, g, AX, ALU.max))
                    nc.vector.tensor_tensor(gs, g, gtop.broadcast_to([P, TT, ng]), ALU.subtract).then_inc(gs_ready, 1)
                    dve.wait_ge(gs_ready, 1)
                    then(nc.vector.tensor_scalar(pen, gs, 0.0, None, ALU.is_ge))
                    then(nc.vector.tensor_scalar(pen, pen, BIG, -BIG, ALU.mult, ALU.add))
                    then(nc.vector.tensor_tensor(z.rearrange("p t (g e) -> p t g e", g=ng), e.rearrange("p t (g e) -> p t g e", g=ng),
                                                 pen.unsqueeze(3).broadcast_to([P, TT, ng, epg]), ALU.add))
                    for t in range(TT):
                        then(nc.vector.max(v8[:, t, :], z[:, t, :]))
                    nc.vector.tensor_tensor(zs, z, v8[:, :, 0:1].broadcast_to([P, TT, NE]), ALU.subtract).then_inc(zs_ready, 1)
                    nc.vector.tensor_tensor(d21, v8[:, :, 1:2], v8[:, :, 0:1], ALU.subtract).then_inc(zs_ready, 1)
                    then(nc.vector.tensor_tensor(sel, z, v8[:, :, 1:2].broadcast_to([P, TT, NE]), ALU.is_ge))
                    dve.wait_ge(ge_ready, 1)
                    then(nc.vector.tensor_reduce(gsum, ge, AX, ALU.add))
                    dve.wait_ge(ze_ready, 2)
                    then(nc.vector.scalar_tensor_tensor(coef, d21, 1.0, gsum, ALU.add, ALU.mult))
                    then(nc.vector.reciprocal(coef, coef))
                    for t in range(TT):
                        nc.vector.scalar_tensor_tensor(gate[:, t, :], ez[:, t, :], coef[:, t, :], sel[:, t, :], ALU.mult, ALU.mult).then_inc(gate_ready, 1)
                    dve.wait_ge(turned, 1)
                    nc.vector.tensor_copy(gT, bank[2][0:NE, 0:T]).then_inc(gT_ready, 1)

        def experts(tag, feed, n0, f, slots_of, per_iter, gate_col):
            ft = f // P
            gu_ready, silu_ready, hid_made, sum_ready = (sem(f"{tag}_{n}") for n in ("gu", "silu", "hid", "sum"))
            s_dve = sem(f"{tag}_dve")
            iters = NE // per_iter
            tmp = ar(12000, 2, T)
            tiles = per_iter * ft

            def slot(n):
                return (n0 + n) % RING

            def after(n, it):
                return it * RING + (n0 + n + 1)

            with nc.Block() as block:
                @block.sync
                def _(sp):
                    with sp.Fori(1, iters) as it:
                        for n in range(RING):
                            sp.wait_ge(w_used, it * RING + (n0 + n - RING + 1))
                            sp.dma_start(ring[:, slot(n), :], feed(it, n)).then_inc(w_loaded[slot(n)], 16)

                @block.tensor
                def _(pe):
                    for b in range(4):
                        nc.tensor.matmul(bank[b][:, :], K("zeros"), cst[:, 0:512], start=True, stop=False, skip_group_check=True)
                    with pe.Fori(0, iters) as it:
                        def here(n):
                            pe.wait_ge(w_loaded[slot(n)], it * 16 + 16 * ((n0 + n) // RING + 1))

                        for q in range(per_iter):
                            gate_n, up_n, down_n, half, ends = slots_of(q)
                            here(gate_n)
                            if up_n != gate_n:
                                here(up_n)
                            gw = ring[:, slot(gate_n), 0:KT * f].rearrange("p (k w) -> p k w", k=KT)
                            o = KT * f if up_n == gate_n else 0
                            uw = ring[:, slot(up_n), o:o + KT * f].rearrange("p (k w) -> p k w", k=KT)
                            dw = ring[:, slot(down_n), half * ft * D:(half + 1) * ft * D].rearrange("p (k w) -> p k w", k=ft)
                            for j in range(ft):
                                t = ft * q + j
                                pe.wait_ge(hid_made, it * tiles + (t + 1))
                                for half_of, w in ((0, gw), (1, uw)):
                                    for k in range(KT):
                                        last = nc.tensor.matmul(bank[4 + t % 4][:, T * half_of:T * half_of + T], w[:, k, P * j:P * j + P], xnT[:, k, :],
                                                                start=k == 0, stop=k == KT - 1)
                                    if j == ft - 1 and (half_of == 1 or up_n != gate_n):
                                        last.then_inc(w_used, 1)
                                if j < ft - 1:
                                    last.then_inc(gu_ready, 1)
                            here(down_n)
                            for j in range(ft):
                                t = ft * q + j
                                pe.wait_ge(hid_made, it * tiles + (t + 5))
                                for d in range(KT):
                                    last = nc.tensor.matmul(bank[d // 2][:, T * (d % 2):T * (d % 2) + T], dw[:, j, P * d:P * d + P], hid[:, t % 4, :],
                                                            start=False, stop=False, skip_group_check=True)
                            if ends:
                                last.then_inc(w_used, 1)
                    nc.tensor.matmul(bank[3][:, :], K("zeros"), cst[:, 0:512], start=False, stop=True, skip_group_check=True).then_inc(sum_ready, 1)

                def pair_ready(eng, it, q, j):
                    if j < ft - 1:
                        eng.wait_ge(gu_ready, it * (per_iter * (ft - 1)) + ((ft - 1) * q + j + 1))
                    else:
                        eng.wait_ge(w_used, after(slots_of(q)[1], it))

                @block.scalar
                def _(act):
                    with act.Fori(0, iters) as it:
                        for q in range(per_iter):
                            for j in range(ft):
                                t = ft * q + j
                                pair_ready(act, it, q, j)
                                nc.scalar.activation(silu[:, t % 4, :], bank[4 + t % 4][:, 0:T], ACT.Silu).then_inc(silu_ready, 1)

                @block.vector
                def _(dve):
                    for b in range(4):
                        nc.vector.memset(ar(12600 + b, 1), 0.0).then_inc(hid_made, 1)
                    with dve.Fori(0, iters) as it:
                        for q in range(per_iter):
                            for j in range(ft):
                                t = ft * q + j
                                gates = GB[:, bass.ds(it * per_iter + q, 1), :].rearrange("p e t -> p (e t)")
                                dve.wait_ge(silu_ready, it * tiles + (t + 1))
                                nc.vector.tensor_tensor(tmp[:, t % 2, :], silu[:, t % 4, :], gates, ALU.mult).then_inc(s_dve, 1)
                                dve.wait_ge(s_dve, it * tiles + (t + 1))
                                nc.vector.tensor_tensor(hid[:, t % 4, :], bank[4 + t % 4][:, T:2 * T], tmp[:, t % 2, :], ALU.mult).then_inc(hid_made, 1)
                    dve.wait_ge(sum_ready, 1)
                    for d in range(KT):
                        y = bank[d // 2][:, T * (d % 2):T * (d % 2) + T]
                        if gate_col is None:
                            nc.vector.tensor_tensor(hT[:, d, :], hT[:, d, :], y, ALU.add)
                        else:
                            nc.vector.scalar_tensor_tensor(hT[:, d, :], y, gate_col[:, d:d + 1], hT[:, d, :], ALU.mult, ALU.add)

        def zero_semaphores():
            with nc.Block() as block:
                @block.sync
                def _(sp):
                    for s in layer_sems + w_loaded + [w_used]:
                        sp.sem_clear(s)

        def fetch_vectors(src, n, row_src, row_n, first_loads):
            vec_in = sem(f"vec_in{n}")
            with nc.Block() as block:
                @block.sync
                def _(sp):
                    sp.dma_start(vec[:, 0:n], src).then_inc(vec_in, 16)
                    sp.dma_start(row[:, 0:row_n], row_src).then_inc(vec_in, 16)
                    first_loads(sp)
                    sp.wait_ge(vec_in, 32)

        setup()
        with ExitStack() as stack:
            owners.append(stack)
            layer_sems.clear()
            with nc.Fori(0, L) as l:
                def loads1(sp):
                    for n in range(2):
                        load(sp, n, dram["w_in1"][l, n])
                    load(sp, 2, dram["w_in1"][l, 2])
                    load(sp, 3, dram["w_rest1"][l], KT * REST)
                    for n in range(2):
                        load(sp, 4 + n, dram["w_o1"][l, n])

                fetch_vectors(dram["vec1"][l], N1, dram["row1"][l], HEADS, loads1)
                norm("n1a", V1("attn_norm"), None, 0)
                project1(l)
                latents()
                turn_qk()
                attention()
                head_rms_out(l)
                norm("n1b", V1("ffn_norm"), None, 11000)
                route("r1", wr1, NG1, None)
                experts("e1", lambda it, n: dram["w_exp1"][l, it * RING + n], MOE1, F1,
                        lambda q: ((0, 0, 2, 0, False), (1, 1, 2, 1, True), (3, 3, 5, 0, False), (4, 4, 5, 1, True))[q], 4, None)
                zero_semaphores()
            owners.pop()
        norm("nf", VG("final_norm"), None, 0, dest=hT)
        with ExitStack() as stack:
            owners.append(stack)
            layer_sems.clear()
            with nc.Fori(0, L) as l:
                def loads2(sp):
                    for n in range(RING):
                        load2(sp, l, n)

                fetch_vectors(dram["vec2"][l], N2, dram["row2"][l], R2_N, loads2)
                modulation(l)
                norm("n2a", gains[:, 0, :], mod[:, 0:8], 0)
                project2(l)
                shift_and_convolve()
                retention()
                head_norm("nret", y_ret, ar(13824, MT, T), "ones", P, HEPS, V2("ret_gn_g_2"), gated(y_ret, sgT))
                rwkv_inputs()
                rwkv_turn()
                rwkv_solve()
                rwkv_chain()
                head_norm("nwkv", y_rwkv, ar(13824, MT, T), "blk64", HD, REPS, V2("rwkv_gn_g_2"), rwkv_finish)
                merge(l)
                project_out2(l)
                norm("n2b", gains[:, 1, :], mod[:, 24:32], 11000)
                route("r2", wr2, NG2, row[0:1, 0:R2_N])
                experts("e2", lambda it, n: dram["w_exp2"][l, it * RING + n], MOE2, F2,
                        lambda q: (3 * q, 3 * q + 1, 3 * q + 2, 0, True), 2, mod[:, 40:48])
                zero_semaphores()
            owners.pop()
        norm("nf2", VG("final_norm_g_2"), None, 0, dest=hT)
        stored = sem("out_stored")
        with nc.Block() as block:
            @block.sync
            def _(sp):
                sp.dma_start(out, hT[:]).then_inc(stored, 16)
                sp.wait_ge(stored, 16)


def columns(a):
    a = np.asarray(a)
    return np.swapaxes(a.reshape(*a.shape[:-1], -1, P), -1, -2)


def tiled(w):
    k, n = w.shape[-2:]
    w = np.moveaxis(w.reshape(*w.shape[:-2], k // P, P, n), -3, -2)
    return w.reshape(*w.shape[:-2], -1)


def in_chunks(w, width=MW):
    k, n = w.shape[-2:]
    w = w.reshape(*w.shape[:-1], n // width, width)
    return tiled(np.moveaxis(w, -2, -3))


def packed(parts, inputs, layered=True):
    return np.concatenate([columns(inputs[n].reshape(L, -1) if layered else inputs[n].reshape(-1)) for n, _ in parts], -1)


def layouts(i):
    w_in = i["w_in"]
    a = {"consts": CONST_TABLE}
    a["x"] = np.moveaxis(i["x"][0].T.reshape(KT, P, T), 0, 1)
    for n in ("positions", "positions_2"):
        a[n] = i[n][0].reshape(TT, P).T
    a["vecg"] = packed(VECG_PARTS, i, False)
    a["vec1"] = packed(VEC1_PARTS, i)
    a["row1"] = i["b_f"].reshape(L, 1, HEADS)
    a["w_in1"] = in_chunks(w_in[:, :, 0:3 * MW])
    a["w_rest1"] = tiled(w_in[:, :, 3 * MW:])
    a["w_o1"] = in_chunks(i["w_o"])
    a["small1"] = np.concatenate([tiled(i["w_uq"]), tiled(i["w_ukv"]), tiled(np.concatenate([i["w_group"], i["w_router"]], -1))], -1)
    gu = np.concatenate([tiled(i["w_gate"]), tiled(i["w_up"])], -1).reshape(L, NE // 4, 2, 2, P, SLOT)
    down = tiled(i["w_down"]).reshape(L, NE // 4, 2, 2, P, SLOT // 2)
    down = np.moveaxis(down, 3, 4).reshape(L, NE // 4, 2, 1, P, SLOT)
    a["w_exp1"] = np.concatenate([gu, down], 3).reshape(L, NE // 4 * RING, P, SLOT)
    w2 = i["w_in_2"]
    a["vec2"] = packed(VEC2_PARTS, i)
    a["row2"] = np.concatenate([i["b_router_group_2"], i["b_router_expert_2"]], -1).reshape(L, 1, R2_N)
    a["w_ada2"] = in_chunks(i["w_ada_2"])
    a["w_in2"] = in_chunks(w2[:, :, 0:7 * MW])
    a["w_low2"] = tiled(w2[:, :, 7 * MW:7 * MW + 2 * P])
    a["w_conv2"] = in_chunks(w2[:, :, 7 * MW + 2 * P:])
    gates = in_chunks(i["w_gate_2"]).reshape(L, 3, 2, P, SLOT)
    a["w_merge2"] = np.concatenate([gates, tiled(i["w_branch_2"])[:, :, None]], 2).reshape(L, 9, P, SLOT)
    a["w_o2"] = in_chunks(i["w_o_2"])
    lora = np.concatenate([i["rwkv_w_lora_2"], i["rwkv_a_lora_2"]], 1)
    a["small2"] = np.concatenate([lora, i["rwkv_g_lora_2"], tiled(np.concatenate([i["w_router_group_2"], i["w_router_expert_2"]], -1))], -1)
    a["w_exp2"] = np.stack([tiled(i[f"w_exp_{n}_2"]) for n in ("gate", "up", "down")], 2).reshape(L, 3 * NE, P, SLOT)
    return {k: np.ascontiguousarray(v) for k, v in a.items()}


def kernel(**inputs):
    import concourse.bacc as bacc
    from concourse.bass_utils import run_bass_kernel_spmd

    nc = bacc.Bacc("TRN2", target_bir_lowering=False, num_devices=1)
    arrays = layouts({k: np.asarray(v) for k, v in inputs.items()})
    dram = {n: nc.dram_tensor(f"in_{n}", a.shape, mybir.dt.from_np(a.dtype), kind="ExternalInput").ap() for n, a in arrays.items()}
    out = nc.dram_tensor("out", (P, KT, T), F32, kind="ExternalOutput").ap()
    build(nc, dram, out)
    r = run_bass_kernel_spmd(nc, [{f"in_{n}": a for n, a in arrays.items()}], core_ids=[0])
    y = np.asarray(r.results[0]["out"])
    return np.ascontiguousarray(np.moveaxis(y, 0, 1).reshape(D, T).T).reshape(1, T, D)
```

```python
from contextlib import ExitStack

import numpy as np

import concourse.bass as bass
from concourse import mybir

F32 = mybir.dt.float32
I32 = mybir.dt.int32
ALU = mybir.AluOpType
ACT = mybir.ActivationFunctionType
AX = mybir.AxisListType.X

P = 128
L = 2
T = 256
TT = T // P
D = 1024
KT = D // P
HEADS = 8
HD = 64
NOPE, ROPE = 64, 32
QKD = NOPE + ROPE
QR, KVR = 256, 128
REST = HEADS + QR + KVR + ROPE
NE = 32
NG1, NG2 = 8, 4
F1, F2 = 256, 512
MW = 512
MT = MW // P
RH = 4
CH = 32
NCH = P // CH
EPS, HEPS, REPS = 1e-6, 1e-5, 64e-5
BIG = 1e30
RING = 6
SLOT = 4096
UQ_N, UKV_N = HEADS * QKD, HEADS * 2 * HD

CONST = {}


def constants():
    p = np.arange(P)
    cols = []

    def put(name, a):
        a = np.asarray(a, np.float32).reshape(P, -1)
        at = sum(c.shape[1] for c in cols)
        CONST[name] = (at, at + a.shape[1])
        cols.append(a)

    put("ident", np.eye(P))
    put("ones", np.ones((P, P)))
    put("zeros", np.zeros((P, P)))
    put("blk64", p[:, None] // HD == p[None, :] // HD)
    key = np.concatenate([p, np.arange(T)])
    query = np.concatenate([np.tile(p[:, None], (1, P)), np.tile(p[:, None] + P, (1, T))], 1)
    put("causal", np.where(key[None, :] <= query, 0.0, -BIG))
    put("tri", np.stack([(p[:, None] + P * s <= np.arange(T)[None, :]) for s in range(TT)], 1))
    for half in (ROPE // 2, P // 2):
        freq = np.float32(10000.0) ** (-np.arange(half, dtype=np.float32) / np.float32(half))
        put(f"freq{half}", np.tile(freq.astype(np.float32)[None, :], (P, 1)))
    lg = np.log1p(-np.exp2(-5.0 - np.arange(RH, dtype=np.float32))).astype(np.float32)
    rel = (p[None, :] - p[:, None]).astype(np.float32)
    scale = np.float32(P ** -0.5)
    put("ret_in", np.stack([np.where(rel >= 0, np.exp(lg[h] * np.maximum(rel, 0)), 0) * scale for h in range(RH)], 1))
    put("ret_k", np.exp(lg[None, :] * (P - 1 - p[:, None])) * scale)
    put("ret_q", np.exp(lg[None, :] * (p[:, None] + 1.0)))
    same = p[:, None] // CH == p[None, :] // CH
    put("before", same & (p[:, None] < p[None, :]))
    put("upto", same & (p[:, None] <= p[None, :]))
    put("after", same & (p[:, None] > p[None, :]))
    put("chunk", p[:, None] // CH == np.arange(NCH)[None, :])
    put("start", np.tile((np.arange(T) % CH == 0)[None, :], (P, 1)))
    put("inner", np.tile((np.arange(T) % CH != 0)[None, :], (P, 1)))
    return np.ascontiguousarray(np.concatenate(cols, 1))


CONST_TABLE = constants()

VEC1, VEC2, VECG = {}, {}, {}
VEC1_PARTS = [("attn_norm", 8), ("q_norm", 2), ("kv_norm", 1), ("fox_out_norm", 4), ("mla_out_norm", 4), ("ffn_norm", 8)]
VEC2_PARTS = [("norm1_g_2", 8), ("norm2_g_2", 8), ("b_ada_2", 48), ("ret_gn_g_2", 4), ("rwkv_mu_2", 14), ("rwkv_w0_2", 4),
              ("rwkv_a0_2", 4), ("rwkv_k_k_2", 4), ("rwkv_k_a_2", 4), ("rwkv_r_k_2", 4), ("rwkv_gn_g_2", 4),
              ("conv_w_2", 12), ("b_gate_2", 24)]
VECG_PARTS = [("final_norm", 8), ("final_norm_g_2", 8), ("c_2", 8)]
for _table, _parts in ((VEC1, VEC1_PARTS), (VEC2, VEC2_PARTS), (VECG, VECG_PARTS)):
    _at = 0
    for _name, _n in _parts:
        _table[_name] = (_at, _at + _n)
        _at += _n
N1 = sum(n for _, n in VEC1_PARTS)
N2 = sum(n for _, n in VEC2_PARTS)
NV = sum(n for _, n in VECG_PARTS)
R1_N, R2_N = NG1 + NE, NG2 + NE
SMALL1 = 2 * UQ_N + UKV_N + KT * R1_N


def build(nc, dram, out):
    ctx = ExitStack()
    with ctx:
        def sb(name, shape, dt=F32):
            return ctx.enter_context(nc.sbuf_tensor(name, shape, dt))

        owners, layer_sems = [ctx], []

        def sem(name):
            s = owners[-1].enter_context(nc.semaphore(name))
            layer_sems.append(s)
            return s

        def step(eng, s):
            count = [0]

            def run(ins):
                count[0] += 1
                ins.then_inc(s, 1)
                eng.wait_ge(s, count[0])
            return run

        ring = sb("ring", [P, RING, SLOT])
        hT = sb("hT", [P, KT, T])
        xnT = sb("xnT", [P, KT, T])
        cst = sb("cst", [P, CONST_TABLE.shape[1]])
        vec = sb("vec", [P, max(N1, N2)])
        vecg = sb("vecg", [P, NV])
        row = sb("row", [1, 64])
        small = sb("small", [P, SMALL1])
        rope_tab = sb("rope_tab", [P, 2, TT, ROPE // 2])
        ret_tab = sb("ret_tab", [P, 2, TT, P // 2])
        arena = sb("arena", [P, 17920])
        mod = sb("mod", [P, 6 * KT])
        gains = sb("gains", [P, 2, KT])
        offs = sb("offs", [P, NE * (T // 64) + 4], I32)
        meta = sb("meta", [P, 2], I32)
        spare = sb("spare", [P, 2])
        pc = sb("pc", [P, MT, TT * NCH])
        bank = [ctx.enter_context(nc.psum_tensor(f"bank{i}", [P, 512], F32)) for i in range(8)]

        def K(name, n=P):
            a, b = CONST[name]
            return cst[0:n, a:b]

        def V1(name):
            a, b = VEC1[name]
            return vec[:, a:b]

        def V2(name):
            a, b = VEC2[name]
            return vec[:, a:b]

        def VG(name):
            a, b = VECG[name]
            return vecg[:, a:b]

        def ar(at, *shape, n=P):
            size = int(np.prod(shape))
            v = arena[0:n, at:at + size]
            if len(shape) == 2:
                v = v.rearrange("p (a b) -> p a b", a=shape[0])
            if len(shape) == 3:
                v = v.rearrange("p (a b c) -> p a b c", a=shape[0], b=shape[1])
            return v

        w_loaded = [sem(f"w_loaded{s}") for s in range(RING)]
        w_used = sem("w_used")

        def load(sp, n, src, width=SLOT):
            if n >= RING:
                sp.wait_ge(w_used, n - RING + 1)
            sp.dma_start(ring[:, n % RING, 0:width], src).then_inc(w_loaded[n % RING], 16)

        def arrived(pe, n):
            pe.wait_ge(w_loaded[n % RING], 16 * (n // RING + 1))

        def chunk(n, kt, width):
            return ring[:, n % RING, 0:kt * width].rearrange("p (k w) -> p k w", k=kt)

        def setup():
            in_loaded = sem("in_loaded")
            s_dve = sem("setup_dve")
            angles = sem("angles_ready")
            pos_i = arena[:, 0:2 * TT].bitcast(I32)
            pos_f = ar(8, 2 * TT)
            turns = ar(16, 2, TT, 80)
            turns_i = arena[:, 400:400 + 320].bitcast(I32)
            ang = ar(800, 2, TT, 80)
            ang2 = ar(1200, 2, TT, 80)
            neg = ar(1600, 2, TT, 80)
            half = (ROPE // 2, P // 2)
            with nc.Block() as block:
                @block.sync
                def _(sp):
                    sp.dma_start(cst[:], dram["consts"]).then_inc(in_loaded, 16)
                    sp.dma_start(hT[:], dram["x"]).then_inc(in_loaded, 16)
                    sp.dma_start(vecg[:], dram["vecg"]).then_inc(in_loaded, 16)
                    sp.dma_start(pos_i[:, 0:TT], dram["positions"]).then_inc(in_loaded, 16)
                    sp.dma_start(pos_i[:, TT:2 * TT], dram["positions_2"]).then_inc(in_loaded, 16)

                @block.vector
                def _(dve):
                    then = step(dve, s_dve)
                    dve.wait_ge(in_loaded, 80)
                    then(nc.vector.tensor_copy(pos_f, pos_i))
                    for a in (ang, ang2):
                        then(nc.vector.memset(a, 0.0))
                    for w in range(2):
                        for t in range(TT):
                            then(nc.vector.tensor_scalar(ang[:, w, t, 0:half[w]], K(f"freq{half[w]}"),
                                                         pos_f[:, TT * w + t:TT * w + t + 1], None, ALU.mult))
                    flat, flat2 = ang.rearrange("p a b c -> p (a b c)"), ang2.rearrange("p a b c -> p (a b c)")
                    tf, nf = turns.rearrange("p a b c -> p (a b c)"), neg.rearrange("p a b c -> p (a b c)")
                    then(nc.vector.tensor_scalar(tf, flat, 1.0 / (2 * np.pi), None, ALU.mult))
                    then(nc.vector.tensor_copy(turns_i, tf))
                    then(nc.vector.tensor_copy(tf, turns_i))
                    c1 = 6.28125
                    c2 = float(np.float32(2 * np.pi - c1).view(np.uint32) & 0xFFFFF000)
                    c2 = float(np.uint32(int(c2)).view(np.float32))
                    c3 = float(2 * np.pi - c1 - c2)
                    for c in (c1, c2, c3):
                        then(nc.vector.scalar_tensor_tensor(flat, tf, -c, flat, ALU.mult, ALU.add))
                    for sign in (1.0, -1.0):
                        then(nc.vector.tensor_scalar(nf, flat, sign, float(np.pi), ALU.mult, ALU.is_gt))
                        then(nc.vector.scalar_tensor_tensor(flat, nf, -sign * 2 * float(np.pi), flat, ALU.mult, ALU.add))
                    then(nc.vector.tensor_scalar(flat, flat, float(np.float32(np.pi)) * (1 - 1e-7), -float(np.float32(np.pi)) * (1 - 1e-7), ALU.min, ALU.max))
                    then(nc.vector.scalar_tensor_tensor(flat2, flat, -1.0, flat, ALU.mult, ALU.max))
                    nc.vector.tensor_scalar(flat2, flat2, -1.0, float(np.pi / 2), ALU.mult, ALU.add).then_inc(angles, 1)

                @block.scalar
                def _(act):
                    act.wait_ge(angles, 1)
                    for w, tab in enumerate((rope_tab, ret_tab)):
                        nc.scalar.activation(tab[:, 0], ang2[:, w, :, 0:half[w]], ACT.Sin)
                        nc.scalar.activation(tab[:, 1], ang[:, w, :, 0:half[w]], ACT.Sin)

        def norm(tag, gain, shift, at, fetch=None, ada=None, dest=None):
            dest = xnT if dest is None else dest
            sq = ar(at, KT, T)
            rstd = ar(at + KT * T, T)
            sums = bank[3]
            sq_ready, sum_ready, ms_ready, root_ready, rstd_ready, scaled = (
                sem(f"{tag}_{n}") for n in ("sq", "sum", "ms", "root", "rstd", "scaled"))
            vec_in = sem(f"{tag}_vec_in") if fetch else None
            sems = ada_sems("ada") if ada else None
            with nc.Block() as block:
                @block.sync
                def _(sp):
                    if fetch:
                        fetch(sp, vec_in)

                @block.scalar
                def _(act):
                    for q in range(4):
                        nc.scalar.activation(sq[:, 2 * q:2 * q + 2, :], hT[:, 2 * q:2 * q + 2, :], ACT.Square).then_inc(sq_ready, 1)
                    act.wait_ge(ms_ready, 1)
                    nc.scalar.activation(rstd, rstd, ACT.Sqrt).then_inc(root_ready, 1)
                    if ada:
                        ada_rows(act, sems, *ada)
                    if shift is not None:
                        for k in range(KT):
                            act.wait_ge(scaled, k + 1)
                            nc.scalar.activation(dest[:, k, :], sq[:, k, :], ACT.Identity, bias=shift[:, k:k + 1])

                @block.tensor
                def _(pe):
                    for k in range(KT):
                        pe.wait_ge(sq_ready, k // 2 + 1)
                        last = nc.tensor.matmul(sums[:, 0:T], K("ones"), sq[:, k, :], start=k == 0, stop=k == KT - 1)
                    last.then_inc(sum_ready, 1)
                    if ada:
                        ada_products(pe, sems, *ada)

                @block.vector
                def _(dve):
                    if ada:
                        nc.vector.memset(c_wide, 0.0).then_inc(sems[0], 1)
                    dve.wait_ge(sum_ready, 1)
                    nc.vector.tensor_scalar(rstd, sums[:, 0:T], 1.0 / D, EPS, ALU.mult, ALU.add).then_inc(ms_ready, 1)
                    dve.wait_ge(root_ready, 1)
                    nc.vector.reciprocal(rstd, rstd).then_inc(rstd_ready, 1)
                    if fetch:
                        dve.wait_ge(vec_in, 32)
                    if ada:
                        first, count = ada
                        ada_columns(dve, sems, 0, count, 0, "norm1_g_2")
                    dve.wait_ge(rstd_ready, 1)
                    for k in range(KT):
                        o = dest if shift is None else sq
                        nc.vector.scalar_tensor_tensor(o[:, k, :], hT[:, k, :], gain[:, k:k + 1], rstd, ALU.mult,
                                                       ALU.mult).then_inc(scaled, 1)

        fqT, fkT = ar(0, 4, T), ar(1024, 4, T)
        fv = ar(2048, TT, MW)
        rest = ar(3072, TT, REST)
        latn = ar(3920, TT, QR + KVR)
        cqT, ckvT = ar(4688, 2, T), ar(5200, T)
        qS = ar(5456, TT, HEADS * QKD).rearrange("p t (h d) -> p t h d", d=QKD)
        kS = ar(6992, TT, HEADS * QKD).rearrange("p t (h d) -> p t h d", d=QKD)
        vS = ar(8528, TT, MW)
        qmT, kmT = ar(9552, HEADS, T, n=QKD), ar(11600, HEADS, T, n=QKD)
        mixT = ar(13648, KT, T)
        lf = ar(15696, TT, HEADS)
        uq = small[:, 0:2 * UQ_N].rearrange("p (k n) -> p k n", k=2)
        ukv = small[:, 2 * UQ_N:2 * UQ_N + UKV_N]
        wr1 = small[:, 2 * UQ_N + UKV_N:SMALL1].rearrange("p (k n) -> p k n", k=KT)
        MOE1 = 6

        def moe1_chunk(l, n):
            return dram["w_exp1"][l, n - MOE1]

        def project1(l):
            small_in = sem("small1_in")
            with nc.Block() as block:
                @block.sync
                def _(sp):
                    sp.dma_start(small[:], dram["small1"][l]).then_inc(small_in, 16)
                    for n in range(MOE1, MOE1 + 4):
                        load(sp, n, moe1_chunk(l, n))
                    sp.wait_ge(small_in, 16)

                @block.tensor
                def _(pe):
                    for n in range(2):
                        arrived(pe, n)
                        w = chunk(n, KT, MW)
                        for j in range(4):
                            for k in range(KT):
                                last = nc.tensor.matmul(bank[2 * n + j // 2][:, T * (j % 2):T * (j % 2) + T], w[:, k, P * j:P * j + P],
                                                        xnT[:, k, :], start=k == 0, stop=k == KT - 1)
                        last.then_inc(w_used, 1)
                    for n, width in ((2, MW), (3, REST)):
                        arrived(pe, n)
                        w = chunk(n, KT, width)
                        for t in range(TT):
                            o = bank[2 * n + t]
                            for k in range(KT):
                                last = nc.tensor.matmul(o[:, 0:width], xnT[:, k, P * t:P * t + P], w[:, k, :],
                                                        start=k == 0, stop=k == KT - 1)
                                if k == 0 and n == 3:
                                    nc.tensor.matmul(o[:, 0:HEADS], K("ones", 1), row[0:1, 0:HEADS], start=False, stop=False)
                        last.then_inc(w_used, 1)

                dests = [fqT[:, 0:2], fqT[:, 2:4], fkT[:, 0:2], fkT[:, 2:4], fv[:, 0], fv[:, 1], rest[:, 0], rest[:, 1]]

                @block.scalar
                def _(act):
                    for b in (0, 2, 4, 6):
                        act.wait_ge(w_used, b // 2 + 1)
                        nc.scalar.copy(dests[b], bank[b][:, 0:REST if b == 6 else 512])

                @block.vector
                def _(dve):
                    for b in (1, 3, 5, 7):
                        dve.wait_ge(w_used, b // 2 + 1)
                        nc.vector.tensor_copy(dests[b], bank[b][:, 0:REST if b == 7 else 512])

        def rotate(then, x1, x2, cos, sin, tmp):
            for o, a, b in ((tmp[0], x1, cos), (tmp[1], x2, sin), (tmp[2], x2, cos)):
                nc.vector.tensor_tensor(o, a, b, ALU.mult)
            then(nc.vector.tensor_tensor(tmp[3], x1, sin, ALU.mult))
            nc.vector.tensor_tensor(x1, tmp[0], tmp[1], ALU.subtract)
            then(nc.vector.tensor_tensor(x2, tmp[2], tmp[3], ALU.add))

        def latents():
            sq_ready, ms_ready, root_ready, lat_ready, turned, lat_T, q_ready, kv_ready, kv_ready2, q_in_sbuf, forget_e, forget_l = (
                sem(f"lat_{n}") for n in ("sq", "ms", "root", "lat", "turned", "T", "q", "kv", "kv2", "qsb", "fe", "fl"))
            s_dve = sem("lat_dve")
            junk = ar(9552, QR)
            ss = ar(15712, 4)
            e = ar(15720, TT, HEADS)
            kr = rest[:, :, REST - ROPE:REST]
            kr1, kr2 = kr[:, :, 0:ROPE // 2], kr[:, :, ROPE // 2:ROPE]
            tmp = [ar(9900 + 256 * i, TT, HEADS * ROPE // 2).rearrange("p t (h d) -> p t h d", h=HEADS) for i in range(4)]
            tmpk = [ar(9900 + 32 * i, TT, ROPE // 2) for i in range(4)]
            fl = rest[:, :, 0:HEADS]
            with nc.Block() as block:
                @block.scalar
                def _(act):
                    for i in range(4):
                        t, lo, n = i % 2, (HEADS, HEADS + QR)[i // 2], (QR, KVR)[i // 2]
                        nc.scalar.activation(junk[:, 0:n], rest[:, t, lo:lo + n], ACT.Square, accum_out=ss[:, i:i + 1]).then_inc(sq_ready, 1)
                        act.wait_ge(sq_ready, i + 1)
                    act.wait_ge(ms_ready, 1)
                    nc.scalar.activation(ss, ss, ACT.Sqrt).then_inc(root_ready, 1)
                    act.wait_ge(forget_e, 1)
                    nc.scalar.activation(e, e, ACT.Exp, scale=-1.0).then_inc(forget_l, 1)
                    act.wait_ge(forget_l, 1)
                    nc.scalar.activation(e, e, ACT.Ln, bias=1.0).then_inc(forget_l, 1)
                    for t in range(TT):
                        act.wait_ge(q_ready, t + 1)
                        for g in range(2):
                            nc.scalar.copy(qS[:, t, 4 * g:4 * g + 4, :], bank[2 + 2 * t + g][:, 0:4 * QKD]).then_inc(q_in_sbuf, 1)
                    for t in range(TT):
                        act.wait_ge((kv_ready, kv_ready2)[t], 1)
                        for g in range(2):
                            kv = bank[(6, 0)[t] + g][:, :].rearrange("p (h d) -> p h d", h=4)
                            nc.scalar.copy(kS[:, t, 4 * g:4 * g + 4, 0:NOPE], kv[:, :, 0:NOPE])
                            nc.scalar.copy(vS[:, t, 256 * g:256 * g + 256].rearrange("p (h d) -> p h d", h=4), kv[:, :, NOPE:NOPE + HD])

                @block.vector
                def _(dve):
                    then = step(dve, s_dve)
                    dve.wait_ge(sq_ready, 4)
                    nc.vector.tensor_scalar(ss[:, 0:2], ss[:, 0:2], 1.0 / QR, EPS, ALU.mult, ALU.add)
                    nc.vector.tensor_scalar(ss[:, 2:4], ss[:, 2:4], 1.0 / KVR, EPS, ALU.mult, ALU.add).then_inc(ms_ready, 1)
                    dve.wait_ge(root_ready, 1)
                    then(nc.vector.reciprocal(ss, ss))
                    for i in range(4):
                        t, lo, n = i % 2, (HEADS, HEADS + QR)[i // 2], (QR, KVR)[i // 2]
                        nc.vector.tensor_scalar(latn[:, t, lo - HEADS:lo - HEADS + n], rest[:, t, lo:lo + n], ss[:, i:i + 1], None,
                                                ALU.mult).then_inc(lat_ready, 1)
                    nc.vector.scalar_tensor_tensor(e, fl, -1.0, fl, ALU.mult, ALU.max).then_inc(forget_e, 1)
                    rotate(then, kr1, kr2, rope_tab[:, 0], rope_tab[:, 1], tmpk)
                    nc.vector.tensor_copy(kS[:, :, :, NOPE:QKD], kr.unsqueeze(2).broadcast_to([P, TT, HEADS, ROPE]))
                    dve.wait_ge(turned, 1)
                    for j in range(2):
                        nc.vector.tensor_scalar(cqT[:, j, :], bank[0][:, T * j:T * j + T], V1("q_norm")[:, j:j + 1], None, ALU.mult).then_inc(lat_T, 1)
                    nc.vector.tensor_scalar(ckvT, bank[1][:, 0:T], V1("kv_norm"), None, ALU.mult).then_inc(lat_T, 1)
                    dve.wait_ge(forget_l, 2)
                    nc.vector.scalar_tensor_tensor(lf, fl, 0.0, e, ALU.min, ALU.subtract)
                    dve.wait_ge(q_in_sbuf, 4)
                    cos, sin = (rope_tab[:, i].unsqueeze(2).broadcast_to([P, TT, HEADS, ROPE // 2]) for i in range(2))
                    rotate(then, qS[:, :, :, NOPE:NOPE + ROPE // 2], qS[:, :, :, NOPE + ROPE // 2:QKD], cos, sin, tmp)

                @block.tensor
                def _(pe):
                    pe.wait_ge(lat_ready, 4)
                    for j in range(3):
                        for t in range(TT):
                            last = nc.tensor.transpose(bank[j // 2][:, T * (j % 2) + P * t:T * (j % 2) + P * t + P],
                                                       latn[:, t, P * j:P * j + P], K("ident"))
                    last.then_inc(turned, 1)
                    pe.wait_ge(lat_T, 3)
                    for t in range(TT):
                        for g in range(2):
                            for k in range(2):
                                last = nc.tensor.matmul(bank[2 + 2 * t + g][:, 0:4 * QKD], cqT[:, k, P * t:P * t + P],
                                                        uq[:, k, 4 * QKD * g:4 * QKD * g + 4 * QKD], start=k == 0, stop=k == 1)
                        last.then_inc(q_ready, 1)
                    for t in range(TT):
                        for g in range(2):
                            last = nc.tensor.matmul(bank[(6, 0)[t] + g][:, :], ckvT[:, P * t:P * t + P], ukv[:, 512 * g:512 * g + 512],
                                                    start=True, stop=True)
                        last.then_inc((kv_ready, kv_ready2)[t], 1)

        def turn_qk():
            turned = sem("qk_turned")
            with nc.Block() as block:
                @block.tensor
                def _(pe):
                    for b in range(8):
                        src = (qS, kS)[b // 4]
                        for i in range(2):
                            for t in range(TT):
                                last = nc.tensor.transpose(bank[b][0:QKD, T * i + P * t:T * i + P * t + P], src[:, t, 2 * (b % 4) + i, :], K("ident"))
                        last.then_inc(turned, 1)

                def to_sbuf(eng, copy, banks):
                    for b in banks:
                        eng.wait_ge(turned, b + 1)
                        copy((qmT, kmT)[b // 4][:, 2 * (b % 4):2 * (b % 4) + 2, :], bank[b][0:QKD, :].rearrange("p (h t) -> p h t", h=2))

                @block.scalar
                def _(act):
                    to_sbuf(act, nc.scalar.copy, (0, 2, 4, 6))

                @block.vector
                def _(dve):
                    to_sbuf(dve, nc.vector.tensor_copy, (1, 3, 5, 7))

        def attention():
            NH = 2 * HEADS
            COLS = P + T
            z_free, decay_ready, scores_ready, z_ready, top_ready, e_ready, r_ready, p_ready, p_turned, pT_ready, out_ready, out_taken = (
                sem(f"att_{n}") for n in ("zfree", "decay", "scores", "z", "top", "e", "r", "p", "turned", "pT", "out", "taken"))
            s_dve = sem("att_dve")
            Z = [ar(3920 + 512 * i, TT, T) for i in range(2)]
            zb = [ar(5456 + 384 * i, COLS) for i in range(2)]
            pT = [ar(6224 + 384 * i, COLS) for i in range(2)]
            top = [ar(15712 + 2 * i, 2) for i in range(2)]
            tot = [ar(15716 + 2 * i, 2) for i in range(2)]
            rec = [ar(15720 + 2 * i, 2) for i in range(2)]
            parts = ((0, P), (P, COLS))
            scale = (HD ** -0.5, QKD ** -0.5)

            def q_of(h):
                return fqT[HD * (h % 2):HD * (h % 2) + HD, h // 2, :] if h < HEADS else qmT[:, h - HEADS, :]

            def k_of(h):
                return fkT[HD * (h % 2):HD * (h % 2) + HD, h // 2, :] if h < HEADS else kmT[:, h - HEADS, :]

            def v_of(h, t):
                return (fv if h < HEADS else vS)[:, t, HD * (h % HEADS):HD * (h % HEADS) + HD]

            with nc.Block() as block:
                @block.tensor
                def _(pe):
                    def scores(h):
                        o = bank[h % 2]
                        if h >= 2:
                            pe.wait_ge(z_ready, h - 1)
                        fox = h < HEADS
                        if fox:
                            pe.wait_ge(decay_ready, h + 1)
                        for t, (a, b) in enumerate(parts):
                            last = nc.tensor.matmul(o[:, a:b], q_of(h)[:, P * t:P * t + P], k_of(h)[:, 0:b - a], start=True, stop=not fox)
                            if fox:
                                last = nc.tensor.matmul(o[:, a:b], K("ones"), Z[h % 2][:, 0, 0:b - a], start=False, stop=t == 0)
                                if t == 1:
                                    last = nc.tensor.matmul(o[:, a + P:b], K("ones"), Z[h % 2][:, 1, P:T], start=False, stop=True)
                        last.then_inc(scores_ready, 1)

                    def turn(h):
                        pe.wait_ge(p_ready, 2 * h + 2)
                        if h >= 2:
                            pe.wait_ge(pT_ready, h - 1)
                        for i in range(3):
                            last = nc.tensor.transpose(bank[2 + h % 2][:, P * i:P * i + P], zb[h % 2][:, P * i:P * i + P], K("ident"))
                        last.then_inc(p_turned, 1)

                    def product(h):
                        pe.wait_ge(pT_ready, h + 1)
                        if h % 2 == 0 and h >= 4:
                            pe.wait_ge(out_taken, h // 2 - 1)
                        o = bank[4 + h // 2 % 2][HD * (h % 2):HD * (h % 2) + HD, :]
                        nc.tensor.matmul(o[:, 0:T], v_of(h, 0), pT[h % 2][:, 0:T], start=True, stop=False)
                        nc.tensor.matmul(o[:, P:T], v_of(h, 1), pT[h % 2][:, T:COLS], start=False, stop=True).then_inc(out_ready, 1)

                    for i in range(NH + 2):
                        if i < NH:
                            scores(i)
                        if 1 <= i <= NH:
                            turn(i - 1)
                        if i >= 2:
                            product(i - 2)

                @block.vector
                def _(dve):
                    then = step(dve, s_dve)

                    def decays(h):
                        if h >= 2:
                            dve.wait_ge(scores_ready, h - 1)
                        for s in range(TT):
                            last = nc.vector.tensor_scalar(Z[h % 2][:, s, :], K("tri")[:, T * s:T * s + T], lf[:, s, h:h + 1], -1.0 / scale[0],
                                                           ALU.mult, ALU.mult)
                        last.then_inc(decay_ready, 1)

                    def softmax(h):
                        z = zb[h % 2]
                        dve.wait_ge(scores_ready, h + 1)
                        if h >= 2:
                            dve.wait_ge(p_turned, h - 1)
                        nc.vector.scalar_tensor_tensor(z, bank[h % 2][:, 0:COLS], scale[h // HEADS], K("causal"), ALU.mult, ALU.add).then_inc(z_ready, 1)
                        dve.wait_ge(z_ready, h + 1)
                        for t, (a, b) in enumerate(parts):
                            last = nc.vector.tensor_reduce(top[h % 2][:, t:t + 1], z[:, a:b], AX, ALU.max, negate=True)
                        last.then_inc(top_ready, 1)

                    def finish(h):
                        dve.wait_ge(e_ready, 2 * h + 2)
                        nc.vector.reciprocal(rec[h % 2], tot[h % 2]).then_inc(r_ready, 1)
                        dve.wait_ge(r_ready, h + 1)
                        for t, (a, b) in enumerate(parts):
                            nc.vector.tensor_scalar(zb[h % 2][:, a:b], zb[h % 2][:, a:b], rec[h % 2][:, t:t + 1], None, ALU.mult).then_inc(p_ready, 1)

                    def take(j):
                        dve.wait_ge(out_ready, 2 * j + 2)
                        nc.vector.tensor_copy(mixT[:, j, :], bank[4 + j % 2][:, 0:T]).then_inc(out_taken, 1)

                    decays(0)
                    for i in range(NH + 3):
                        if i + 1 < HEADS:
                            decays(i + 1)
                        if i < NH:
                            softmax(i)
                            finish(i)
                        if i >= 3 and (i - 3) % 2 == 1:
                            take((i - 3) // 2)

                @block.scalar
                def _(act):
                    def exps(h):
                        act.wait_ge(top_ready, h + 1)
                        for t, (a, b) in enumerate(parts):
                            nc.scalar.activation(zb[h % 2][:, a:b], zb[h % 2][:, a:b], ACT.Exp, bias=top[h % 2][:, t:t + 1],
                                                 accum_out=tot[h % 2][:, t:t + 1]).then_inc(e_ready, 1)

                    def to_sbuf(h):
                        act.wait_ge(p_turned, h + 1)
                        if h >= 2:
                            act.wait_ge(out_ready, h - 1)
                        nc.scalar.copy(pT[h % 2], bank[2 + h % 2][:, 0:COLS]).then_inc(pT_ready, 1)

                    for i in range(NH + 1):
                        if i < NH:
                            exps(i)
                        if i >= 1:
                            to_sbuf(i - 1)

        def head_rms_out(l):
            sq_ready, sums_ready, ms_ready, root_ready, rstd_ready, mix_ready = (
                sem(f"mix_{n}") for n in ("sq", "sums", "ms", "root", "rstd", "ready"))
            sq = ar(5456, KT, T)
            gain = vec[:, VEC1["fox_out_norm"][0]:VEC1["mla_out_norm"][1]]
            with nc.Block() as block:
                @block.sync
                def _(sp):
                    for n in range(MOE1 + 4, MOE1 + 6):
                        load(sp, n, moe1_chunk(l, n))

                @block.scalar
                def _(act):
                    for b in range(4):
                        nc.scalar.activation(sq[:, 2 * b:2 * b + 2, :], mixT[:, 2 * b:2 * b + 2, :], ACT.Square).then_inc(sq_ready, 1)
                    for b in range(4):
                        act.wait_ge(ms_ready, b + 1)
                        nc.scalar.activation(sq[:, 2 * b:2 * b + 2, :], sq[:, 2 * b:2 * b + 2, :], ACT.Sqrt).then_inc(root_ready, 1)

                @block.tensor
                def _(pe):
                    for b in range(4):
                        pe.wait_ge(sq_ready, b + 1)
                        nc.tensor.matmul(bank[b][:, :], K("blk64"), sq[:, 2 * b:2 * b + 2, :], start=True, stop=True).then_inc(sums_ready, 1)
                    pe.wait_ge(mix_ready, KT)
                    for n in range(4, 6):
                        arrived(pe, n)
                        w = chunk(n, KT, MW)
                        for j in range(4):
                            b = 4 + 2 * (n - 4) + j // 2
                            for k in range(KT):
                                last = nc.tensor.matmul(bank[b][:, T * (j % 2):T * (j % 2) + T], w[:, k, P * j:P * j + P], mixT[:, k, :],
                                                        start=k == 0, stop=k == KT - 1)
                        last.then_inc(w_used, 1)

                @block.vector
                def _(dve):
                    for b in range(4):
                        dve.wait_ge(sums_ready, b + 1)
                        nc.vector.tensor_scalar(sq[:, 2 * b:2 * b + 2, :], bank[b][:, :], 1.0 / HD, EPS, ALU.mult, ALU.add).then_inc(ms_ready, 1)
                    for b in range(4):
                        dve.wait_ge(root_ready, b + 1)
                        nc.vector.reciprocal(sq[:, 2 * b:2 * b + 2, :], sq[:, 2 * b:2 * b + 2, :]).then_inc(rstd_ready, 1)
                    for j in range(KT):
                        dve.wait_ge(rstd_ready, j // 2 + 1)
                        nc.vector.scalar_tensor_tensor(mixT[:, j, :], mixT[:, j, :], gain[:, j:j + 1], sq[:, j, :], ALU.mult,
                                                       ALU.mult).then_inc(mix_ready, 1)
                    for n in range(4, 6):
                        dve.wait_ge(w_used, n + 1)
                        for i in range(2):
                            j = 4 * (n - 4) + 2 * i
                            nc.vector.tensor_tensor(hT[:, j:j + 2, :], hT[:, j:j + 2, :], bank[4 + 2 * (n - 4) + i][:, :], ALU.add)

        qt, kt_, vt = (ar(1024 * i, TT, MW) for i in range(3))
        sgT = ar(3072, MT, T)
        mixed = ar(4096, 14, T)
        rT, kT, vT = (ar(4096 + 1024 * i, MT, T) for i in range(3))
        lowT = ar(7168, 2, T)
        convT = [ar(7680 + 1024 * i, MT, T) for i in range(3)]
        y_ret, y_rwkv, y_conv = (ar(10752 + 1024 * i, MT, T) for i in range(3))
        lora_wa, lora_g = small[:, 0:MW], small[:, MW:2 * MW]
        wr2 = small[:, 2 * MW:2 * MW + KT * R2_N].rearrange("p (k n) -> p k n", k=KT)
        ADA, CONV, RWKV, LORA, RET, ADA_REST, MERGE, OUT2, MOE2 = 0, 4, 7, 10, 11, 15, 23, 32, 34

        def load2(sp, l, n):
            if n < CONV:
                load(sp, n, dram["w_ada2"][l, n])
            elif n < RWKV:
                load(sp, n, dram["w_conv2"][l, n - CONV])
            elif n < LORA:
                load(sp, n, dram["w_in2"][l, n - RWKV + 4])
            elif n == LORA:
                load(sp, n, dram["w_low2"][l], KT * 2 * P)
            elif n < ADA_REST:
                load(sp, n, dram["w_in2"][l, n - RET])
            elif n < MERGE:
                load(sp, n, dram["w_ada2"][l, n - ADA_REST + CONV])
            elif n < OUT2:
                load(sp, n, dram["w_merge2"][l, n - MERGE])
            elif n < MOE2:
                load(sp, n, dram["w_o2"][l, n - OUT2])
            else:
                load(sp, n, dram["w_exp2"][l, n - MOE2])

        BAND = P // 4
        c_wide = y_rwkv.rearrange("p j t -> p (j t)")[:, 0:KT * BAND].rearrange("p (k b) -> p k b", k=KT)
        c_rows = y_ret.rearrange("p (i j) t -> p i (j t)", i=2)

        def ada_sems(tag):
            return [sem(f"{tag}_{n}") for n in ("zero", "c", "taken", "turned", "mod")]

        def ada_products(pe, sems, first, count, b=0):
            cleared, c_ready, row_taken, row_turned, mod_ready = sems

            def turn(i):
                pe.wait_ge(row_taken, i + 1)
                for j in range(4):
                    last = nc.tensor.matmul(bank[b][:, 4 * i + j:4 * i + j + 1], c_rows[:, i % 2, P * j:P * j + P], K("ones")[:, 0:1], start=True, stop=True)
                last.then_inc(row_turned, 1)

            pe.wait_ge(c_ready, 1)
            for i in range(count):
                arrived(pe, first + i)
                w = chunk(first + i, KT, MW)
                for k in range(KT):
                    band = slice(BAND * (k % 4), BAND * (k % 4) + BAND)
                    last = nc.tensor.matmul(bank[b + 1 + i % 2][band, :], c_wide[:, k, :], w[:, k, :], start=k < 4, stop=k >= 4)
                last.then_inc(w_used, 1)
                if i:
                    turn(i - 1)
            turn(count - 1)

        def ada_rows(act, sems, first, count, b=0):
            cleared, c_ready, row_taken, row_turned, mod_ready = sems
            act.wait_ge(cleared, 1)
            nc.scalar.activation(c_wide[:, :, 0], VG("c_2"), ACT.Silu).then_inc(c_ready, 1)
            for i in range(count):
                act.wait_ge(w_used, first + i + 1)
                if i >= 2:
                    act.wait_ge(row_turned, i - 1)
                nc.scalar.copy(c_rows[:, i % 2, :], bank[b + 1 + i % 2][:, :]).then_inc(row_taken, 1)

        def ada_columns(dve, sems, at, count, i, g, b=0):
            cleared, c_ready, row_taken, row_turned, mod_ready = sems
            dve.wait_ge(row_turned, count)
            cols = slice(at, at + 4 * count)
            nc.vector.tensor_tensor(mod[:, cols], bank[b][:, 0:4 * count], V2("b_ada_2")[:, cols], ALU.add).then_inc(mod_ready, 1)
            dve.wait_ge(mod_ready, 1)
            nc.vector.scalar_tensor_tensor(gains[:, i, :], mod[:, 24 * i + 8:24 * i + 16], 1.0, V2(g), ALU.add, ALU.mult).then_inc(mod_ready, 1)
            dve.wait_ge(mod_ready, 2)

        def project2(l):
            s_dve = sem("p2_dve")
            before = ar(13824, 14, T)
            mu, cw = V2("rwkv_mu_2"), V2("conv_w_2")
            taken = [sem("p2_act_taken"), sem("p2_dve_taken")]
            loads = []
            for n in range(3):
                loads += [(CONV + n, convT[n][:, 2 * i:2 * i + 2, :], MW) for i in range(2)]
            for n, d in enumerate((rT, kT, vT)):
                loads += [(RWKV + n, d[:, 2 * i:2 * i + 2, :], MW) for i in range(2)]
            loads += [(LORA, lowT, MW)]
            for n in range(3):
                loads += [(RET + n, (qt, kt_, vt)[n][:, t, :], MW) for t in range(TT)]
            loads += [(RET + 3, sgT[:, 2 * i:2 * i + 2, :], MW) for i in range(2)]
            at_conv, at_rkv, at_low = 6, 12, 13
            with nc.Block() as block:
                @block.sync
                def _(sp):
                    for n in range(CONV + RING, ADA_REST + RING):
                        load2(sp, l, n)

                @block.tensor
                def _(pe):
                    for i, (n, d, width) in enumerate(loads):
                        o = bank[i % 8]
                        first = i == 0 or loads[i - 1][0] != n
                        if first:
                            arrived(pe, n)
                        if i >= 8:
                            pe.wait_ge(taken[i % 2], (i - 8) // 2 + 1)
                        if RET <= n < RET + 3:
                            w = chunk(n, KT, MW)
                            for k in range(KT):
                                last = nc.tensor.matmul(o[:, 0:MW], xnT[:, k, P * (not first):P * (not first) + P], w[:, k, :], start=k == 0, stop=k == KT - 1)
                        else:
                            w = chunk(n, KT, 2 * P if n == LORA else MW)
                            for j in range(2):
                                for k in range(KT):
                                    col = P * (j + 2 * (not first))
                                    last = nc.tensor.matmul(o[:, T * j:T * j + T], w[:, k, col:col + P], xnT[:, k, :], start=k == 0, stop=k == KT - 1)
                        if i + 1 == len(loads) or loads[i + 1][0] != n:
                            last.then_inc(w_used, 1)

                def take(eng, copy, i):
                    eng.wait_ge(w_used, loads[i][0] + 1)
                    copy(loads[i][1], bank[i % 8][:, 0:loads[i][2]]).then_inc(taken[i % 2], 1)

                @block.scalar
                def _(act):
                    for i in range(0, len(loads), 2):
                        take(act, nc.scalar.copy, i)

                @block.vector
                def _(dve):
                    then = step(dve, s_dve)

                    def taken_up_to(n):
                        dve.wait_ge(taken[0], (n + 1) // 2)
                        dve.wait_ge(taken[1], n // 2)

                    def convolve():
                        h, b, c = convT
                        taken_up_to(at_conv)
                        then(nc.vector.tensor_tensor(c, c, h, ALU.mult))
                        for j in range(MT):
                            last = nc.vector.tensor_scalar(y_conv[:, j, :], c[:, j, :], cw[:, 2 * MT + j:2 * MT + j + 1], None, ALU.mult)
                        then(last)
                        for d in (1, 2):
                            for j in range(MT):
                                col = (2 - d) * MT + j
                                last = nc.vector.scalar_tensor_tensor(y_conv[:, j, d:T], c[:, j, 0:T - d], cw[:, col:col + 1], y_conv[:, j, d:T], ALU.mult, ALU.add)
                            then(last)
                        nc.vector.tensor_tensor(y_conv, y_conv, b, ALU.mult)

                    def shift(a, b, n):
                        taken_up_to(n)
                        nc.vector.tensor_tensor(before[:, a:b, 1:T], mixed[:, a:b, 0:T - 1], mixed[:, a:b, 1:T], ALU.subtract)
                        then(nc.vector.tensor_scalar(before[:, a:b, 0:1], mixed[:, a:b, 0:1], -1.0, None, ALU.mult))
                        for j in range(a, b):
                            nc.vector.scalar_tensor_tensor(mixed[:, j, :], before[:, j, :], mu[:, j:j + 1], mixed[:, j, :], ALU.mult, ALU.add)

                    for i in range(1, len(loads), 2):
                        take(dve, nc.vector.tensor_copy, i)
                        if i == at_conv + 1:
                            convolve()
                        if i == at_rkv + 1:
                            shift(0, 12, at_rkv)
                        if i == at_low + 2:
                            shift(12, 14, at_low)

        def retention(l):
            sems = ada_sems("ada_rest")
            mod_ready = sems[4]
            rest = (ADA_REST, MERGE - ADA_REST)
            rot_ready, turned, qk_ready, s_ready, st_ready, o_ready, o_taken = (sem(f"ret_{n}") for n in ("rot", "turned", "qk", "s", "st", "o", "taken"))
            s_dve = sem("ret_dve")
            tmp = [ar(13824 + 512 * i, TT, 4 * 64).rearrange("p t (h d) -> p t h d", h=RH) for i in range(4)]
            qd, kd = ar(15872, RH, P), ar(16384, RH, P)
            tr = [ar(7680 + 512 * i, RH, P) for i in range(5)]
            st = [ar(13824 + 512 * i, RH, P) for i in range(2)]
            state = ar(14848, RH, P)
            def halves(x):
                v = x.rearrange("p t (h d) -> p t h d", h=RH)
                return v[:, :, :, 0:64], v[:, :, :, 64:P]
            with nc.Block() as block:
                @block.sync
                def _(sp):
                    for n in range(ADA_REST + RING, MERGE + RING):
                        load2(sp, l, n)

                @block.scalar
                def _(act):
                    ada_rows(act, sems, *rest, b=5)
                    nc.scalar.activation(sgT, sgT, ACT.Silu)

                @block.vector
                def _(dve):
                    then = step(dve, s_dve)
                    nc.vector.memset(c_wide, 0.0).then_inc(sems[0], 1)
                    cos, sin = (ret_tab[:, i].unsqueeze(2).broadcast_to([P, TT, RH, 64]) for i in range(2))
                    for x in (qt, kt_):
                        rotate(then, *halves(x), cos, sin, tmp)
                    heads = lambda x: x.rearrange("p (h d) -> p h d", h=RH)
                    nc.vector.tensor_tensor(qd, heads(qt[:, 1, :]), K("ret_q").unsqueeze(2).broadcast_to([P, RH, P]), ALU.mult).then_inc(rot_ready, 1)
                    nc.vector.tensor_tensor(kd, heads(kt_[:, 0, :]), K("ret_k").unsqueeze(2).broadcast_to([P, RH, P]), ALU.mult).then_inc(rot_ready, 1)
                    ada_columns(dve, sems, 4 * CONV, rest[1], 1, "norm2_g_2", b=5)
                    for i in range(5):
                        dve.wait_ge(turned, i + 1)
                        nc.vector.tensor_copy(tr[i], bank[i][:, :]).then_inc(qk_ready, 1)
                    dve.wait_ge(s_ready, 1)
                    nc.vector.tensor_copy(state, bank[7][:, :]).then_inc(st_ready, 1)
                    for t in range(TT):
                        dve.wait_ge(s_ready, t + 2)
                        nc.vector.tensor_tensor(st[t], bank[5 + t][:, :], K("ret_in"), ALU.mult).then_inc(st_ready, 1)
                    for i in range(2):
                        dve.wait_ge(o_ready, i + 1)
                        nc.vector.tensor_copy(y_ret[:, 2 * i:2 * i + 2, :], bank[i][:, :]).then_inc(o_taken, 1)

                @block.tensor
                def _(pe):
                    ada_products(pe, sems, *rest, b=5)
                    pe.wait_ge(rot_ready, 2)
                    srcs = [qt[:, 0, :], qt[:, 1, :], kt_[:, 0, :], kt_[:, 1, :], qd.rearrange("p h d -> p (h d)")]
                    for i, x in enumerate(srcs):
                        for h in range(RH):
                            last = nc.tensor.transpose(bank[i][:, P * h:P * h + P], x[:, P * h:P * h + P], K("ident"))
                        last.then_inc(turned, 1)
                    for h in range(RH):
                        last = nc.tensor.matmul(bank[7][:, P * h:P * h + P], kd[:, h, :], vt[:, 0, P * h:P * h + P], start=True, stop=True)
                    last.then_inc(s_ready, 1)
                    pe.wait_ge(qk_ready, 5)
                    pe.wait_ge(mod_ready, 1)
                    for t in range(TT):
                        for h in range(RH):
                            last = nc.tensor.matmul(bank[5 + t][:, P * h:P * h + P], tr[2 + t][:, h, :], tr[t][:, h, :], start=True, stop=True)
                        last.then_inc(s_ready, 1)
                    pe.wait_ge(st_ready, 3)
                    for h in range(RH):
                        for t in range(TT):
                            o = bank[h // 2][:, T * (h % 2) + P * t:T * (h % 2) + P * t + P]
                            last = nc.tensor.matmul(o, vt[:, t, P * h:P * h + P], st[t][:, h, :], start=True, stop=t == 0)
                            if t:
                                last = nc.tensor.matmul(o, state[:, h, :], tr[4][:, h, :], start=False, stop=True)
                        if h % 2:
                            last.then_inc(o_ready, 1)

        def head_norm(tag, y, sq, sums, n, eps, gain, finish):
            mean_ready, flat, sq_ready, var_ready, ms_ready, root_ready = (sem(f"{tag}_{x}") for x in ("mean", "flat", "sq", "var", "ms", "root"))
            s_dve = sem(f"{tag}_dve")
            with nc.Block() as block:
                @block.tensor
                def _(pe):
                    for i in range(2):
                        nc.tensor.matmul(bank[i][:, :], K(sums), y[:, 2 * i:2 * i + 2, :], start=True, stop=True).then_inc(mean_ready, 1)
                    for i in range(2):
                        pe.wait_ge(sq_ready, i + 1)
                        nc.tensor.matmul(bank[2 + i][:, :], K(sums), sq[:, 2 * i:2 * i + 2, :], start=True, stop=True).then_inc(var_ready, 1)

                @block.scalar
                def _(act):
                    for i in range(2):
                        act.wait_ge(flat, i + 1)
                        nc.scalar.activation(sq[:, 2 * i:2 * i + 2, :], y[:, 2 * i:2 * i + 2, :], ACT.Square).then_inc(sq_ready, 1)
                    for i in range(2):
                        act.wait_ge(ms_ready, i + 1)
                        nc.scalar.activation(sq[:, 2 * i:2 * i + 2, :], sq[:, 2 * i:2 * i + 2, :], ACT.Sqrt).then_inc(root_ready, 1)

                @block.vector
                def _(dve):
                    then = step(dve, s_dve)
                    for i in range(2):
                        dve.wait_ge(mean_ready, i + 1)
                        nc.vector.scalar_tensor_tensor(y[:, 2 * i:2 * i + 2, :], bank[i][:, :].rearrange("p (a t) -> p a t", a=2), -1.0 / n,
                                                       y[:, 2 * i:2 * i + 2, :], ALU.mult, ALU.add).then_inc(flat, 1)
                    for i in range(2):
                        dve.wait_ge(var_ready, i + 1)
                        nc.vector.tensor_scalar(sq[:, 2 * i:2 * i + 2, :], bank[2 + i][:, :], 1.0 / n, eps, ALU.mult, ALU.add).then_inc(ms_ready, 1)
                    for i in range(2):
                        dve.wait_ge(root_ready, i + 1)
                        then(nc.vector.reciprocal(sq[:, 2 * i:2 * i + 2, :], sq[:, 2 * i:2 * i + 2, :]))
                    for j in range(MT):
                        last = nc.vector.scalar_tensor_tensor(y[:, j, :], y[:, j, :], gain[:, j:j + 1], sq[:, j, :], ALU.mult, ALU.mult)
                    then(last)
                    finish(then)

        wT, aT, gT = (ar(7680 + 1024 * i, MT, T) for i in range(3))
        khT, ktT, cumT, icumT, exT = ar(0, MT, T), ar(1024, MT, T), ar(2048, MT, T), ar(3072, MT, T), ar(13824, MT, T)
        qrT = ar(14848, MT * TT * 2, P).rearrange("p (j t i) s -> p j t i s", j=MT, t=TT)
        bT, kdT = aT, ktT
        bonus = cumT
        Vtok, Ktok, Btok = ar(0, TT, MW), ar(3072, TT, MW), ar(7680, TT, MW)
        X = ar(4096, TT * 4, 2 * P)
        X5 = X.rearrange("p q (w i d) -> p q w i d", w=2, i=2)

        def rwkv_inputs():
            low_ready, lora_ready, w_ready, a_ready, kk_ready, sq_ready, ss_ready, ms_ready, root_ready, rk_ready, rk_sum, kt_ready = (
                sem(f"wkv_{n}") for n in ("low", "lora", "w", "a", "kk", "sq", "ss", "ms", "root", "rk", "rksum", "kt"))
            s_dve, s_act = sem("wkv_dve"), sem("wkv_act")
            d0, d1 = ar(14848, MT, T), ar(15872, MT, T)
            sq = ar(16896, MT, T)
            def wide(name):
                return K(name).unsqueeze(1).broadcast_to([P, MT, T])
            with nc.Block() as block:
                @block.scalar
                def _(act):
                    nc.scalar.activation(lowT[0:64, 0, :], lowT[0:64, 0, :], ACT.Tanh).then_inc(low_ready, 1)
                    nc.scalar.activation(lowT[:, 1, :], lowT[:, 1, :], ACT.Sigmoid).then_inc(low_ready, 1)
                    for j in range(MT):
                        act.wait_ge(lora_ready, 1)
                        nc.scalar.activation(wT[:, j, :], bank[j // 2][:, T * (j % 2):T * (j % 2) + T], ACT.Sigmoid, bias=V2("rwkv_w0_2")[:, j:j + 1]).then_inc(s_act, 1)
                    for j in range(MT):
                        act.wait_ge(lora_ready, 2)
                        nc.scalar.activation(aT[:, j, :], bank[2 + j // 2][:, T * (j % 2):T * (j % 2) + T], ACT.Sigmoid, bias=V2("rwkv_a0_2")[:, j:j + 1]).then_inc(a_ready, 1)
                    act.wait_ge(s_act, 4)
                    nc.scalar.activation(wT, wT, ACT.Exp, scale=-float(np.exp(-0.5))).then_inc(w_ready, 1)
                    act.wait_ge(lora_ready, 3)
                    for i in range(2):
                        nc.scalar.copy(gT[:, 2 * i:2 * i + 2, :], bank[4 + i][:, :])
                    act.wait_ge(kk_ready, 1)
                    nc.scalar.activation(sq, khT, ACT.Square).then_inc(sq_ready, 1)
                    for i in range(2):
                        act.wait_ge(ms_ready, i + 1)
                        nc.scalar.activation(sq[:, 2 * i:2 * i + 2, :], sq[:, 2 * i:2 * i + 2, :], ACT.Sqrt).then_inc(root_ready, 1)

                @block.tensor
                def _(pe):
                    pe.wait_ge(low_ready, 2)
                    for i in range(3):
                        lo, hi, w, x = ((0, 64, lora_wa, lowT[:, 0, :]), (64, P, lora_wa, lowT[:, 0, :]), (0, P, lora_g, lowT[:, 1, :]))[i]
                        for j in range(MT):
                            last = nc.tensor.matmul(bank[2 * i + j // 2][:, T * (j % 2):T * (j % 2) + T], w[lo:hi, P * j:P * j + P], x[lo:hi, :], start=True, stop=True)
                        last.then_inc(lora_ready, 1)
                    pe.wait_ge(sq_ready, 1)
                    for i in range(2):
                        nc.tensor.matmul(bank[6 + i][:, :], K("blk64"), sq[:, 2 * i:2 * i + 2, :], start=True, stop=True).then_inc(ss_ready, 1)
                    pe.wait_ge(rk_ready, 1)
                    for i in range(2):
                        nc.tensor.matmul(bank[6 + i][:, :], K("blk64"), d0[:, 2 * i:2 * i + 2, :], start=True, stop=True).then_inc(rk_sum, 1)

                @block.vector
                def _(dve):
                    then = step(dve, s_dve)
                    for j in range(MT):
                        last = nc.vector.tensor_scalar(khT[:, j, :], kT[:, j, :], V2("rwkv_k_k_2")[:, j:j + 1], None, ALU.mult)
                    last.then_inc(kk_ready, 1)
                    for j in range(MT):
                        dve.wait_ge(a_ready, j + 1)
                        then(nc.vector.tensor_scalar(ktT[:, j, :], aT[:, j, :], -1.0, V2("rwkv_k_a_2")[:, j:j + 1], ALU.add, ALU.mult))
                    then(nc.vector.scalar_tensor_tensor(ktT, ktT, 1.0, kT, ALU.add, ALU.mult))
                    dve.wait_ge(w_ready, 1)
                    nc.vector.tensor_tensor(d0, wT, wide("inner"), ALU.mult)
                    then(nc.vector.tensor_tensor(d1, wT, wide("start"), ALU.mult))
                    flat = lambda x: x.rearrange("p j t -> p (j t)")
                    then(nc.vector.tensor_tensor_scan(flat(cumT), flat(d0), flat(d1), 0.0, ALU.mult, ALU.add))
                    nc.vector.memset(exT[:, :, 0:1], 1.0)
                    then(nc.vector.tensor_tensor(exT[:, :, 1:T], cumT[:, :, 0:T - 1], wide("inner")[:, :, 1:T], ALU.mult))
                    then(nc.vector.tensor_tensor(exT[:, :, 1:T], exT[:, :, 1:T], wide("start")[:, :, 1:T], ALU.add))
                    nc.vector.reciprocal(icumT, cumT)
                    nc.vector.tensor_copy(pc[:], cumT.rearrange("p j (c s) -> p j c s", s=CH)[:, :, :, CH - 1])
                    for j in range(MT):
                        last = nc.vector.scalar_tensor_tensor(d0[:, j, :], rT[:, j, :], V2("rwkv_r_k_2")[:, j:j + 1], ktT[:, j, :], ALU.mult, ALU.mult)
                    for i in range(2):
                        dve.wait_ge(ss_ready, i + 1)
                        nc.vector.tensor_scalar(sq[:, 2 * i:2 * i + 2, :], bank[6 + i][:, :], 1e-12, None, ALU.max).then_inc(ms_ready, 1)
                    for i in range(2):
                        dve.wait_ge(root_ready, i + 1)
                        then(nc.vector.reciprocal(sq[:, 2 * i:2 * i + 2, :], sq[:, 2 * i:2 * i + 2, :]))
                    nc.vector.tensor_tensor(khT, khT, sq, ALU.mult).then_inc(rk_ready, 1)
                    dve.wait_ge(rk_ready, 1)
                    nc.vector.tensor_tensor(rT, rT, cumT, ALU.mult)
                    nc.vector.tensor_tensor(exT, exT, khT, ALU.mult)
                    then(nc.vector.tensor_tensor(aT, aT, khT, ALU.mult))
                    nc.vector.tensor_tensor(bT, aT, icumT, ALU.mult)
                    then(nc.vector.tensor_tensor(kdT, ktT, icumT, ALU.mult))
                    for i in range(2):
                        dve.wait_ge(rk_sum, i + 1)
                        then(nc.vector.tensor_tensor(bonus[:, 2 * i:2 * i + 2, :], vT[:, 2 * i:2 * i + 2, :], bank[6 + i][:, :].rearrange("p (a t) -> p a t", a=2), ALU.mult))
                    for t in range(TT):
                        nc.vector.tensor_copy(qrT[:, :, t, 0, :], exT[:, :, P * t:P * t + P])
                        nc.vector.tensor_copy(qrT[:, :, t, 1, :], rT[:, :, P * t:P * t + P])

        def rwkv_turn():
            turned = sem("wkvt_turned")
            srcs = [(lambda j, t: qrT[:, j, t, 0, :], None), (lambda j, t: vT[:, j, P * t:P * t + P], Vtok),
                    (lambda j, t: kdT[:, j, P * t:P * t + P], Ktok), (lambda j, t: bT[:, j, P * t:P * t + P], Btok)]
            with nc.Block() as block:
                @block.tensor
                def _(pe):
                    for b in range(8):
                        for j in range(MT):
                            last = nc.tensor.transpose(bank[b][:, P * j:P * j + P], srcs[b // 2][0](j, b % 2), K("ident"))
                        last.then_inc(turned, 1)

                def take(eng, copy, t):
                    for i in range(4):
                        b = 2 * i + t
                        eng.wait_ge(turned, b + 1)
                        if i == 0:
                            copy(X[:, 4 * t:4 * t + 4, 0:P], bank[b][:, :].rearrange("p (q d) -> p q d", q=4))
                        else:
                            copy(srcs[i][1][:, t, :], bank[b][:, :])

                @block.scalar
                def _(act):
                    take(act, nc.scalar.copy, 0)

                @block.vector
                def _(dve):
                    take(dve, nc.vector.tensor_copy, 1)

        def rwkv_solve():
            mats, masked, akv_ready, x_ready, sq_done, pow_ready, x_prod, fin_ready, fin_taken, y_set = (
                sem(f"sol_{n}") for n in ("mats", "masked", "akv", "x", "sqr", "pow", "xprod", "fin", "taken", "yset"))
            s_dve = sem("sol_dve")
            M1, M2 = ar(6144, 4, 2 * P), ar(13824, 4, 2 * P)
            Lm = ar(7168, 4, P)
            powers = [ar(13824, 2, 512), ar(16896, 2, 512)]
            masks = cst[:, CONST["before"][0]:CONST["upto"][1]]
            groups = [(t, h) for t in range(TT) for h in (0, 4)]

            def part(x, h):
                return x[HD * (h % 2):HD * (h % 2) + HD]

            with nc.Block() as block:
                @block.tensor
                def _(pe):
                    for g, (t, h0) in enumerate(groups):
                        if g:
                            pe.wait_ge(fin_taken, 2 * g)
                            pe.wait_ge(pow_ready, 7 * g)
                        for x, b0 in ((kdT, 0), (bT, 2)):
                            for i in range(4):
                                h = h0 + i
                                last = nc.tensor.matmul(bank[b0 + i % 2][:, T * (i // 2):T * (i // 2) + T], part(x, h)[:, h // 2, P * t:P * t + P],
                                                        part(qrT, h)[:, h // 2, t, :, :], start=True, stop=True)
                            last.then_inc(mats, 1)
                        for i in range(4):
                            h = h0 + i
                            last = nc.tensor.matmul(bank[(4, 7)[i % 2]][:, P * (i // 2):P * (i // 2) + P], part(qrT, h)[:, h // 2, t, 0, :], part(bT, h)[:, h // 2, P * t:P * t + P],
                                                    start=True, stop=True)
                        last.then_inc(mats, 1)
                        pe.wait_ge(masked, 6 * g + 2)
                        for i in range(4):
                            h = h0 + i
                            nc.tensor.matmul(bank[5][:, HD * i:HD * i + HD], M2[:, i, 0:P], Vtok[:, t, HD * h:HD * h + HD], start=True, stop=True)
                            last = nc.tensor.matmul(bank[6][HD * (i % 2):HD * (i % 2) + HD, P * (i // 2):P * (i // 2) + P], Vtok[:, t, HD * h:HD * h + HD],
                                                    M2[:, i, P:2 * P], start=True, stop=True)
                        last.then_inc(akv_ready, 1)
                        pe.wait_ge(masked, 6 * g + 6)
                        for r in range(5):
                            if r == 0:
                                low = lambda i: Lm[:, i, :]
                                top = lambda i: M1[:, i, 0:P]
                            else:
                                pw = powers[(r - 1) % 2]
                                pe.wait_ge(pow_ready, 7 * g + (2 * r if r < 4 else 7))
                                low = lambda i, pw=pw: pw[:, 0, P * i:P * i + P]
                                top = lambda i, pw=pw: pw[:, 1, P * i:P * i + P]
                            if r < 4:
                                b0 = 2 * (r % 2)
                                for which in ((0, 1) if r < 3 else (1,)):
                                    for i in range(4):
                                        a, b = (top(i), low(i)) if which == 0 else (low(i), top(i))
                                        last = nc.tensor.matmul(bank[b0 + which][:, P * i:P * i + P], a, b, start=True, stop=True)
                                    last.then_inc(sq_done, 1)
                            pe.wait_ge(x_ready, 6 * g + r + 1)
                            for i in range(4):
                                o = bank[5][:, T * (i // 2):T * (i // 2) + T].rearrange("p (w i d) -> p w i d", w=2, i=2)[:, :, i % 2, :]
                                last = nc.tensor.matmul(o, top(i), X5[:, 4 * t + (h0 + i) // 2, :, i % 2, :], start=True, stop=True)
                            last.then_inc(x_prod, 1)
                        pe.wait_ge(x_ready, 6 * g + 6)
                        for i in range(4):
                            u = 4 * t + (h0 + i) // 2
                            rows, cols = slice(HD * (i % 2), HD * (i % 2) + HD), slice(P * (i // 2), P * (i // 2) + P)
                            nc.tensor.matmul(bank[6][rows, cols], X5[:, u, 0, i % 2, :], M1[:, i, P:2 * P], start=True, stop=True)
                            last = nc.tensor.matmul(bank[7][rows, cols], X5[:, u, 1, i % 2, :], M1[:, i, P:2 * P], start=True, stop=True)
                        last.then_inc(fin_ready, 1)

                @block.scalar
                def _(act):
                    for g in range(len(groups)):
                        for i in range(7):
                            act.wait_ge(sq_done, 7 * g + i + 1)
                            r, which = (i // 2, i % 2) if i < 6 else (3, 1)
                            nc.scalar.copy(powers[r % 2][:, which, :], bank[2 * (r % 2) + which][:, :]).then_inc(pow_ready, 1)

                @block.vector
                def _(dve):
                    for g, (t, h0) in enumerate(groups):
                        xs = X[:, 4 * t + h0 // 2:4 * t + h0 // 2 + 2, :]
                        ys = y_rwkv[:, h0 // 2:h0 // 2 + 2, P * t:P * t + P]
                        pair = masks.unsqueeze(1).broadcast_to([P, 2, 2 * P])
                        for m, dst in enumerate((M2, M1)):
                            dve.wait_ge(mats, 3 * g + m + 1)
                            for i in range(2):
                                nc.vector.tensor_tensor(dst[:, i:4:2, :], bank[2 * m + i][:, :].rearrange("p (a s) -> p a s", a=2), pair,
                                                        ALU.mult).then_inc(masked, 1)
                        dve.wait_ge(mats, 3 * g + 3)
                        for i in range(2):
                            nc.vector.tensor_tensor(Lm[:, i:4:2, :], bank[(4, 7)[i]][:, 0:T].rearrange("p (a s) -> p a s", a=2),
                                                    K("after").unsqueeze(1).broadcast_to([P, 2, P]), ALU.mult).then_inc(masked, 1)
                        dve.wait_ge(akv_ready, g + 1)
                        nc.vector.tensor_copy(xs[:, :, P:2 * P], bank[5][:, 0:2 * P].rearrange("p (q d) -> p q d", q=2)).then_inc(x_ready, 1)
                        nc.vector.tensor_copy(ys, bank[6][:, 0:T].rearrange("p (a s) -> p a s", a=2)).then_inc(y_set, 1)
                        for r in range(5):
                            dve.wait_ge(x_prod, 5 * g + r + 1)
                            px = bank[5][:, :].rearrange("p (q s) -> p q s", q=2)
                            if r == 0:
                                last = nc.vector.tensor_tensor(xs, xs, px, ALU.subtract)
                            elif r < 4:
                                last = nc.vector.tensor_tensor(xs, xs, px, ALU.add)
                            else:
                                last = nc.vector.scalar_tensor_tensor(xs, px, -1.0, xs, ALU.mult, ALU.subtract)
                            last.then_inc(x_ready, 1)
                        dve.wait_ge(fin_ready, g + 1)
                        dve.wait_ge(y_set, g + 1)
                        rs = qrT[:, h0 // 2:h0 // 2 + 2, t, 1, :]
                        nc.vector.tensor_tensor(rs, rs, bank[6][:, 0:T].rearrange("p (a s) -> p a s", a=2), ALU.add).then_inc(fin_taken, 1)
                        nc.vector.tensor_tensor(ys, ys, bank[7][:, 0:T].rearrange("p (a s) -> p a s", a=2), ALU.add).then_inc(fin_taken, 1)

        def rwkv_chain():
            gh_ready, gh_taken, next_ready, state_ready, y_ready, y_taken = (
                sem(f"chn_{n}") for n in ("gh", "taken", "next", "state", "y", "ytaken"))
            s_dve = sem("chn_dve")
            half_at = ((13824, 16896), (8704, 1024))
            G, H = ([ar(half_at[f][i], 2 * NCH, P).rearrange("p (q c) s -> p q c s", q=2) for f in range(2)] for i in range(2))
            S = [qrT[:, :, i, 0, :] for i in range(2)]
            y_bank, s_bank = bank[6], bank[7]
            with nc.Block() as block:
                @block.tensor
                def _(pe):
                    def products(t, f):
                        for q in (2 * f, 2 * f + 1):
                            at, col, u = 2 * P * (q % 2), slice(P * q, P * q + P), 4 * t + q
                            bands = [(bank[4 * f + c], slice(CH * c, CH * c + CH)) for c in range(NCH)]
                            for o, r in bands:
                                nc.tensor.matmul(o[:, at:at + P], X[r, u, 0:P], Btok[r, t, col], start=True, stop=True)
                            for o, r in bands:
                                nc.tensor.matmul(o[:, at + P:at + 2 * P], Ktok[r, t, col], Vtok[r, t, col], start=True, stop=False)
                            for o, r in bands:
                                last = nc.tensor.matmul(o[:, at + P:at + 2 * P], Btok[r, t, col], X[r, u, P:2 * P], start=False, stop=True)
                        last.then_inc(gh_ready, 1)

                    def chain(t):
                        pe.wait_ge(gh_taken, 2 * t + 2)
                        for c in range(NCH):
                            n = NCH * t + c
                            pe.wait_ge(state_ready, n + 1)
                            for q in range(4):
                                last = nc.tensor.matmul(s_bank[:, P * q:P * q + P], G[q // 2][:, q % 2, c, :], S[n % 2][:, q, :], start=True, stop=True)
                            last.then_inc(next_ready, 1)
                            if n:
                                pe.wait_ge(y_taken, n)
                            for q in range(4):
                                last = nc.tensor.matmul(y_bank[:, CH * q:CH * q + CH], S[n % 2][:, q, :], qrT[:, q, t, 1, CH * c:CH * c + CH], start=True, stop=True)
                            last.then_inc(y_ready, 1)

                    products(0, 0)
                    products(0, 1)
                    pe.wait_ge(gh_taken, 1)
                    products(1, 0)
                    chain(0)
                    pe.wait_ge(state_ready, NCH + 1)
                    pe.wait_ge(y_taken, NCH)
                    products(1, 1)
                    chain(1)

                @block.vector
                def _(dve):
                    then = step(dve, s_dve)
                    nc.vector.memset(S[0], 0.0).then_inc(state_ready, 1)
                    blocks = K("blk64").unsqueeze(1).broadcast_to([P, 2, P])
                    for t in range(TT):
                        if t:
                            dve.wait_ge(state_ready, NCH * t + 1)
                        for f in range(2):
                            dve.wait_ge(gh_ready, 2 * t + f + 1)
                            for c in range(NCH):
                                o = bank[4 * f + c][:, :].rearrange("p (q k s) -> p q k s", q=2, k=2)
                                nc.vector.tensor_tensor(G[f][:, :, c, :], o[:, :, 0, :], blocks, ALU.mult)
                                last = nc.vector.tensor_tensor(H[f][:, :, c, :], o[:, :, 1, :], blocks, ALU.mult)
                            then(last)
                            nc.vector.tensor_tensor(H[f], H[f], pc[:, 2 * f:2 * f + 2, NCH * t:NCH * t + NCH].unsqueeze(3).broadcast_to([P, 2, NCH, P]), ALU.mult)
                            flat = G[f].rearrange("p q c s -> p (q c) s")
                            nc.vector.tensor_tensor(flat, flat, K("ident").unsqueeze(1).broadcast_to([P, 2 * NCH, P]), ALU.add).then_inc(gh_taken, 1)
                        dve.wait_ge(gh_taken, 2 * t + 2)
                        for c in range(NCH):
                            n = NCH * t + c
                            dve.wait_ge(next_ready, n + 1)
                            for q in range(4):
                                last = nc.vector.scalar_tensor_tensor(S[(n + 1) % 2][:, q, :], s_bank[:, P * q:P * q + P], pc[:, q, n:n + 1], H[q // 2][:, q % 2, c, :], ALU.mult, ALU.add)
                            last.then_inc(state_ready, 1)
                            dve.wait_ge(y_ready, n + 1)
                            ys = y_rwkv[:, :, P * t + CH * c:P * t + CH * c + CH]
                            nc.vector.tensor_tensor(ys, ys, y_bank[:, 0:4 * CH].rearrange("p (q s) -> p q s", q=4), ALU.add).then_inc(y_taken, 1)

        merged = ar(14848, KT, T)

        def merge(l):
            pair_ready, gate_ready, taken, s_dve = sem("mrg_pair"), sem("mrg_gate"), sem("mrg_taken"), sem("mrg_dve")
            ys = (y_ret, y_rwkv, y_conv)
            sg = ar(13824, 4, T)
            tmp = ar(0, 2, T)
            with nc.Block() as block:
                @block.sync
                def _(sp):
                    for n in range(MERGE + RING, MOE2 + 4):
                        load2(sp, l, n)

                @block.tensor
                def _(pe):
                    for i in range(3):
                        n = MERGE + 3 * i
                        for d in range(KT):
                            m = KT * i + d
                            if d % 4 == 0:
                                arrived(pe, n + d // 4)
                            if m >= 8:
                                pe.wait_ge(taken, m - 7)
                            w = chunk(n + d // 4, KT, MW)
                            for k in range(KT):
                                last = nc.tensor.matmul(bank[m % 8][:, 0:T], w[:, k, P * (d % 4):P * (d % 4) + P], xnT[:, k, :], start=k == 0, stop=k == KT - 1)
                            if d % 4 == 3:
                                last.then_inc(w_used, 1)
                            if d == 0:
                                arrived(pe, n + 2)
                            w = chunk(n + 2, MT, D)
                            for k in range(MT):
                                last = nc.tensor.matmul(bank[m % 8][:, T:2 * T], w[:, k, P * d:P * d + P], ys[i][:, k, :], start=k == 0, stop=k == MT - 1)
                            last.then_inc(w_used if d == KT - 1 else pair_ready, 1)

                @block.scalar
                def _(act):
                    for i in range(3):
                        for d in range(KT):
                            m = KT * i + d
                            if d < KT - 1:
                                act.wait_ge(pair_ready, (KT - 1) * i + d + 1)
                            else:
                                act.wait_ge(w_used, MERGE + 3 * i + 3)
                            if m >= 4:
                                act.wait_ge(taken, m - 3)
                            nc.scalar.activation(sg[:, m % 4, :], bank[m % 8][:, 0:T], ACT.Sigmoid, bias=V2("b_gate_2")[:, m:m + 1]).then_inc(gate_ready, 1)

                @block.vector
                def _(dve):
                    then = step(dve, s_dve)
                    for m in range(3 * KT):
                        d = m % KT
                        dve.wait_ge(gate_ready, m + 1)
                        if m < KT:
                            nc.vector.tensor_tensor(merged[:, d, :], sg[:, m % 4, :], bank[m % 8][:, T:2 * T], ALU.mult).then_inc(taken, 1)
                        else:
                            nc.vector.tensor_tensor(tmp[:, m % 2, :], sg[:, m % 4, :], bank[m % 8][:, T:2 * T], ALU.mult).then_inc(taken, 1)
                            dve.wait_ge(taken, m + 1)
                            then(nc.vector.tensor_tensor(merged[:, d, :], merged[:, d, :], tmp[:, m % 2, :], ALU.add))

        def project_out2(l):
            with nc.Block() as block:
                @block.sync
                def _(sp):
                    for n in range(MOE2 + 4, MOE2 + RING):
                        load2(sp, l, n)

                @block.tensor
                def _(pe):
                    for n in range(OUT2, OUT2 + 2):
                        arrived(pe, n)
                        w = chunk(n, KT, MW)
                        for j in range(4):
                            for k in range(KT):
                                last = nc.tensor.matmul(bank[2 * (n - OUT2) + j // 2][:, T * (j % 2):T * (j % 2) + T], w[:, k, P * j:P * j + P], merged[:, k, :],
                                                        start=k == 0, stop=k == KT - 1)
                        last.then_inc(w_used, 1)

                @block.vector
                def _(dve):
                    for d in range(KT):
                        dve.wait_ge(w_used, OUT2 + d // 4 + 1)
                        nc.vector.scalar_tensor_tensor(hT[:, d, :], bank[d // 2][:, T * (d % 2):T * (d % 2) + T], mod[:, 16 + d:17 + d], hT[:, d, :], ALU.mult, ALU.add)

        def gated(y, g):
            def finish(then):
                nc.vector.tensor_tensor(y, y, g, ALU.mult)
            return finish

        def rwkv_finish(then):
            then(nc.vector.tensor_tensor(y_rwkv, y_rwkv, bonus, ALU.add))
            nc.vector.tensor_tensor(y_rwkv, y_rwkv, gT, ALU.mult)

        WIN = 64
        ROUNDS = T // WIN
        SLOTS = 2 * T
        Xs = ar(0, KT, SLOTS + WIN)
        by_slot = ar(4608, TT, SLOTS + WIN)
        Xw = ar(5760, KT, 2 * WIN)
        silu, hid = ar(6784, F2), ar(7296, F2)
        hidT = ar(7808, F2 // P, P)
        gw, gwT = ar(8320, TT, 2 * WIN), ar(8576, T)
        Yw = ar(8832, D)
        iota = ar(9856, SLOTS)
        left = ar(10368, NE * ROUNDS)
        once = ar(10500, TT, SLOTS)
        xtok = ar(11524, TT, D)

        def route(tag, wr, ng, bias_row, iters):
            epg = NE // ng
            nr = ng + NE
            logits_ready, gs_ready, ge_ready, zs_ready, ze_ready, gate_ready, tok_turned, tok_taken, sel_ready, rank_ready, once_ready, gathered, slots_in = (
                sem(f"{tag}_{n}") for n in ("logits", "gs", "ge", "zs", "ze", "gate", "turned", "ttaken", "sel", "rank", "once", "gath", "slots"))
            s_dve = sem(f"{tag}_dve")
            at = 13572
            lg = ar(at, TT, nr)
            gs, ge, pen = (ar(at + 100 + 16 * i, TT, ng) for i in range(3))
            gtop, gsum, coef, hi, lo, ghi, glo = (ar(at + 160 + 2 * i, TT, 1) for i in range(7))
            z, zs, ez, sel, gate, pos, mark, eq = (ar(at + 200 + 64 * i, TT, NE) for i in range(8))
            v8 = ar(at + 720, TT, 8)
            d21 = ar(at + 740, TT, 1)
            count, cum, first = (ar(at + 760 + 32 * i, NE) for i in range(3))
            most, more = (ar(at + 920 + i, 1) for i in range(2))
            more3 = ar(at + 924, 3)
            by_hi = ar(5760, TT, SLOTS)
            gather_banks = (0, 1, 2, 4, 5, 6, 7, 3)
            with nc.Block() as block:
                @block.sync
                def _(sp):
                    sp.dma_start(iota, dram["slots"]).then_inc(slots_in, 16)

                @block.tensor
                def _(pe):
                    for t in range(TT):
                        for k in range(KT):
                            last = nc.tensor.matmul(bank[t][:, 0:nr], xnT[:, k, P * t:P * t + P], wr[:, k, :], start=k == 0, stop=k == KT - 1)
                            if k == 0 and bias_row is not None:
                                nc.tensor.matmul(bank[t][:, 0:nr], K("ones", 1), bias_row, start=False, stop=False)
                        last.then_inc(logits_ready, 1)
                    for i in range(4):
                        for k in range(4):
                            last = nc.tensor.transpose(bank[4 + i][:, P * k:P * k + P], xnT[:, 4 * (i % 2) + k, P * (i // 2):P * (i // 2) + P], K("ident"))
                        last.then_inc(tok_turned, 1)
                    pe.wait_ge(sel_ready, 1)
                    tri = K("tri")
                    o = bank[3]
                    nc.tensor.matmul(o[:, 0:NE], tri[:, 0:P], sel[:, 0, :], start=True, stop=True)
                    nc.tensor.matmul(o[:, NE:2 * NE], K("ones"), sel[:, 0, :], start=True, stop=False)
                    nc.tensor.matmul(o[:, NE:2 * NE], tri[:, T + P:2 * T], sel[:, 1, :], start=False, stop=True)
                    for t in range(TT):
                        last = nc.tensor.matmul(o[:, 2 * NE:3 * NE], K("ones"), sel[:, t, :], start=t == 0, stop=t == TT - 1)
                    last.then_inc(rank_ready, 1)
                    pe.wait_ge(tok_taken, 4)
                    pe.wait_ge(once_ready, TT)
                    for d in range(KT):
                        for t in range(TT):
                            last = nc.tensor.matmul(bank[gather_banks[d]][:, :], xtok[:, t, P * d:P * d + P], once[:, t, :], start=t == 0, stop=t == TT - 1)
                        last.then_inc(gathered, 1)
                @block.scalar
                def _(act):
                    act.wait_ge(gs_ready, 1)
                    nc.scalar.activation(ge, gs, ACT.Exp).then_inc(ge_ready, 1)
                    act.wait_ge(zs_ready, 2)
                    nc.scalar.activation(ez, zs, ACT.Exp).then_inc(ze_ready, 1)
                    nc.scalar.activation(d21, d21, ACT.Exp).then_inc(ze_ready, 1)
                    for i in range(4):
                        act.wait_ge(tok_turned, i + 1)
                        nc.scalar.copy(xtok[:, i // 2, MW * (i % 2):MW * (i % 2) + MW], bank[4 + i][:, :]).then_inc(tok_taken, 1)
                    for d in range(KT):
                        act.wait_ge(gathered, d + 1)
                        nc.scalar.copy(Xs[:, d, 0:SLOTS], bank[gather_banks[d]][:, :])

                @block.vector
                def _(dve):
                    then = step(dve, s_dve)
                    nc.vector.memset(Xs[:, :, SLOTS:SLOTS + WIN], 0.0)
                    nc.vector.memset(by_slot[:, :, SLOTS:SLOTS + WIN], 0.0)
                    dve.wait_ge(logits_ready, 2)
                    for t in range(TT):
                        then(nc.vector.tensor_copy(lg[:, t, :], bank[t][:, 0:nr]))
                    g, e = lg[:, :, 0:ng], lg[:, :, ng:nr]
                    then(nc.vector.tensor_reduce(gtop, g, AX, ALU.max))
                    nc.vector.tensor_tensor(gs, g, gtop.broadcast_to([P, TT, ng]), ALU.subtract).then_inc(gs_ready, 1)
                    dve.wait_ge(gs_ready, 1)
                    then(nc.vector.tensor_scalar(pen, gs, 0.0, None, ALU.is_ge))
                    then(nc.vector.tensor_scalar(pen, pen, BIG, -BIG, ALU.mult, ALU.add))
                    then(nc.vector.tensor_tensor(z.rearrange("p t (g e) -> p t g e", g=ng), e.rearrange("p t (g e) -> p t g e", g=ng),
                                                 pen.unsqueeze(3).broadcast_to([P, TT, ng, epg]), ALU.add))
                    for t in range(TT):
                        then(nc.vector.max(v8[:, t, :], z[:, t, :]))
                    nc.vector.tensor_tensor(sel, z, v8[:, :, 1:2].broadcast_to([P, TT, NE]), ALU.is_ge).then_inc(sel_ready, 1)
                    nc.vector.tensor_tensor(zs, z, v8[:, :, 0:1].broadcast_to([P, TT, NE]), ALU.subtract).then_inc(zs_ready, 1)
                    nc.vector.tensor_tensor(d21, v8[:, :, 1:2], v8[:, :, 0:1], ALU.subtract).then_inc(zs_ready, 1)
                    dve.wait_ge(sel_ready, 1)
                    dve.wait_ge(rank_ready, 1)
                    then(nc.vector.tensor_copy(count, bank[3][:, 2 * NE:3 * NE]))
                    then(nc.vector.tensor_tensor_scan(cum, K("ones")[:, 0:NE], count, 0.0, ALU.mult, ALU.add))
                    then(nc.vector.tensor_tensor(first, cum, count, ALU.subtract))
                    then(nc.vector.tensor_tensor(pos, bank[3][:, 0:2 * NE].rearrange("p (t e) -> p t e", t=TT), first.unsqueeze(1).broadcast_to([P, TT, NE]), ALU.add))
                    then(nc.vector.tensor_tensor(mark, pos, sel, ALU.mult))
                    then(nc.vector.tensor_reduce(hi, mark, AX, ALU.max))
                    then(nc.vector.scalar_tensor_tensor(eq, pos, -4096.0, sel, ALU.add, ALU.mult))
                    then(nc.vector.tensor_reduce(lo, eq, AX, ALU.min))
                    then(nc.vector.tensor_scalar(lo, lo, 4096.0, None, ALU.add))
                    dve.wait_ge(slots_in, 16)
                    for t in range(TT):
                        then(nc.vector.tensor_scalar(once[:, t, :], iota, lo[:, t, :], None, ALU.is_equal))
                        nc.vector.scalar_tensor_tensor(once[:, t, :], iota, hi[:, t, :], once[:, t, :], ALU.is_equal, ALU.add).then_inc(once_ready, 1)
                    dve.wait_ge(ge_ready, 1)
                    then(nc.vector.tensor_reduce(gsum, ge, AX, ALU.add))
                    dve.wait_ge(ze_ready, 2)
                    then(nc.vector.scalar_tensor_tensor(coef, d21, 1.0, gsum, ALU.add, ALU.mult))
                    then(nc.vector.reciprocal(coef, coef))
                    for t in range(TT):
                        then(nc.vector.scalar_tensor_tensor(gate[:, t, :], ez[:, t, :], coef[:, t, :], sel[:, t, :], ALU.mult, ALU.mult))
                    for slot, of in ((hi, ghi), (lo, glo)):
                        then(nc.vector.tensor_tensor(eq, mark, slot.broadcast_to([P, TT, NE]), ALU.is_equal))
                        then(nc.vector.tensor_tensor(eq, eq, gate, ALU.mult))
                        then(nc.vector.tensor_reduce(of, eq, AX, ALU.add))
                    for t in range(TT):
                        nc.vector.tensor_scalar(by_slot[:, t, 0:SLOTS], iota, lo[:, t, :], glo[:, t, :], ALU.is_equal, ALU.mult)
                        then(nc.vector.tensor_scalar(by_hi[:, t, :], iota, hi[:, t, :], ghi[:, t, :], ALU.is_equal, ALU.mult))
                        nc.vector.tensor_tensor(by_slot[:, t, 0:SLOTS], by_slot[:, t, 0:SLOTS], by_hi[:, t, :], ALU.add)
                    for r in range(ROUNDS):
                        nc.vector.tensor_scalar(offs[:, NE * r:NE * r + NE], first, float(WIN * r), float(SLOTS), ALU.add, ALU.min)
                        nc.vector.tensor_scalar(left[:, NE * r:NE * r + NE], count, float(-WIN * r), None, ALU.add)
                    nc.vector.memset(offs[:, NE * ROUNDS:NE * ROUNDS + 2], SLOTS)
                    then(nc.vector.tensor_reduce(most, count, AX, ALU.max))
                    for r in range(1, ROUNDS):
                        last = nc.vector.tensor_scalar(more3[:, r - 1:r], most, float(WIN * r), None, ALU.is_gt)
                    then(last)
                    then(nc.vector.tensor_reduce(more, more3, AX, ALU.add))
                    nc.vector.tensor_scalar(meta[:, 0:1], more, float(iters), float(iters), ALU.mult, ALU.add)

        def experts(tag, feed, n0, f, pairs, gate_col):
            ft = f // P
            xw_ready, silu_ready, hid_made, turned, hidT_ready, gw_ready, gw_turned, gwT_ready, y1_done, y1_taken, y0_taken, sum_ready = (
                sem(f"{tag}_{n}") for n in ("xw", "silu", "hid", "turned", "hidT", "gw", "gwturned", "gwT", "y1", "y1taken", "y0taken", "sum"))
            np_ = len(pairs)
            iters = NE // 2 // np_
            per_turn = 1 + max(max(c) for c in pairs)
            shared = pairs[0][0] == pairs[0][2]
            gate_bank, up_bank, turn_bank, y0_bank = bank[4], bank[4 if shared else 5], bank[6], bank[7]
            y1_bank = bank[5]
            up_at = f if shared else 0

            def slot(n):
                return (n0 + n) % RING

            def turns(eng):
                return eng.value_load(meta[0:1, 0:1], min_val=iters, max_val=ROUNDS * iters)

            def offset(eng, p):
                at = p if isinstance(p, int) else p.with_bounds(min_val=0, max_val=NE * ROUNDS + 1)
                return eng.value_load(offs[0:1, bass.ds(at, 1)], min_val=0, max_val=SLOTS)

            def chunk_used(eng, it, n):
                eng.wait_ge(w_used, it * per_turn + (n0 + n + 1))

            def rows(i):
                return slice(WIN * i, WIN * i + WIN)

            with nc.Block() as block:
                @block.sync
                def _(sp):
                    def fetch(it, n, turn):
                        sp.wait_ge(w_used, it * per_turn + (n0 + n - RING + 1))
                        sp.dma_start(ring[:, slot(n), :], feed(turn, n)).then_inc(w_loaded[slot(n)], 16)

                    for n in range(RING, per_turn):
                        fetch(0, n, 0)
                    with sp.Fori(1, turns(sp)) as it:
                        turn = it % iters
                        for n in range(per_turn):
                            fetch(it, n, turn)

                @block.tensor
                def _(pe):
                    def combine(ds):
                        for d in ds:
                            nc.tensor.matmul(bank[d // 2][:, T * (d % 2):T * (d % 2) + T], Yw[:, P * d:P * d + P], gwT, start=False, stop=False, skip_group_check=True)

                    for b in range(4):
                        nc.tensor.matmul(bank[b][:, :], K("zeros"), cst[:, 0:512], start=True, stop=False, skip_group_check=True)
                    with pe.Fori(0, turns(pe)) as it:
                        def here(n):
                            pe.wait_ge(w_loaded[slot(n)], it * (16 * per_turn // RING) + 16 * ((n0 + n) // RING + 1))

                        for i, (ga, gb, ua, ub, da, db) in enumerate(pairs):
                            p = it * np_ + (i + 1)
                            pe.wait_ge(xw_ready, p)
                            for o, at, wa, wb in ((gate_bank, 0, ga, gb),) if shared else ((gate_bank, 0, ga, gb), (up_bank, 0, ua, ub)):
                                here(wa)
                                here(wb)
                                if o is y1_bank:
                                    pe.wait_ge(y1_taken, p)
                                for k in range(KT):
                                    for e, n in enumerate((wa, wb)):
                                        last = nc.tensor.matmul(o[rows(e), 0:MW], Xw[:, k, WIN * e:WIN * e + WIN], ring[:, slot(n), MW * k:MW * k + MW],
                                                                start=k == 0, stop=k == KT - 1)
                                        if k == KT - 1:
                                            last.then_inc(w_used, 1)
                            pe.wait_ge(y1_taken, p)
                            pe.wait_ge(y0_taken, p)
                            pe.wait_ge(gwT_ready, p)
                            combine(range(0, 4))
                            pe.wait_ge(hid_made, p)
                            for j in range(ft):
                                last = nc.tensor.transpose(turn_bank[:, P * j:P * j + P], hid[:, P * j:P * j + P], K("ident"))
                            last.then_inc(turned, 1)
                            combine(range(4, 8))
                            pe.wait_ge(gw_ready, p)
                            for t in range(TT):
                                last = nc.tensor.transpose(y0_bank[:, P * t:P * t + P], gw[:, t, :], K("ident"))
                            last.then_inc(gw_turned, 1)
                            here(da)
                            if db != da:
                                here(db)
                            pe.wait_ge(hidT_ready, p)
                            for half, o in ((1, y1_bank), (0, y0_bank)):
                                if half == 0:
                                    pe.wait_ge(gwT_ready, p + 1)
                                for j in range(ft):
                                    for e, n in enumerate((da, db)):
                                        at = (ft * e if da == db else 0) * D + D * j + MW * half
                                        last = nc.tensor.matmul(o[rows(e), :], hidT[:, j, WIN * e:WIN * e + WIN], ring[:, slot(n), at:at + MW],
                                                                start=j == 0, stop=j == ft - 1)
                                        if half == 0 and j == ft - 1 and (e == 1 or db != da):
                                            last.then_inc(w_used, 1)
                                if half == 1:
                                    last.then_inc(y1_done, 1)
                    n_pairs = turns(pe) * np_
                    pe.wait_ge(y1_taken, n_pairs + 1)
                    pe.wait_ge(y0_taken, n_pairs + 1)
                    combine(range(8))
                    nc.tensor.matmul(bank[3][:, :], K("zeros"), cst[:, 0:512], start=False, stop=True, skip_group_check=True).then_inc(sum_ready, 1)

                @block.scalar
                def _(act):
                    act.wait_ge(y0_taken, 1)
                    nc.scalar.copy(spare[:, 0:1], K("zeros")[:, 0:1]).then_inc(y1_taken, 1)
                    with act.Fori(0, turns(act)) as it:
                        for i, (ga, gb, ua, ub, da, db) in enumerate(pairs):
                            p = it * np_ + (i + 1)
                            chunk_used(act, it, ub)
                            nc.scalar.activation(silu[:, 0:f], gate_bank[:, 0:f], ACT.Silu).then_inc(silu_ready, 1)
                            act.wait_ge(turned, p)
                            nc.scalar.copy(hidT[:, 0:ft, :], turn_bank[:, 0:f].rearrange("p (j s) -> p j s", j=ft)).then_inc(hidT_ready, 1)
                            act.wait_ge(y1_done, p)
                            nc.scalar.copy(Yw[:, MW:D], y1_bank[:, :]).then_inc(y1_taken, 1)

                @block.vector
                def _(dve):
                    def windows(p):
                        for e in range(2):
                            off = offset(dve, 2 * p + e)
                            last = nc.vector.tensor_copy(Xw[:, :, WIN * e:WIN * e + WIN], Xs[:, :, bass.ds(off, WIN)])
                        last.then_inc(xw_ready, 1)

                    nc.vector.memset(gwT, 0.0).then_inc(gwT_ready, 1)
                    nc.vector.memset(Yw, 0.0).then_inc(y0_taken, 1)
                    dve.wait_ge(gwT_ready, 1)
                    windows(0)
                    with dve.Fori(0, turns(dve)) as it:
                        for i, (ga, gb, ua, ub, da, db) in enumerate(pairs):
                            p = it * np_ + (i + 1)
                            dve.wait_ge(silu_ready, p)
                            nc.vector.tensor_tensor(hid[:, 0:f], up_bank[:, up_at:up_at + f], silu[:, 0:f], ALU.mult).then_inc(hid_made, 1)
                            for e in range(2):
                                w = it * (2 * np_) + (2 * i + e)
                                off = offset(dve, w)
                                last = nc.vector.scalar_tensor_tensor(gw[:, :, WIN * e:WIN * e + WIN], iota[:, 0:WIN].unsqueeze(1).broadcast_to([P, TT, WIN]),
                                                                      left[:, bass.ds(w.with_bounds(min_val=0, max_val=NE * ROUNDS - 1), 1)], by_slot[:, :, bass.ds(off, WIN)],
                                                                      ALU.is_le, ALU.mult)
                            last.then_inc(gw_ready, 1)
                            windows(it * np_ + (i + 1))
                            dve.wait_ge(gw_turned, p)
                            nc.vector.tensor_copy(gwT, y0_bank[:, 0:T]).then_inc(gwT_ready, 1)
                            chunk_used(dve, it, db)
                            nc.vector.tensor_copy(Yw[:, 0:MW], y0_bank[:, :]).then_inc(y0_taken, 1)
                    dve.wait_ge(sum_ready, 1)
                    for d in range(KT):
                        y = bank[d // 2][:, T * (d % 2):T * (d % 2) + T]
                        if gate_col is None:
                            nc.vector.tensor_tensor(hT[:, d, :], hT[:, d, :], y, ALU.add)
                        else:
                            nc.vector.scalar_tensor_tensor(hT[:, d, :], y, gate_col[:, d:d + 1], hT[:, d, :], ALU.mult, ALU.add)

        def zero_semaphores():
            with nc.Block() as block:
                @block.sync
                def _(sp):
                    for s in layer_sems + w_loaded + [w_used]:
                        sp.sem_clear(s)

        def fetch_vectors(sp, vec_in, src, n, row_src, row_n):
            sp.dma_start(vec[:, 0:n], src).then_inc(vec_in, 16)
            sp.dma_start(row[:, 0:row_n], row_src).then_inc(vec_in, 16)

        setup()
        with ExitStack() as stack:
            owners.append(stack)
            layer_sems.clear()
            with nc.Fori(0, L) as l:
                def fetch1(sp, vec_in):
                    fetch_vectors(sp, vec_in, dram["vec1"][l], N1, dram["row1"][l], HEADS)
                    for n in range(2):
                        load(sp, n, dram["w_in1"][l, n])
                    load(sp, 2, dram["w_in1"][l, 2])
                    load(sp, 3, dram["w_rest1"][l], KT * REST)
                    for n in range(2):
                        load(sp, 4 + n, dram["w_o1"][l, n])
                    sp.wait_ge(vec_in, 32)

                norm("n1a", V1("attn_norm"), None, 0, fetch=fetch1)
                project1(l)
                latents()
                turn_qk()
                attention()
                head_rms_out(l)
                norm("n1b", V1("ffn_norm"), None, 11000)
                route("r1", wr1, NG1, None, NE // 4)
                experts("e1", lambda it, n: dram["w_exp1"][l, it * RING + n], MOE1, F1, ((0, 1, 0, 1, 2, 2), (3, 4, 3, 4, 5, 5)), None)
                zero_semaphores()
            owners.pop()
        norm("nf", VG("final_norm"), None, 0, dest=hT)
        with ExitStack() as stack:
            owners.append(stack)
            layer_sems.clear()
            with nc.Fori(0, L) as l:
                small_in = sem("small2_in")

                def fetch2(sp, vec_in):
                    load2(sp, l, 0)
                    fetch_vectors(sp, vec_in, dram["vec2"][l], N2, dram["row2"][l], R2_N)
                    sp.dma_start(small[:, 0:2 * MW + KT * R2_N], dram["small2"][l]).then_inc(small_in, 16)
                    for n in range(1, CONV + RING):
                        load2(sp, l, n)
                    sp.wait_ge(vec_in, 32)
                    sp.wait_ge(small_in, 16)

                norm("n2a", gains[:, 0, :], mod[:, 0:8], 0, fetch=fetch2, ada=(ADA, CONV - ADA))
                project2(l)
                retention(l)
                head_norm("nret", y_ret, ar(13824, MT, T), "ones", P, HEPS, V2("ret_gn_g_2"), gated(y_ret, sgT))
                rwkv_inputs()
                rwkv_turn()
                rwkv_solve()
                rwkv_chain()
                head_norm("nwkv", y_rwkv, ar(13824, MT, T), "blk64", HD, REPS, V2("rwkv_gn_g_2"), rwkv_finish)
                merge(l)
                project_out2(l)
                norm("n2b", gains[:, 1, :], mod[:, 24:32], 11000)
                route("r2", wr2, NG2, row[0:1, 0:R2_N], NE // 2)
                experts("e2", lambda it, n: dram["w_exp2"][l, it * RING + n], MOE2, F2, ((0, 1, 2, 3, 4, 5),), mod[:, 40:48])
                zero_semaphores()
            owners.pop()
        norm("nf2", VG("final_norm_g_2"), None, 0, dest=hT)
        stored = sem("out_stored")
        with nc.Block() as block:
            @block.sync
            def _(sp):
                sp.dma_start(out, hT[:]).then_inc(stored, 16)
                sp.wait_ge(stored, 16)


def columns(a):
    a = np.asarray(a)
    return np.swapaxes(a.reshape(*a.shape[:-1], -1, P), -1, -2)


def tiled(w):
    k, n = w.shape[-2:]
    w = np.moveaxis(w.reshape(*w.shape[:-2], k // P, P, n), -3, -2)
    return w.reshape(*w.shape[:-2], -1)


def in_chunks(w, width=MW):
    k, n = w.shape[-2:]
    w = w.reshape(*w.shape[:-1], n // width, width)
    return tiled(np.moveaxis(w, -2, -3))


def packed(parts, inputs, layered=True):
    return np.concatenate([columns(inputs[n].reshape(L, -1) if layered else inputs[n].reshape(-1)) for n, _ in parts], -1)


def layouts(i):
    w_in = i["w_in"]
    a = {"consts": CONST_TABLE, "slots": np.tile(np.arange(1, 2 * T + 1, dtype=np.float32), (P, 1))}
    a["x"] = np.moveaxis(i["x"][0].T.reshape(KT, P, T), 0, 1)
    for n in ("positions", "positions_2"):
        a[n] = i[n][0].reshape(TT, P).T
    a["vecg"] = packed(VECG_PARTS, i, False)
    a["vec1"] = packed(VEC1_PARTS, i)
    a["row1"] = i["b_f"].reshape(L, 1, HEADS)
    a["w_in1"] = in_chunks(w_in[:, :, 0:3 * MW])
    a["w_rest1"] = tiled(w_in[:, :, 3 * MW:])
    a["w_o1"] = in_chunks(i["w_o"])
    a["small1"] = np.concatenate([tiled(i["w_uq"]), tiled(i["w_ukv"]), tiled(np.concatenate([i["w_group"], i["w_router"]], -1))], -1)
    gu = tiled(np.concatenate([i["w_gate"], i["w_up"]], -1)).reshape(L, NE // 4, 2, 2, P, SLOT)
    down = tiled(i["w_down"]).reshape(L, NE // 4, 2, 2, P, SLOT // 2)
    down = np.moveaxis(down, 3, 4).reshape(L, NE // 4, 2, 1, P, SLOT)
    a["w_exp1"] = np.concatenate([gu, down], 3).reshape(L, NE // 4 * RING, P, SLOT)
    w2 = i["w_in_2"]
    a["vec2"] = packed(VEC2_PARTS, i)
    a["row2"] = np.concatenate([i["b_router_group_2"], i["b_router_expert_2"]], -1).reshape(L, 1, R2_N)
    a["w_ada2"] = in_chunks(i["w_ada_2"])
    a["w_in2"] = in_chunks(w2[:, :, 0:7 * MW])
    a["w_low2"] = tiled(w2[:, :, 7 * MW:7 * MW + 2 * P])
    a["w_conv2"] = in_chunks(w2[:, :, 7 * MW + 2 * P:])
    gates = in_chunks(i["w_gate_2"]).reshape(L, 3, 2, P, SLOT)
    a["w_merge2"] = np.concatenate([gates, tiled(i["w_branch_2"])[:, :, None]], 2).reshape(L, 9, P, SLOT)
    a["w_o2"] = in_chunks(i["w_o_2"])
    lora = np.concatenate([i["rwkv_w_lora_2"], i["rwkv_a_lora_2"]], 1)
    a["small2"] = np.concatenate([lora, i["rwkv_g_lora_2"], tiled(np.concatenate([i["w_router_group_2"], i["w_router_expert_2"]], -1))], -1)
    a["w_exp2"] = np.stack([tiled(i[f"w_exp_{n}_2"]) for n in ("gate", "up", "down")], 2)
    a["w_exp2"] = np.moveaxis(a["w_exp2"].reshape(L, NE // 2, 2, 3, P, SLOT), 2, 3).reshape(L, 3 * NE, P, SLOT)
    return {k: np.ascontiguousarray(v) for k, v in a.items()}


def kernel(**inputs):
    import concourse.bacc as bacc
    from concourse.bass_utils import run_bass_kernel_spmd

    nc = bacc.Bacc("TRN2", target_bir_lowering=False, num_devices=1)
    arrays = layouts({k: np.asarray(v) for k, v in inputs.items()})
    dram = {n: nc.dram_tensor(f"in_{n}", a.shape, mybir.dt.from_np(a.dtype), kind="ExternalInput").ap() for n, a in arrays.items()}
    out = nc.dram_tensor("out", (P, KT, T), F32, kind="ExternalOutput").ap()
    build(nc, dram, out)
    r = run_bass_kernel_spmd(nc, [{f"in_{n}": a for n, a in arrays.items()}], core_ids=[0])
    y = np.asarray(r.results[0]["out"])
    return np.ascontiguousarray(np.moveaxis(y, 0, 1).reshape(D, T).T).reshape(1, T, D)
```
